# Optimizing a Trainium2 kernel written in Bass

```python
import jax, jax.numpy as jnp
from jax import lax
import numpy as np

D_MODEL = 1024
BATCH = 1
SEQ = 1024
DEPTH = 1

GRID_W = 64
CTX_LEN = 256
HEAD_DIM = 64
N_HEADS_A = 8
N_KV_A = 2
GQA_GROUP = N_HEADS_A // N_KV_A
N_HEADS_B = 8
WIDTH_A = N_HEADS_A * HEAD_DIM
WIDTH_KV_A = N_KV_A * HEAD_DIM
WIDTH_B = N_HEADS_B * HEAD_DIM
MIX_WIDTH = WIDTH_A + WIDTH_B
IN_WIDTH = WIDTH_A + 2 * WIDTH_KV_A + 3 * WIDTH_B
WINDOW = 128
BLOCK_A = 128
NA_ROWS = 8
NA_COLS = 16
NA_Q_COLS = 16
NA_K_COLS = 32
N_EXPERTS = 32
TOP_K = 4
D_FF_EXPERT = D_MODEL
SWIGLU_LIMIT = 7.0
SWIGLU_ALPHA = 1.702
MOE_BLOCK = 128
ROPE_BASE = 10000.0
EPS = 1e-6
NEG_INF = -1e30

kernel_name = 'hybrid_window_natten_moe_dit_block'

def rmsnorm(x, g):
    xf = x.astype(jnp.float32)
    y = xf * lax.rsqrt(jnp.mean(xf * xf, axis=-1, keepdims=True) + EPS)
    return (y * g.astype(jnp.float32)).astype(x.dtype)

def modulate(x, shift, scale):
    return x * (1 + scale) + shift

def rope_1d(x, ang):
    n = x.shape[-1] // 2
    x1, x2 = x[..., :n], x[..., n:]
    cos = jnp.cos(ang)[:, None, :]
    sin = jnp.sin(ang)[:, None, :]
    return jnp.concatenate([x1 * cos - x2 * sin, x2 * cos + x1 * sin], axis=-1)

def axial_rope(x, ang_row, ang_col):
    half = HEAD_DIM // 2
    xf = x.astype(jnp.float32)
    out = jnp.concatenate([rope_1d(xf[..., :half], ang_row), rope_1d(xf[..., half:], ang_col)], axis=-1)
    return out.astype(x.dtype)

def split_projection(p):
    B, T, _ = p.shape
    cuts = [WIDTH_A, WIDTH_A + WIDTH_KV_A, WIDTH_A + 2 * WIDTH_KV_A,
            WIDTH_A + 2 * WIDTH_KV_A + WIDTH_B, WIDTH_A + 2 * WIDTH_KV_A + 2 * WIDTH_B]
    qa, ka, va, qb, kb, vb = jnp.split(p, cuts, axis=-1)
    qa = qa.reshape(B, T, N_HEADS_A, HEAD_DIM)
    ka = ka.reshape(B, T, N_KV_A, HEAD_DIM)
    va = va.reshape(B, T, N_KV_A, HEAD_DIM)
    qb = qb.reshape(B, T, N_HEADS_B, HEAD_DIM)
    kb = kb.reshape(B, T, N_HEADS_B, HEAD_DIM)
    vb = vb.reshape(B, T, N_HEADS_B, HEAD_DIM)
    return qa, ka, va, qb, kb, vb

def window_attention(q, k, v, kc, vc, sink):
    B, L = q.shape[:2]
    C = kc.shape[1]
    nb = L // BLOCK_A
    span = BLOCK_A + 2 * WINDOW
    scale = HEAD_DIM ** -0.5
    kp = jnp.pad(k, ((0, 0), (WINDOW, WINDOW), (0, 0), (0, 0)))
    vp = jnp.pad(v, ((0, 0), (WINDOW, WINDOW), (0, 0), (0, 0)))
    qb = q.reshape(B, nb, BLOCK_A, N_KV_A, GQA_GROUP, HEAD_DIM)
    r = jnp.arange(BLOCK_A)
    j = jnp.arange(span)
    band = jnp.abs(j[None, :] - WINDOW - r[:, None]) <= WINDOW
    sink_g = sink.astype(jnp.float32).reshape(N_KV_A, GQA_GROUP)[None, :, :, None, None]

    def block(i):
        qi = lax.dynamic_index_in_dim(qb, i, axis=1, keepdims=False)
        ki = lax.dynamic_slice_in_dim(kp, i * BLOCK_A, span, axis=1)
        vi = lax.dynamic_slice_in_dim(vp, i * BLOCK_A, span, axis=1)
        kpos = i * BLOCK_A - WINDOW + j
        valid = band & (kpos >= 0)[None, :] & (kpos < L)[None, :]
        s_loc = jnp.einsum('bqkgd,bskd->bkgqs', qi, ki, preferred_element_type=jnp.float32) * scale
        s_loc = jnp.where(valid, s_loc, NEG_INF)
        s_ctx = jnp.einsum('bqkgd,bckd->bkgqc', qi, kc, preferred_element_type=jnp.float32) * scale
        s_sink = jnp.broadcast_to(sink_g, s_ctx.shape[:-1] + (1,))
        p = jax.nn.softmax(jnp.concatenate([s_loc, s_ctx, s_sink], axis=-1), axis=-1)
        p_loc = p[..., :span].astype(v.dtype)
        p_ctx = p[..., span:span + C].astype(v.dtype)
        o = jnp.einsum('bkgqs,bskd->bqkgd', p_loc, vi) + jnp.einsum('bkgqc,bckd->bqkgd', p_ctx, vc)
        return o.reshape(B, BLOCK_A, WIDTH_A)

    out = lax.map(block, jnp.arange(nb))
    return jnp.moveaxis(out, 0, 1).reshape(B, L, WIDTH_A)

def neighbourhood_attention(q, k, v, kc, vc, rpb):
    B, L = q.shape[:2]
    rows_n = L // GRID_W
    kr = min(NA_ROWS, rows_n)
    scale = HEAD_DIM ** -0.5
    qg = q.reshape(B, rows_n, GRID_W, N_HEADS_B, HEAD_DIM)
    kg = k.reshape(B, rows_n, GRID_W, N_HEADS_B, HEAD_DIM)
    vg = v.reshape(B, rows_n, GRID_W, N_HEADS_B, HEAD_DIM)
    n_cb = GRID_W // NA_Q_COLS
    qcol = np.arange(GRID_W)
    col_start = np.clip(qcol - NA_COLS // 2, 0, GRID_W - NA_COLS).reshape(n_cb, NA_Q_COLS)
    blk_start = np.clip(np.arange(n_cb) * NA_Q_COLS - NA_COLS // 2, 0, GRID_W - NA_K_COLS)
    key_cols = blk_start[:, None] + np.arange(NA_K_COLS)
    qcols = qcol.reshape(n_cb, NA_Q_COLS)
    kc3 = key_cols[:, None, :]
    cs3 = col_start[:, :, None]
    col_ok = (kc3 >= cs3) & (kc3 < cs3 + NA_COLS)
    dcol_idx = np.clip(kc3 - qcols[:, :, None] + NA_COLS - 1, 0, 2 * NA_COLS - 2)
    mask = jnp.asarray(col_ok)[:, :, None, :]

    def row_block(r):
        rs = jnp.clip(r - kr // 2, 0, rows_n - kr)
        qr = lax.dynamic_index_in_dim(qg, r, axis=1, keepdims=False).reshape(B, n_cb, NA_Q_COLS, N_HEADS_B, HEAD_DIM)
        k_rows = lax.dynamic_slice_in_dim(kg, rs, kr, axis=1)
        v_rows = lax.dynamic_slice_in_dim(vg, rs, kr, axis=1)
        kblk = k_rows[:, :, key_cols]
        vblk = v_rows[:, :, key_cols]
        drow_idx = rs - r + jnp.arange(kr) + NA_ROWS - 1
        bias = rpb[:, drow_idx][:, :, dcol_idx].astype(jnp.float32)
        bias = jnp.transpose(bias, (0, 2, 3, 1, 4))
        s = jnp.einsum('bnqhd,banchd->bhnqac', qr, kblk, preferred_element_type=jnp.float32) * scale + bias[None]
        s = jnp.where(mask, s, NEG_INF).reshape(B, N_HEADS_B, n_cb, NA_Q_COLS, kr * NA_K_COLS)
        s_ctx = jnp.einsum('bnqhd,bchd->bhnqc', qr, kc, preferred_element_type=jnp.float32) * scale
        p = jax.nn.softmax(jnp.concatenate([s, s_ctx], axis=-1), axis=-1)
        n_loc = kr * NA_K_COLS
        p_loc = p[..., :n_loc].reshape(B, N_HEADS_B, n_cb, NA_Q_COLS, kr, NA_K_COLS).astype(v.dtype)
        p_ctx = p[..., n_loc:].astype(v.dtype)
        o = jnp.einsum('bhnqac,banchd->bnqhd', p_loc, vblk) + jnp.einsum('bhnqc,bchd->bnqhd', p_ctx, vc)
        return o.reshape(B, GRID_W, WIDTH_B)

    out = lax.map(row_block, jnp.arange(rows_n))
    return jnp.moveaxis(out, 0, 1).reshape(B, L, WIDTH_B)

def context_attention(q, k, v, sink):
    B, C, Hq, _ = q.shape
    Hkv = k.shape[2]
    G = Hq // Hkv
    qg = q.reshape(B, C, Hkv, G, HEAD_DIM)
    s = jnp.einsum('bqkgd,bckd->bkgqc', qg, k, preferred_element_type=jnp.float32) * HEAD_DIM ** -0.5
    if sink is not None:
        sink_g = sink.astype(jnp.float32).reshape(Hkv, G)[None, :, :, None, None]
        s = jnp.concatenate([s, jnp.broadcast_to(sink_g, s.shape[:-1] + (1,))], axis=-1)
    p = jax.nn.softmax(s, axis=-1)[..., :C].astype(v.dtype)
    o = jnp.einsum('bkgqc,bckd->bqkgd', p, v)
    return o.reshape(B, C, Hq * HEAD_DIM)

def moe_ffn(h, w_router, b_router, w1, b1, w2, b2):
    B, T, D = h.shape
    n_tok = B * T
    t = h.reshape(n_tok, D)
    logits = jnp.dot(t, w_router, preferred_element_type=jnp.float32) + b_router.astype(jnp.float32)
    top_val, top_idx = lax.top_k(logits, TOP_K)
    top_w = jax.nn.softmax(top_val, axis=-1)
    n_assign = n_tok * TOP_K
    flat_e = top_idx.reshape(-1)
    flat_tok = jnp.repeat(jnp.arange(n_tok, dtype=jnp.int32), TOP_K)
    flat_w = top_w.reshape(-1)
    order = jnp.argsort(flat_e)
    sorted_e = flat_e[order]
    counts = jnp.bincount(flat_e, length=N_EXPERTS)
    padded = (counts + MOE_BLOCK - 1) // MOE_BLOCK * MOE_BLOCK
    pad_end = jnp.cumsum(padded)
    pad_start = pad_end - padded
    grp_start = jnp.cumsum(counts) - counts
    dest = pad_start[sorted_e] + (jnp.arange(n_assign) - grp_start[sorted_e])
    n_blocks = -(-n_assign // MOE_BLOCK) + N_EXPERTS
    n_rows = n_blocks * MOE_BLOCK
    row_tok = jnp.zeros((n_rows,), jnp.int32).at[dest].set(flat_tok[order])
    row_w = jnp.zeros((n_rows,), jnp.float32).at[dest].set(flat_w[order])
    blk_expert = jnp.minimum(jnp.searchsorted(pad_end, jnp.arange(n_blocks) * MOE_BLOCK, side='right'), N_EXPERTS - 1)

    def expert_block(args):
        idx, e = args
        xb = t[idx]
        hu = xb @ w1[e] + b1[e]
        glu = jnp.minimum(hu[:, 0::2], SWIGLU_LIMIT)
        lin = jnp.clip(hu[:, 1::2], -SWIGLU_LIMIT, SWIGLU_LIMIT)
        act = glu * jax.nn.sigmoid(SWIGLU_ALPHA * glu) * (lin + 1)
        return act @ w2[e] + b2[e]

    y = lax.map(expert_block, (row_tok.reshape(n_blocks, MOE_BLOCK), blk_expert))
    y = y.reshape(n_rows, D) * row_w[:, None].astype(y.dtype)
    out = jax.ops.segment_sum(y, row_tok, num_segments=n_tok)
    return out.reshape(B, T, D)

def setup_inputs(seed: int = 0) -> dict:
    key = jax.random.key(seed)
    ks = jax.random.split(key, 22)
    f32 = jnp.float32

    def nrm(k, shape, s):
        return jax.random.normal(k, shape, f32) * s

    def gain(k, shape):
        return 1.0 + 0.05 * jax.random.normal(k, shape, f32)

    return {
        'x': nrm(ks[0], (BATCH, SEQ, D_MODEL), 1.0),
        'c': nrm(ks[1], (BATCH, D_MODEL), 1.0),
        'ctx': nrm(ks[2], (BATCH, CTX_LEN, D_MODEL), 1.0),
        'c_ctx': nrm(ks[3], (D_MODEL,), 1.0),
        'w_ada': nrm(ks[4], (DEPTH, D_MODEL, 6 * D_MODEL), 0.5 * D_MODEL ** -0.5),
        'b_ada': nrm(ks[5], (DEPTH, 6 * D_MODEL), 0.01),
        'g_pre_mix': gain(ks[6], (DEPTH, D_MODEL)),
        'g_post_mix': gain(ks[7], (DEPTH, D_MODEL)),
        'g_pre_ffn': gain(ks[8], (DEPTH, D_MODEL)),
        'g_post_ffn': gain(ks[9], (DEPTH, D_MODEL)),
        'w_in': nrm(ks[10], (DEPTH, D_MODEL, IN_WIDTH), D_MODEL ** -0.5),
        'g_grp_a': gain(ks[11], (DEPTH, WIDTH_A)),
        'g_grp_b': gain(ks[12], (DEPTH, WIDTH_B)),
        'sink_a': nrm(ks[13], (DEPTH, N_HEADS_A), 0.5),
        'rpb_b': nrm(ks[14], (DEPTH, N_HEADS_B, 2 * NA_ROWS - 1, 2 * NA_COLS - 1), 0.2),
        'w_out': nrm(ks[15], (DEPTH, MIX_WIDTH, D_MODEL), MIX_WIDTH ** -0.5),
        'w_router': nrm(ks[16], (DEPTH, D_MODEL, N_EXPERTS), D_MODEL ** -0.5),
        'b_router': nrm(ks[17], (DEPTH, N_EXPERTS), 0.01),
        'w_mlp1': nrm(ks[18], (DEPTH, N_EXPERTS, D_MODEL, 2 * D_FF_EXPERT), D_MODEL ** -0.5),
        'b_mlp1': nrm(ks[19], (DEPTH, N_EXPERTS, 2 * D_FF_EXPERT), 0.01),
        'w_mlp2': nrm(ks[20], (DEPTH, N_EXPERTS, D_FF_EXPERT, D_MODEL), D_FF_EXPERT ** -0.5),
        'b_mlp2': nrm(ks[21], (DEPTH, N_EXPERTS, D_MODEL), 0.01),
    }

def reference(x, c, ctx, c_ctx, w_ada, b_ada, g_pre_mix, g_post_mix, g_pre_ffn, g_post_ffn,
              w_in, g_grp_a, g_grp_b, sink_a, rpb_b, w_out, w_router, b_router,
              w_mlp1, b_mlp1, w_mlp2, b_mlp2):
    B, L, _ = x.shape
    pos = jnp.arange(L)
    rows = (pos // GRID_W).astype(jnp.float32)
    cols = (pos % GRID_W).astype(jnp.float32)
    n_freq = HEAD_DIM // 4
    freqs = ROPE_BASE ** (-jnp.arange(n_freq, dtype=jnp.float32) / n_freq)
    ang_row = rows[:, None] * freqs[None, :]
    ang_col = cols[:, None] * freqs[None, :]

    for layer in range(DEPTH):
        mod = (jax.nn.silu(c) @ w_ada[layer] + b_ada[layer])[:, None, :]
        mod_c = jax.nn.silu(c_ctx) @ w_ada[layer] + b_ada[layer]
        sh1, sc1, ga1, sh2, sc2, ga2 = jnp.split(mod, 6, axis=-1)
        csh1, csc1, cga1, csh2, csc2, cga2 = jnp.split(mod_c, 6, axis=-1)

        h = modulate(rmsnorm(x, g_pre_mix[layer]), sh1, sc1)
        hc = modulate(rmsnorm(ctx, g_pre_mix[layer]), csh1, csc1)
        qa, ka, va, qb, kb, vb = split_projection(h @ w_in[layer])
        qac, kac, vac, qbc, kbc, vbc = split_projection(hc @ w_in[layer])
        qa = axial_rope(qa, ang_row, ang_col)
        ka = axial_rope(ka, ang_row, ang_col)
        oa = window_attention(qa, ka, va, kac, vac, sink_a[layer])
        ob = neighbourhood_attention(qb, kb, vb, kbc, vbc, rpb_b[layer])
        mix = jnp.concatenate([rmsnorm(oa, g_grp_a[layer]), rmsnorm(ob, g_grp_b[layer])], axis=-1) @ w_out[layer]
        x = x + ga1 * rmsnorm(mix, g_post_mix[layer])

        h2 = modulate(rmsnorm(x, g_pre_ffn[layer]), sh2, sc2)
        y = moe_ffn(h2, w_router[layer], b_router[layer], w_mlp1[layer], b_mlp1[layer], w_mlp2[layer], b_mlp2[layer])
        x = x + ga2 * rmsnorm(y, g_post_ffn[layer])

        if layer < DEPTH - 1:
            oac = context_attention(qac, kac, vac, sink_a[layer])
            obc = context_attention(qbc, kbc, vbc, None)
            mixc = jnp.concatenate([rmsnorm(oac, g_grp_a[layer]), rmsnorm(obc, g_grp_b[layer])], axis=-1) @ w_out[layer]
            ctx = ctx + cga1 * rmsnorm(mixc, g_post_mix[layer])
            h2c = modulate(rmsnorm(ctx, g_pre_ffn[layer]), csh2, csc2)
            yc = moe_ffn(h2c, w_router[layer], b_router[layer], w_mlp1[layer], b_mlp1[layer], w_mlp2[layer], b_mlp2[layer])
            ctx = ctx + cga2 * rmsnorm(yc, g_post_ffn[layer])
    return x


_drawn_inputs = setup_inputs


def setup_inputs(seed=0):
    import zlib

    import numpy as np

    out = dict(_drawn_inputs(seed))
    spreads = {}
    factors = {'g_post_ffn': 3.78,
     'sink_a': 8.0,
     'rpb_b': 2.883,
     'b_router': 3.642,
     'b_mlp1': 8.0,
     'b_mlp2': 8.0}
    for name, (base, spread) in spreads.items():
        noise = np.random.default_rng([zlib.crc32(name.encode()), seed]).standard_normal(out[name].shape)
        drawn = base * np.exp(spread * noise) if base else spread * noise
        out[name] = __import__('jax').numpy.asarray(drawn.astype(out[name].dtype))
    for name, factor in factors.items():
        out[name] = (out[name] * factor).astype(out[name].dtype)
    return out
```

```python
import concourse.bass as bass
from concourse import mybir
from contextlib import ExitStack
import numpy as np

F32 = mybir.dt.float32
F32R = mybir.dt.float32r
BF16 = mybir.dt.bfloat16
I32 = mybir.dt.int32
U32 = mybir.dt.uint32
ALU = mybir.AluOpType
ACT = mybir.ActivationFunctionType
AX = mybir.AxisListType

P = 128
D = 1024
KD = D // P
SEQ, CTX = 1024, 256
T = SEQ // P
TC = CTX // P
HD = 64
NHA, NKVA, NHB = 8, 2, 8
NH = NHA + NHB
GRID_W, GRID_H = 64, SEQ // 64
NA_ROWS, NA_COLS = 8, 16
WINDOW = 128
IN_W = 2304
E, TOPK, FF = 32, 4, 1024
EPS = 1e-6
LIMIT, ALPHA = 7.0, 1.702
NEG = -1e30
UNIT = 512
LA = P + 2 * WINDOW
LBR = 10
LB = LBR * GRID_W
RPB_R, RPB_C = 2 * NA_ROWS - 1, 2 * NA_COLS - 1
BROWS = NHB * RPB_R + 4
BW = GRID_W + RPB_C - 1
MAXB = E + (SEQ * TOPK - E) // P + 1
SLOTS = (MAXB + 1) * P


def constants():
    f = np.float32
    out = {}
    out["k_ident"] = np.eye(P, dtype=f)
    d = np.arange(P)
    partner = np.where((d % 32) < 16, d + 16, d - 16)
    perm = np.zeros((P, P), f)
    perm[partner, d] = 1
    out["k_perm"] = perm
    pos = np.arange(SEQ)
    rows, cols = (pos // GRID_W).astype(f), (pos % GRID_W).astype(f)
    nf = HD // 4
    freqs = (f(10000.0) ** (-np.arange(nf, dtype=f) / f(nf))).astype(f)
    fr = freqs[d % 16]
    isrow = (d % HD) < 32
    ang = np.where(isrow[:, None], fr[:, None] * rows[None], fr[:, None] * cols[None]).astype(f)
    sign = np.where((d % 32) < 16, -1.0, 1.0).astype(f)
    out["k_cos"] = np.cos(ang).astype(f)
    out["k_sin"] = (np.sin(ang) * sign[:, None]).astype(f)
    mask_a = np.zeros((T, P, LA + CTX), f)
    mask_b = np.zeros((T, P, LB), f)
    tab = np.zeros((T, 4), np.int32)
    for i in range(T):
        k0 = min(max(i - 1, 0), T - 3) * P
        q = i * P + np.arange(P)
        k = k0 + np.arange(LA)
        mask_a[i, :, :LA] = np.where(np.abs(k[None] - q[:, None]) <= WINDOW, 0, NEG)
        base = min(max(2 * i - NA_ROWS // 2, 0), GRID_H - LBR)
        r, qc = q // GRID_W, q % GRID_W
        rs = np.clip(r - NA_ROWS // 2, 0, GRID_H - NA_ROWS)
        cs = np.clip(qc - NA_COLS // 2, 0, GRID_W - NA_COLS)
        kr, kc = base + np.arange(LBR), np.arange(GRID_W)
        ok = ((kr[None] >= rs[:, None]) & (kr[None] < rs[:, None] + NA_ROWS))[:, :, None] & \
             ((kc[None] >= cs[:, None]) & (kc[None] < cs[:, None] + NA_COLS))[:, None, :]
        mask_b[i] = np.where(ok, 0, NEG).reshape(P, LB)
        tab[i] = (k0, base * GRID_W, base - 2 * i + 7 + 2, base - 2 * i - 1 + 7 + 2)
    out["k_mask_a"], out["k_mask_b"] = mask_a, mask_b
    out["k_tiles"] = tab.reshape(1, 4 * T)
    out["k_tri"] = np.triu(np.ones((P, P), f), 1)
    out["k_iota"] = np.broadcast_to(np.arange(P, dtype=f), (P, P)).copy()
    out["k_zeros"] = np.zeros((1, BROWS * BW), f)
    out["k_onehot"] = (np.arange(96)[:, None] % E == np.arange(E)[None]).astype(f)
    token = np.arange(P)[:, None, None] + P * np.arange(T)[None, None]
    record = np.stack(np.broadcast_arrays(token, token + SEQ * np.arange(TOPK)[None, :, None]), axis=-1)
    out["k_record"] = record.reshape(P, TOPK * T * 2).astype(np.int32)
    spare = TOPK * SEQ + np.arange(SLOTS) % P
    out["k_empty"] = np.stack([0 * spare, spare], axis=-1).astype(np.int32)
    return out


def raw_ap(ap, offset, dims):
    return bass.AP(tensor=ap.tensor, offset=offset, ap=dims)


class Kernel:

    def __init__(self, nc, io, dbg=None):
        self.nc, self.io, self.dbg = nc, io, dbg or {}

    def build(self, upto=9):
        nc, io = self.nc, self.io
        with ExitStack() as ctx:
            self.psum = ctx.enter_context(nc.psum_tensor("psum", [P, 8, 512], F32))
            self.ident = ctx.enter_context(nc.sbuf_tensor("ident", [P, P], F32))
            self.eps = ctx.enter_context(nc.sbuf_tensor("eps", [P, 1], F32))
            self.colv = ctx.enter_context(nc.sbuf_tensor("colv", [P, 48], F32))
            self.weights = ctx.enter_context(nc.sbuf_tensor("route_w", [P, T, TOPK], F32))
            self.slots = ctx.enter_context(nc.sbuf_tensor("route_slot", [P, TOPK, T], I32))
            self.table = ctx.enter_context(nc.sbuf_tensor("block_table", [1, 80], I32))
            dram = lambda n, s, d=F32: nc.dram_tensor(n, s, d, kind="Internal").ap()
            self.mod_d = dram("mod_d", (2, 6 * D))
            self.skew_d = dram("skew_d", (GRID_W, BROWS, BW))
            self.bias_d = dram("bias_d", (GRID_W, BROWS, GRID_W))
            self.mix_d = dram("mix_d", (SEQ, D))
            self.x1_d = dram("x1_d", (SEQ, D))
            self.h2_d = dram("h2_d", (SEQ, D))
            self.slot_d = dram("slot_d", (SLOTS, 2), I32)
            self.y_d = dram("y_d", (TOPK * SEQ + P, D))
            with ExitStack() as early:
              self.ring = early.enter_context(nc.sbuf_tensor("ring", [P, 2, KD, UNIT], F32))
              with ExitStack() as qkv:
                  self.qa = qkv.enter_context(nc.sbuf_tensor("qaT", [P, 4, SEQ], F32))
                  self.ka = qkv.enter_context(nc.sbuf_tensor("kaT", [P, SEQ + CTX], F32))
                  self.qb = qkv.enter_context(nc.sbuf_tensor("qbT", [P, 4, SEQ], F32))
                  self.kb = qkv.enter_context(nc.sbuf_tensor("kbT", [P, 4, SEQ + CTX], F32))
                  self.v = qkv.enter_context(nc.sbuf_tensor("v", [P, T + TC, NKVA * HD + NHB * HD], F32))
                  front(self)
                  if upto >= 2:
                      attention(self)
              if upto >= 3:
                  middle(self)
            if upto >= 4:
                experts(self)
            if upto >= 5:
                combine(self)


def scope(nc, ctx):
    sb = lambda name, shape, dt=F32: ctx.enter_context(nc.sbuf_tensor(name, shape, dt))
    sem = lambda name: ctx.enter_context(nc.semaphore(name))
    return sb, sem


def linker(engine, sem, base=0):
    n = [0]

    def link(ins):
        n[0] += 1
        ins.then_inc(sem, 1)
        engine.wait_ge(sem, base + n[0])
    link.count = n
    return link


def front(K):
    nc, io, ps, ring = K.nc, K.io, K.psum, K.ring
    w_ada = io["w_ada"][0].rearrange("(k p) n -> p k n", p=P)
    w_in = io["w_in"][0].rearrange("(k p) n -> p k n", p=P)
    ctx = ExitStack()
    with ctx:
        sb, sem = scope(nc, ctx)
        hT = sb("hT", [P, KD, SEQ + CTX])
        xin = sb("xin", [P, 2, D])
        modrow = sb("modrow", [2, 6 * D])
        cosT, sinT = sb("cosT", [P, SEQ]), sb("sinT", [P, SEQ])
        perm = sb("perm", [P, P])
        raw = sb("raw", [P, 2, UNIT])
        squares = raw[:, :, :].rearrange("p a n -> p (a n)")
        rot = sb("rot", [P, 2, UNIT])
        crow = sb("crow", [16, P])
        csig = sb("csig", [16, P])
        csilu = sb("csilu", [16, P])
        cT = sb("cT", [P, 16])
        modc = sb("modc", [48, P])
        aff = sb("aff", [P, 2, 2, KD])
        stat = sb("stat", [P, 2, 3])

        const_loaded, ident_loaded, c_loaded, b_loaded = sem("const_loaded"), sem("ident_loaded"), sem("c_loaded"), sem("b_loaded")
        mod_stored_late = sem("mod_stored_late")
        unit_loaded = [sem("unit_loaded0"), sem("unit_loaded1")]
        unit_used = sem("unit_used")
        x_loaded = [sem("x_loaded0"), sem("x_loaded1")]
        x_scaled, xt_done, ht_done = sem("x_scaled"), sem("xt_done"), sem("ht_done")
        ss_done, rms_done, rstd_done = sem("ss_done"), sem("rms_done"), sem("rstd_done")
        sig_done, silu_done, ct_done, ct_copied = sem("sig_done"), sem("silu_done"), sem("ct_done"), sem("ct_copied")
        ada_done, mod_done, mod_stored = sem("ada_done"), sem("mod_done"), sem("mod_stored")
        modc_loaded, modc_t, aff_done = sem("modc_loaded"), sem("modc_t"), sem("aff_done")
        group_done, group_copied = sem("group_done"), sem("group_copied")
        perm_done, rope_done = sem("perm_done"), sem("rope_done")
        eps_set, empty_stored, skew_zeroed, skew_stored = sem("eps_set"), sem("empty_stored"), sem("skew_zeroed"), sem("skew_stored")
        bias_stored, dve_own = sem("bias_stored"), sem("dve_own")

        units = [("ada", u) for u in range(4)] + [("in", u) for u in range(5)] + [("ada", u) for u in range(4, 12)]
        groups = []
        for u, tiles in enumerate([[("qa", j) for j in range(4)],
                                   [("ka", 0), ("va", 0), ("qb", 0), ("qb", 1)],
                                   [("qb", 2), ("qb", 3), ("kb", 0), ("kb", 1)],
                                   [("kb", 2), ("kb", 3), ("vb", 0)],
                                   [("vb", 1)]]):
            col = 0
            for kind, j in tiles:
                width = 2 * P if kind == "vb" else P
                if kind in ("va", "vb"):
                    groups += [(u, kind, j, col, tt, width) for tt in range(T + TC)]
                else:
                    groups += [(u, kind, j, col, hf, UNIT) for hf in range(2)]
                    if kind in ("ka", "kb"):
                        groups.append((u, kind, j, col, 2, CTX))
                col += width
        ropes = [g for g, x in enumerate(groups) if x[1] in ("qa", "ka") and x[4] < 2]

        block = ctx.enter_context(nc.Block())

        @block.sync
        def _(sp):
            sp.dma_start(crow[0:8, :], io["c"][0].rearrange("(k p) -> k p", p=P)).then_inc(c_loaded, 16)
            sp.dma_start(crow[8:16, :], io["c_ctx"].rearrange("(k p) -> k p", p=P)).then_inc(c_loaded, 16)
            sp.dma_start(K.ident[:, :], io["k_ident"]).then_inc(ident_loaded, 16)

            def load_x(t):
                if t >= 2:
                    sp.wait_ge(xt_done, t - 1)
                src = io["x"][0][t * P:(t + 1) * P, :] if t < T else io["ctx"][0][(t - T) * P:(t - T + 1) * P, :]
                sp.dma_start(xin[:, t % 2, :], src).then_inc(x_loaded[t % 2], 16)

            load_x(0)
            load_x(1)
            for n, (kind, u) in enumerate(units):
                if n >= 2:
                    sp.wait_ge(unit_used, n - 1)
                src = w_ada if kind == "ada" else w_in
                cols = min(UNIT, src.shape[2] - u * UNIT)
                sp.dma_start(ring[:, n % 2, :, 0:cols], src[:, :, u * UNIT:u * UNIT + cols]).then_inc(unit_loaded[n % 2], 16)
                if n == 5:
                    for t in range(2, T + TC):
                        load_x(t)
            sp.wait_ge(mod_done, 12)
            sp.dma_start(K.mod_d[:, 2 * D:], modrow[:, 2 * D:]).then_inc(mod_stored_late, 16)
            sp.wait_ge(mod_stored_late, 16)
            sp.wait_ge(bias_stored, 16)

        @block.gpsimd
        def _(pool):
            pool.memset(K.eps[:, :], EPS).then_inc(eps_set, 1)
            for dst, src in ((perm[:, :], io["k_perm"]), (cosT[:, :], io["k_cos"]), (sinT[:, :], io["k_sin"])):
                pool.dma_start(dst, src).then_inc(const_loaded, 16)
            for r in range(2):
                pool.dma_start(modrow[r:r + 1, :], io["b_ada"]).then_inc(b_loaded, 16)
            for r, name in ((32, "g_pre_mix"), (40, "g_grp_a"), (44, "g_grp_b")):
                n = io[name].shape[1] // P
                pool.dma_start(modc[r:r + n, :], io[name][0].rearrange("(k p) -> k p", p=P)).then_inc(modc_loaded, 16)
            pool.dma_start(K.slot_d, io["k_empty"]).then_inc(empty_stored, 16)
            pool.dma_start(K.skew_d.rearrange("q n k -> q (n k)"), io["k_zeros"].to_broadcast([GRID_W, BROWS * BW])).then_inc(skew_zeroed, 16)
            pool.wait_ge(skew_zeroed, 16)
            rpb = raw_ap(io["rpb_b"], 0, [[0, GRID_W], [RPB_C, NHB * RPB_R], [1, RPB_C]])
            pool.dma_start(raw_ap(K.skew_d, 2 * BW, [[BROWS * BW + 1, GRID_W], [BW, NHB * RPB_R], [1, RPB_C]]), rpb).then_inc(skew_stored, 16)
            pool.wait_ge(skew_stored, 16)
            pool.dma_start(K.bias_d, K.skew_d[:, :, NA_COLS - 1:NA_COLS - 1 + GRID_W]).then_inc(bias_stored, 16)
            pool.wait_ge(empty_stored, 16)
            pool.wait_ge(mod_done, 4)
            pool.dma_start(K.mod_d[:, 0:2 * D], modrow[:, 0:2 * D]).then_inc(mod_stored, 16)
            pool.wait_ge(mod_stored, 16)
            for r in range(2):
                pool.dma_start(modc[16 * r:16 * r + 16, :], K.mod_d[r, 0:2 * D].rearrange("(n p) -> n p", p=P)).then_inc(modc_loaded, 16)
            pool.wait_ge(modc_loaded, 80)

        @block.scalar
        def _(act):
            act.wait_ge(c_loaded, 32)
            act.activation(csig[:, :], crow[:, :], ACT.Sigmoid).then_inc(sig_done, 1)
            act.wait_ge(eps_set, 1)
            for t in range(T + TC):
                act.wait_ge(x_loaded[t % 2], 16 * (t // 2 + 1))
                if t:
                    act.wait_ge(ss_done, t)
                if t >= 2:
                    act.wait_ge(x_scaled, t - 1)
                act.activation(squares, xin[:, t % 2, :], ACT.Square, accum_out=stat[:, t % 2, 0:1]).then_inc(ss_done, 1)
                act.wait_ge(ss_done, t + 1)
                act.activation(stat[:, t % 2, 1:2], stat[:, t % 2, 0:1], ACT.Sqrt, bias=K.eps[:, :], scale=1.0 / D).then_inc(rms_done, 1)
            rope = 0
            for g, (u, kind, j, col, part, width) in enumerate(groups):
                bank = g % 4
                act.wait_ge(group_done, g + 1)
                if kind in ("qa", "ka") and part < 2:
                    if rope >= 2:
                        act.wait_ge(rope_done, rope - 1)
                    act.activation(raw[:, rope % 2, :], ps[:, bank, :], ACT.Copy, scale=HD ** -0.5 if kind == "qa" else 1.0).then_inc(group_copied, 1)
                    rope += 1
                    continue
                if kind == "ka":
                    dst = K.ka[:, SEQ:]
                elif kind == "qb":
                    dst = K.qb[:, j, part * UNIT:part * UNIT + width]
                elif kind == "kb":
                    dst = K.kb[:, j, part * UNIT:part * UNIT + width]
                elif kind == "va":
                    dst = K.v[:, part, 0:P]
                else:
                    dst = K.v[:, part, P + j * width:P + (j + 1) * width]
                act.activation(dst, ps[:, bank, 0:width], ACT.Copy, scale=HD ** -0.5 if kind == "qb" else 1.0).then_inc(group_copied, 1)

        @block.vector
        def _(dve):
            link = linker(dve, dve_own)
            dve.wait_ge(sig_done, 1)
            dve.tensor_tensor(csilu[:, :], crow[:, :], csig[:, :], ALU.mult).then_inc(silu_done, 1)
            dve.wait_ge(ct_done, 1)
            dve.tensor_copy(cT[:, :], ps[:, 2, 0:16]).then_inc(ct_copied, 1)
            dve.wait_ge(b_loaded, 32)

            def ada(u):
                dve.wait_ge(ada_done, u + 1)
                row = modrow[0:2, u * UNIT:(u + 1) * UNIT]
                dve.tensor_tensor(row, ps[0:2, u % 2, :], row, ALU.add).then_inc(mod_done, 1)

            def scale(t):
                dve.wait_ge(rms_done, t + 1)
                link(dve.reciprocal(stat[:, t % 2, 2:3], stat[:, t % 2, 1:2]))
                dve.tensor_scalar(xin[:, t % 2, :], xin[:, t % 2, :], stat[:, t % 2, 2:3], None, ALU.mult).then_inc(x_scaled, 1)

            for u in range(4):
                ada(u)
            scale(0)
            scale(1)
            dve.wait_ge(modc_t, 1)
            link(dve.tensor_copy(K.colv[:, :], ps[:, 2, 0:48]))
            for r in range(2):
                dve.scalar_tensor_tensor(aff[:, r, 0, :], K.colv[:, 16 * r + 8:16 * r + 16], 1.0, K.colv[:, 32:40], ALU.add, ALU.mult).then_inc(aff_done, 1)
                dve.tensor_copy(aff[:, r, 1, :], K.colv[:, 16 * r:16 * r + 8]).then_inc(aff_done, 1)
            dve.wait_ge(aff_done, 4)
            for t in range(T + TC):
                r = 0 if t < T else 1
                dve.wait_ge(xt_done, t + 1)
                for k in range(KD):
                    last = dve.tensor_scalar(hT[:, k, t * P:(t + 1) * P], ps[:, 4 + 2 * (t % 2) + k // 4, (k % 4) * P:(k % 4 + 1) * P],
                                             aff[:, r, 0, k:k + 1], aff[:, r, 1, k:k + 1], ALU.mult, ALU.add)
                last.then_inc(ht_done, 1)
                if t + 2 < T + TC:
                    scale(t + 2)
            dve.wait_ge(const_loaded, 48)
            for n, g in enumerate(ropes):
                _, kind, j, _, hf, _ = groups[g]
                cols = slice(hf * UNIT, (hf + 1) * UNIT)
                dve.wait_ge(group_copied, g + 1)
                link(dve.tensor_tensor(rot[:, 0, :], raw[:, n % 2, :], cosT[:, cols], ALU.mult))
                dve.wait_ge(perm_done, n + 1)
                link(dve.tensor_tensor(rot[:, 1, :], ps[:, 4 + n % 2, :], sinT[:, cols], ALU.mult))
                if kind == "qa":
                    for half in range(2):
                        head, src = 2 * j + half, slice(HD * half, HD * half + HD)
                        g0 = HD * (head // (NHA // NKVA))
                        last = dve.tensor_tensor(K.qa[g0:g0 + HD, head % 4, cols], rot[src, 0, :], rot[src, 1, :], ALU.add)
                else:
                    last = dve.tensor_tensor(K.ka[:, cols], rot[:, 0, :], rot[:, 1, :], ALU.add)
                last.then_inc(rope_done, 1)
                dve.wait_ge(rope_done, n + 1)
            for u in range(4, 12):
                ada(u)

        @block.tensor
        def _(pe):
            pe.wait_ge(silu_done, 1)
            pe.wait_ge(const_loaded, 48)
            pe.wait_ge(ident_loaded, 16)
            pe.transpose(ps[:, 2, 0:16], csilu[:, :], K.ident[0:16, 0:16]).then_inc(ct_done, 1)
            pe.wait_ge(ct_copied, 1)
            cols = cT[:, :].rearrange("p (v k) -> p k v", v=2)

            def ada(n, u):
                pe.wait_ge(unit_loaded[n % 2], 16 * (n // 2 + 1))
                if u >= 2:
                    pe.wait_ge(mod_done, u - 1)
                for k in range(KD):
                    last = pe.matmul(ps[0:2, u % 2, :], cols[:, k, :], ring[:, n % 2, k, :], start=(k == 0), stop=(k == KD - 1))
                last.then_inc(ada_done, 1)
                pe.wait_ge(ada_done, u + 1)
                pe.sem_inc(unit_used, 1)

            for n in range(4):
                ada(n, units[n][1])
            pe.wait_ge(modc_loaded, 80)
            pe.transpose(ps[:, 2, 0:48], modc[:, :], K.ident[0:48, 0:48]).then_inc(modc_t, 1)
            for t in range(T + TC):
                pe.wait_ge(x_scaled, t + 1)
                if t >= 2:
                    pe.wait_ge(ht_done, t - 1)
                for k in range(KD):
                    last = pe.transpose(ps[:, 4 + 2 * (t % 2) + k // 4, (k % 4) * P:(k % 4 + 1) * P], xin[:, t % 2, k * P:(k + 1) * P], K.ident[:, :])
                last.then_inc(xt_done, 1)
            pe.wait_ge(ht_done, T + TC)
            pe.wait_ge(mod_done, 4)
            pe.wait_ge(aff_done, 4)
            rope = 0

            def rotate(n, g):
                pe.wait_ge(group_copied, g + 1)
                if n >= 2:
                    pe.wait_ge(rope_done, n - 1)
                pe.matmul(ps[:, 4 + n % 2, :], perm[:, :], raw[:, n % 2, :], start=True, stop=True).then_inc(perm_done, 1)

            pending = None
            for g, (u, kind, j, col, part, width) in enumerate(groups):
                n = 4 + u
                slot = n % 2
                if g == 0 or groups[g - 1][0] != u:
                    pe.wait_ge(unit_loaded[slot], 16 * (n // 2 + 1))
                if g >= 4:
                    pe.wait_ge(group_copied, g - 3)
                for k in range(KD):
                    if kind in ("va", "vb"):
                        lhs, rhs = hT[:, k, part * P:(part + 1) * P], ring[:, slot, k, col:col + width]
                    else:
                        lhs, rhs = ring[:, slot, k, col:col + P], hT[:, k, part * UNIT:part * UNIT + width]
                    last = pe.matmul(ps[:, g % 4, 0:width], lhs, rhs, start=(k == 0), stop=(k == KD - 1))
                last.then_inc(group_done, 1)
                if g + 1 == len(groups) or groups[g + 1][0] != u:
                    pe.wait_ge(group_done, g + 1)
                    pe.sem_inc(unit_used, 1)
                if pending is not None:
                    rotate(*pending)
                    pending = None
                if g in ropes:
                    pending = (ropes.index(g), g)
            pe.wait_ge(group_copied, len(groups))
            for n in range(9, 17):
                ada(n, units[n][1])


def attention(K):
    nc, io, ps, ring = K.nc, K.io, K.psum, K.ring
    w_out = io["w_out"][0].rearrange("(k p) n -> p k n", p=P)
    ctx = ExitStack()
    with ctx:
        sb, sem = scope(nc, ctx)
        qz = sb("qz", [P, NH, P])
        bias = sb("bias", [P, NHB, LB])
        mask_a, mask_b = sb("mask_a", [P, LA + CTX]), sb("mask_b", [P, LB])
        zeros = sb("zeros", [P, CTX])
        S = sb("S", [P, 2, LB + CTX])
        PT = sb("PT", [P, 2, 7 * P])
        o = sb("o", [P, 2, NHA * HD])
        squares = sb("squares", [P, NHA * HD])
        sink = sb("sink", [P, NHA])
        negm, den, sinkd, sinke, rden = sb("negm", [P, NH]), sb("den", [P, NH]), sb("sinkd", [P, NHA]), sb("sinke", [P, NHA]), sb("rden", [P, NH])
        mx = sb("mx", [P, NH, 2])
        stat = sb("stat2", [P, 2, 3])
        gate = sb("gate", [P, 1])
        tiles = sb("tiles", [1, 4 * T], I32)

        tiles_loaded, sink_loaded, zeros_set, qz_set = sem("tiles_loaded"), sem("sink_loaded"), sem("zeros_set"), sem("qz_set")
        mask_a_loaded, bias_loaded, wout_loaded = sem("mask_a_loaded"), sem("bias_loaded"), sem("wout_loaded")
        mask_a_free, bias_free, q_free, o_free = sem("mask_a_free"), sem("bias_free"), sem("q_free"), sem("o_free")
        q_ready, bias_ready = sem("q_ready"), sem("bias_ready")
        s_done, s_masked, p_done, pt_done, pt_low, pt_high, pv_done = (sem(n) for n in ("s_done", "s_masked", "p_done", "pt_done", "pt_low", "pt_high", "pv_done"))
        sinkd_done, sinke_done, o_scaled, rms_done, o_done, o_stored = (sem(n) for n in ("sinkd_done", "sinke_done", "o_scaled", "rms2_done", "o_done", "o_stored"))
        dve_own, act_own = sem("dve_own2"), sem("act_own2")
        DVE_OWN, ACT_OWN = NH + 5, 2

        block = ctx.enter_context(nc.Block())

        @block.sync
        def _(sp):
            sp.dma_start(tiles[:, :], io["k_tiles"]).then_inc(tiles_loaded, 16)
            for n in range(2):
                sp.dma_start(ring[:, n, :, :], w_out[:, :, n * UNIT:(n + 1) * UNIT]).then_inc(wout_loaded, 16)
            sp.wait_ge(tiles_loaded, 16)
            with sp.Fori(0, T) as i:
                sp.wait_ge(mask_a_free, i + 1)
                sp.dma_start(mask_a[:, :], io["k_mask_a"][bass.ds(i, 1), :, :].rearrange("a p n -> (a p) n")).then_inc(mask_a_loaded, 16)
                first = [sp.value_load(tiles[0:1, bass.ds(i * 4 + 2 + half, 1)], min_val=0, max_val=BROWS - LBR - 15 * (NHB - 1)) for half in range(2)]
                sp.wait_ge(bias_free, i + 1)
                for half in range(2):
                    src = K.bias_d.rearrange("q n k -> q (n k)")
                    src = bass.AP(tensor=src.tensor, offset=first[half] * GRID_W, ap=[[BROWS * GRID_W, GRID_W], [RPB_R * GRID_W, NHB], [1, LB]])
                    sp.dma_start(bias[GRID_W * half:GRID_W * (half + 1), :, :], src).then_inc(bias_loaded, 16)
                sp.dma_start(mask_b[:, :], io["k_mask_b"][bass.ds(i, 1), :, :].rearrange("a p n -> (a p) n")).then_inc(bias_loaded, 16)
                sp.wait_ge(o_done, 2 * i + 2)
                sp.dma_start(K.mix_d[bass.ds(i * P, P), :], o[:, :, :].rearrange("p a n -> p (a n)")).then_inc(o_stored, 16)
                sp.wait_ge(o_stored, 16 * i + 16)
                sp.sem_inc(o_free, 1)
            sp.wait_ge(o_stored, 16 * T)
            sp.wait_ge(wout_loaded, 32)

        @block.gpsimd
        def _(pool):
            pool.memset(zeros[:, :], 0.0).then_inc(zeros_set, 1)
            pool.memset(qz[:, :, :], 0.0).then_inc(qz_set, 1)
            pool.dma_start(sink[:, :], io["sink_a"].to_broadcast([P, NHA])).then_inc(sink_loaded, 16)
            pool.wait_ge(qz_set, 1)
            with pool.Fori(0, T) as i:
                pool.wait_ge(q_free, i + 1)
                for half in range(2):
                    part = slice(HD * half, HD * half + HD)
                    pool.tensor_copy(qz[part, 4 * half:4 * half + 4, :], K.qa[part, :, bass.ds(i * P, P)])
                    last = pool.tensor_copy(qz[part, NHA + half:NH:2, :], K.qb[part, :, bass.ds(i * P, P)])
                last.then_inc(q_ready, 1)
                pool.wait_ge(q_ready, i + 1)
                pool.wait_ge(bias_loaded, 48 * i + 48)
                pool.tensor_tensor(bias[:, :, :], bias[:, :, :], mask_b[:, :].rearrange("p (a n) -> p a n", a=1).to_broadcast([P, NHB, LB]), ALU.add).then_inc(bias_ready, 1)
            pool.wait_ge(sink_loaded, 16)

        def keys(s):
            return LA + CTX if s < NHA else LB + CTX

        @block.tensor
        def _(pe):
            pe.sem_inc(q_free, 1)
            pe.wait_ge(tiles_loaded, 16)
            with pe.Fori(0, T) as i:
                k_a = pe.value_load(tiles[0:1, bass.ds(i * 4, 1)], min_val=0, max_val=SEQ - LA)
                k_b = pe.value_load(tiles[0:1, bass.ds(i * 4 + 1, 1)], min_val=0, max_val=SEQ - LB)
                pe.wait_ge(q_ready, i + 1)

                def scores(s):
                    if s >= 2:
                        pe.wait_ge(s_masked, i * NH + s - 1)
                    bank = 2 * (s % 2)
                    q = qz[:, s, :]
                    flat = ps[:, bank:bank + 2, :].rearrange("p b n -> p (b n)")
                    if s < NHA:
                        pe.matmul(flat[:, 128:512], q, K.ka[:, bass.ds(k_a, LA)], start=True, stop=True)
                        pe.matmul(flat[:, 512:768], q, K.ka[:, SEQ:], start=True, stop=True).then_inc(s_done, 1)
                    else:
                        kt = K.kb[:, (s - NHA) // 2, :]
                        pe.matmul(flat[:, 0:512], q, kt[:, bass.ds(k_b, 512)], start=True, stop=True)
                        pe.matmul(flat[:, 512:640], q, kt[:, bass.ds(k_b + 512, 128)], start=True, stop=True)
                        pe.matmul(flat[:, 640:896], q, kt[:, SEQ:], start=True, stop=True).then_inc(s_done, 1)

                def transposes(s):
                    if s >= 1:
                        pe.wait_ge(pt_low, i * NH + s)
                        pe.wait_ge(pt_high, i * NH + s)
                    pe.wait_ge(p_done, i * NH + s + 1)
                    for c in range(keys(s) // P):
                        last = pe.transpose(ps[:, 4 + c // 4, (c % 4) * P:(c % 4 + 1) * P], S[:, s % 2, c * P:(c + 1) * P], K.ident[:, :])
                    last.then_inc(pt_done, 1)

                def values(s):
                    pe.wait_ge(pt_low, i * NH + s + 1)
                    pe.wait_ge(pt_high, i * NH + s + 1)
                    chunks = keys(s) // P
                    head = s % NHA
                    col = HD * (head // (NHA // NKVA)) if s < NHA else P + HD * head
                    local = chunks - TC
                    start = k_a if s < NHA else k_b
                    for c in range(chunks):
                        row = (start >> 7) + c if c < local else None
                        v = K.v[:, bass.ds(row, 1), col:col + HD].rearrange("p a n -> p (a n)") if c < local else K.v[:, T + c - local, col:col + HD]
                        last = pe.matmul(ps[:, 6 + s // NHA, head * HD:(head + 1) * HD], PT[:, s % 2, c * P:(c + 1) * P], v, start=(c == 0), stop=(c == chunks - 1))
                    last.then_inc(pv_done, 1)

                scores(0)
                for s in range(NH):
                    if s + 1 < NH:
                        scores(s + 1)
                    if s + 1 == NH - 1:
                        pass
                    transposes(s)
                    if s >= 1:
                        values(s - 1)
                values(NH - 1)
                pe.wait_ge(pv_done, i * NH + NH)
                pe.sem_inc(q_free, 1)
                pe.wait_ge(o_scaled, 2 * i + 2)

        @block.scalar
        def _(act):
            with act.Fori(0, T) as i:
                link = linker(act, act_own, i * ACT_OWN)

                def probs(s):
                    act.wait_ge(s_masked, i * NH + s + 1)
                    act.activation(S[:, s % 2, 0:keys(s)], S[:, s % 2, 0:keys(s)], ACT.Exp, bias=negm[:, s:s + 1], accum_out=den[:, s:s + 1]).then_inc(p_done, 1)

                def evacuate(s):
                    act.wait_ge(pt_done, i * NH + s + 1)
                    if s >= 2:
                        act.wait_ge(pv_done, i * NH + s - 1)
                    act.activation(PT[:, s % 2, 0:512], ps[:, 4, :], ACT.Copy).then_inc(pt_low, 1)

                def rms(g):
                    act.wait_ge(o_scaled, 2 * i + g + 1)
                    link(act.activation(squares[:, :], o[:, g, :], ACT.Square, accum_out=stat[:, g, 0:1]))
                    act.activation(stat[:, g, 1:2], stat[:, g, 0:1], ACT.Sqrt, bias=K.eps[:, :], scale=1.0 / (NHA * HD)).then_inc(rms_done, 1)

                for s in range(NH):
                    probs(s)
                    if s >= 1:
                        evacuate(s - 1)
                    if s == NHA:
                        act.wait_ge(sinkd_done, i + 1)
                        act.activation(sinke[:, :], sinkd[:, :], ACT.Exp).then_inc(sinke_done, 1)
                evacuate(NH - 1)
                rms(0)
                rms(1)

        @block.vector
        def _(dve):
            dve.sem_inc(mask_a_free, 1)
            dve.sem_inc(bias_free, 1)
            dve.sem_inc(o_free, 1)
            dve.wait_ge(sink_loaded, 16)
            dve.wait_ge(zeros_set, 1)
            with dve.Fori(0, T) as i:
                link = linker(dve, dve_own, i * DVE_OWN)

                def mask(s):
                    dve.wait_ge(s_done, i * NH + s + 1)
                    if s >= 2:
                        dve.wait_ge(pt_done, i * NH + s - 1)
                    flat = ps[:, 2 * (s % 2):2 * (s % 2) + 2, :].rearrange("p b n -> p (b n)")
                    dve.memset(gate[:, :], 0.0)
                    if s < NHA:
                        link(dve.tensor_tensor_reduce(S[:, s % 2, 0:keys(s)], flat[:, 128:768], mask_a[:, :], 1.0, sink[:, s:s + 1], ALU.add, ALU.max, mx[:, s, 0:1]))
                        dve.tensor_scalar(negm[:, s:s + 1], mx[:, s, 0:1], -1.0, None, ALU.mult).then_inc(s_masked, 1)
                    else:
                        dve.tensor_tensor_reduce(S[:, s % 2, 0:LB], flat[:, 0:LB], bias[:, s - NHA, :], 1.0, NEG, ALU.add, ALU.max, mx[:, s, 0:1])
                        link(dve.tensor_tensor_reduce(S[:, s % 2, LB:LB + CTX], flat[:, LB:LB + CTX], zeros[:, :], 1.0, NEG, ALU.add, ALU.max, mx[:, s, 1:2]))
                        dve.tensor_scalar(negm[:, s:s + 1], mx[:, s, 0:1], mx[:, s, 1:2], -1.0, ALU.max, ALU.mult).then_inc(s_masked, 1)

                def evacuate(s):
                    dve.wait_ge(pt_done, i * NH + s + 1)
                    if s >= 2:
                        dve.wait_ge(pv_done, i * NH + s - 1)
                    dve.tensor_copy(PT[:, s % 2, 512:keys(s)], ps[:, 5, 0:keys(s) - 512]).then_inc(pt_high, 1)

                def output(g):
                    heads = slice(g * NHA, (g + 1) * NHA)
                    if g == 0:
                        dve.wait_ge(sinke_done, i + 1)
                        link(dve.tensor_tensor(den[:, heads], den[:, heads], sinke[:, :], ALU.add))
                        dve.wait_ge(o_free, i + 1)
                    link(dve.reciprocal(rden[:, heads], den[:, heads]))
                    dve.wait_ge(pv_done, i * NH + (g + 1) * NHA)
                    r = rden[:, heads].rearrange("p (h a) -> p h a", a=1).to_broadcast([P, NHA, HD])
                    dve.tensor_tensor(o[:, g, :].rearrange("p (h d) -> p h d", h=NHA), ps[:, 6 + g, :].rearrange("p (h d) -> p h d", h=NHA), r, ALU.mult).then_inc(o_scaled, 1)

                def norm(g):
                    dve.wait_ge(rms_done, 2 * i + g + 1)
                    link(dve.reciprocal(stat[:, g, 2:3], stat[:, g, 1:2]))
                    dve.tensor_scalar(o[:, g, :], o[:, g, :], stat[:, g, 2:3], None, ALU.mult).then_inc(o_done, 1)

                dve.wait_ge(mask_a_loaded, 16 * i + 16)
                for s in range(NH):
                    if s == NHA:
                        dve.sem_inc(mask_a_free, 1)
                        dve.wait_ge(p_done, i * NH + NHA)
                        dve.tensor_tensor(sinkd[:, :], sink[:, :], negm[:, 0:NHA], ALU.add).then_inc(sinkd_done, 1)
                        dve.wait_ge(bias_ready, i + 1)
                    mask(s)
                    if s >= 1:
                        evacuate(s - 1)
                    if s == NHA + 2:
                        output(0)
                dve.sem_inc(bias_free, 1)
                evacuate(NH - 1)
                dve.wait_ge(p_done, i * NH + NH)
                output(1)
                norm(0)
                norm(1)
                assert link.count[0] == DVE_OWN, link.count


def middle(K):
    nc, io, ps, ring = K.nc, K.io, K.psum, K.ring
    ctx = ExitStack()
    with ctx:
        sb, sem = scope(nc, ctx)
        mix, xin = sb("mix", [P, 2, D]), sb("xres", [P, 2, D])
        mixT, h2T = sb("mixT", [P, KD, P]), sb("h2T", [P, KD, P])
        mixT2, h2T2 = sb("mixT2", [P, KD, P]), sb("h2T2", [P, KD, P])
        x1, h2 = sb("x1", [P, 2, D]), sb("h2", [P, 2, D])
        squares = sb("squares3", [P, D])
        gate1, scale2, shift2, gain = sb("gate1", [P, D]), sb("scale2", [P, D]), sb("shift2", [P, D]), sb("gain", [P, 2, D])
        w_router, b_router = sb("w_router", [P, KD, E]), sb("b_router", [P, E])
        stat = sb("stat3", [P, T, 6])
        tri, iota, ones = sb("tri", [P, P]), sb("iota", [P, P]), sb("ones", [P, P])
        record = sb("record", [P, TOPK, T, 2], I32)
        logit = sb("logit", [P, T, E])
        top, topi, topf = sb("top", [P, T, 8]), sb("topi", [P, T, 8], U32), sb("topf", [P, T, 8])
        pick = sb("pick", [P, TOPK, T, E])
        chosen, before = sb("chosen", [P, T, E]), sb("before", [P, T + 1, E])
        base, prod = sb("base", [P, T, E]), sb("prod", [P, T, E])
        nblk = sb("nblk", [P, 2, E])
        scan = sb("scan", [P, 2, E])
        start, count = sb("start", [P, E]), sb("count", [P, E])
        slotf = sb("slotf", [P, TOPK, T])
        expd, exps, norm = sb("expd", [P, T, TOPK]), sb("exps", [P, T, TOPK]), sb("norm", [P, T, 2])
        NTAB = MAXB + 2
        cmp, tabf = sb("cmp", [1, NTAB, E]), sb("tabf", [1, 2, NTAB])

        rows_loaded, tabs_loaded, ones_set = sem("rows_loaded"), sem("tabs_loaded"), sem("ones_set")
        mix_loaded = [sem("mix_loaded0"), sem("mix_loaded1")]
        xr_loaded = [sem("xr_loaded0"), sem("xr_loaded1")]
        stored = [sem("stored0"), sem("stored1")]
        mt_done, mt_copied, proj_done, x1_done, h2_done, h2_shifted = (sem(n) for n in ("mt_done", "mt_copied", "proj_done", "x1_done", "h2_done", "h2_shifted"))
        h2t_done, h2t_copied, logit_done, rms1_done, rms2_done = (sem(n) for n in ("h2t_done", "h2t_copied", "logit_done", "rms1_done", "rms2b_done"))
        chosen_done, pos_done, expd_done, exps_done, route_done, scattered = (sem(n) for n in ("chosen_done", "pos_done", "expd_done", "exps_done", "route_done", "scattered"))
        dve_own, act_own = sem("dve_own3"), sem("act_own3")
        mts, h2ts = [mixT, mixT2], [h2T, h2T2]

        block = ctx.enter_context(nc.Block())

        @block.sync
        def _(sp):
            def load(t):
                if t >= 2:
                    sp.wait_ge(mt_done, t - 1)
                    sp.wait_ge(x1_done, t - 1)
                sp.dma_start(mix[:, t % 2, :], K.mix_d[t * P:(t + 1) * P, :]).then_inc(mix_loaded[t % 2], 16)
                sp.dma_start(xin[:, t % 2, :], io["x"][0][t * P:(t + 1) * P, :]).then_inc(xr_loaded[t % 2], 16)

            load(0)
            load(1)
            for t in range(T):
                sp.wait_ge(h2_shifted, t + 1)
                sp.dma_start(K.x1_d[t * P:(t + 1) * P, :], x1[:, t % 2, :]).then_inc(stored[t % 2], 16)
                sp.dma_start(K.h2_d[t * P:(t + 1) * P, :], h2[:, t % 2, :]).then_inc(stored[t % 2], 16)
                if t + 2 < T:
                    load(t + 2)
            for s in range(2):
                sp.wait_ge(stored[s], 32 * (T // 2))

        @block.gpsimd
        def _(pool):
            pool.memset(ones[:, :], 1.0).then_inc(ones_set, 1)
            for dst, src in ((gate1, K.mod_d[0:1, 2 * D:3 * D]), (shift2, K.mod_d[0:1, 3 * D:4 * D]), (scale2, K.mod_d[0:1, 4 * D:5 * D])):
                pool.dma_start(dst[:, :], src.to_broadcast([P, D])).then_inc(rows_loaded, 16)
            pool.dma_start(gain[:, 0, :], io["g_post_mix"].to_broadcast([P, D])).then_inc(rows_loaded, 16)
            pool.dma_start(gain[:, 1, :], io["g_pre_ffn"].to_broadcast([P, D])).then_inc(rows_loaded, 16)
            pool.dma_start(w_router[:, :, :], io["w_router"][0].rearrange("(k p) n -> p k n", p=P)).then_inc(tabs_loaded, 16)
            pool.dma_start(b_router[:, :], io["b_router"].to_broadcast([P, E])).then_inc(tabs_loaded, 16)
            pool.dma_start(tri[:, :], io["k_tri"]).then_inc(tabs_loaded, 16)
            pool.dma_start(iota[:, :], io["k_iota"]).then_inc(tabs_loaded, 16)
            pool.dma_start(record[:, :, :, :].rearrange("p k t a -> p (k t a)"), io["k_record"]).then_inc(tabs_loaded, 16)
            pool.wait_ge(rows_loaded, 80)
            for t in range(T):
                pool.wait_ge(h2_done, t + 1)
                pool.tensor_tensor(h2[:, t % 2, :], h2[:, t % 2, :], shift2[:, :], ALU.add).then_inc(h2_shifted, 1)
            pool.wait_ge(tabs_loaded, 80)
            pool.wait_ge(route_done, 1)
            for k in range(TOPK):
                for t in range(T):
                    pool.indirect_dma_start(K.slot_d, bass.IndirectOffsetOnAxis(ap=K.slots[:, k, t:t + 1], axis=0), record[:, k, t, :], None).then_inc(scattered, 16)
            pool.wait_ge(scattered, 16 * TOPK * T)

        @block.tensor
        def _(pe):
            def to_columns(t):
                pe.wait_ge(mix_loaded[t % 2], 16 * (t // 2 + 1))
                if t:
                    pe.wait_ge(mt_copied, t)
                for k in range(KD):
                    last = pe.transpose(ps[:, k // 4, (k % 4) * P:(k % 4 + 1) * P], mix[:, t % 2, k * P:(k + 1) * P], K.ident[:, :])
                last.then_inc(mt_done, 1)

            def project(t):
                pe.wait_ge(mt_copied, t + 1)
                if t:
                    pe.wait_ge(x1_done, t)
                for n in range(2):
                    for k in range(KD):
                        last = pe.matmul(ps[:, 2 + n, :], mts[t % 2][:, k, :], ring[:, n, k, :], start=(k == 0), stop=(k == KD - 1))
                last.then_inc(proj_done, 1)

            def route(t):
                pe.wait_ge(h2_shifted, t + 1)
                if t:
                    pe.wait_ge(h2t_copied, t)
                for k in range(KD):
                    last = pe.transpose(ps[:, 4 + k // 4, (k % 4) * P:(k % 4 + 1) * P], h2[:, t % 2, k * P:(k + 1) * P], K.ident[:, :])
                last.then_inc(h2t_done, 1)
                pe.wait_ge(h2t_copied, t + 1)
                for k in range(KD):
                    last = pe.matmul(ps[:, 6, t * E:(t + 1) * E], h2ts[t % 2][:, k, :], w_router[:, k, :], start=(k == 0), stop=(k == KD - 1))
                last.then_inc(logit_done, 1)

            pe.wait_ge(tabs_loaded, 80)
            to_columns(0)
            for t in range(T):
                if t + 1 < T:
                    to_columns(t + 1)
                project(t)
                if t:
                    route(t - 1)
            route(T - 1)
            pe.wait_ge(ones_set, 1)
            pe.wait_ge(chosen_done, 1)
            flat = lambda x: x.rearrange("p t e -> p (t e)")
            pe.matmul(ps[:, 7, 0:T * E], tri[:, :], flat(chosen[:, :, :]), start=True, stop=False)
            pe.matmul(ps[:, 7, 0:T * E], ones[:, :], flat(before[:, 0:T, :]), start=False, stop=True)
            pe.matmul(ps[:, 7, T * E:(T + 1) * E], ones[:, :], before[:, T, :], start=True, stop=True).then_inc(pos_done, 1)

        @block.scalar
        def _(act):
            link = linker(act, act_own)

            def copy_h2(t):
                act.wait_ge(h2t_done, t + 1)
                if t >= 2:
                    act.wait_ge(logit_done, t - 1)
                act.activation(h2ts[t % 2][:, :, :].rearrange("p k n -> p (k n)"), ps[:, 4:6, :].rearrange("p b n -> p (b n)"), ACT.Copy).then_inc(h2t_copied, 1)

            for t in range(T):
                act.wait_ge(proj_done, t + 1)
                link(act.activation(squares[:, :], ps[:, 2:4, :].rearrange("p b n -> p (b n)"), ACT.Square, accum_out=stat[:, t, 0:1]))
                act.activation(stat[:, t, 1:2], stat[:, t, 0:1], ACT.Sqrt, bias=K.eps[:, :], scale=1.0 / D).then_inc(rms1_done, 1)
                act.wait_ge(x1_done, t + 1)
                link(act.activation(squares[:, :], x1[:, t % 2, :], ACT.Square, accum_out=stat[:, t, 3:4]))
                act.activation(stat[:, t, 4:5], stat[:, t, 3:4], ACT.Sqrt, bias=K.eps[:, :], scale=1.0 / D).then_inc(rms2_done, 1)
                if t:
                    copy_h2(t - 1)
            copy_h2(T - 1)
            act.wait_ge(expd_done, 1)
            act.activation(exps[:, :, :], expd[:, :, :], ACT.Exp).then_inc(exps_done, 1)

        @block.vector
        def _(dve):
            link = linker(dve, dve_own)
            dve.wait_ge(rows_loaded, 80)
            link(dve.tensor_tensor(gate1[:, :], gate1[:, :], gain[:, 0, :], ALU.mult))
            link(dve.scalar_tensor_tensor(scale2[:, :], scale2[:, :], 1.0, gain[:, 1, :], ALU.add, ALU.mult))

            def copy_mix(t):
                dve.wait_ge(mt_done, t + 1)
                if t >= 2:
                    dve.wait_ge(proj_done, t - 1)
                for k in range(KD):
                    last = dve.tensor_scalar(mts[t % 2][:, k, :], ps[:, k // 4, (k % 4) * P:(k % 4 + 1) * P], K.colv[:, 40 + k:41 + k], None, ALU.mult)
                last.then_inc(mt_copied, 1)

            copy_mix(0)
            for t in range(T):
                if t + 1 < T:
                    copy_mix(t + 1)
                s = t % 2
                dve.wait_ge(rms1_done, t + 1)
                link(dve.reciprocal(stat[:, t, 2:3], stat[:, t, 1:2]))
                if t >= 2:
                    dve.wait_ge(stored[s], 32 * (t // 2))
                    dve.wait_ge(h2t_done, t - 1)
                link(dve.scalar_tensor_tensor(x1[:, s, :], ps[:, 2:4, :].rearrange("p b n -> p (b n)"), stat[:, t, 2:3], gate1[:, :], ALU.mult, ALU.mult))
                dve.wait_ge(xr_loaded[s], 16 * (t // 2 + 1))
                dve.tensor_tensor(x1[:, s, :], x1[:, s, :], xin[:, s, :], ALU.add).then_inc(x1_done, 1)
                dve.wait_ge(rms2_done, t + 1)
                link(dve.reciprocal(stat[:, t, 5:6], stat[:, t, 4:5]))
                dve.scalar_tensor_tensor(h2[:, s, :], x1[:, s, :], stat[:, t, 5:6], scale2[:, :], ALU.mult, ALU.mult).then_inc(h2_done, 1)
            dve.wait_ge(logit_done, T)
            dve.wait_ge(tabs_loaded, 80)
            row = lambda x: x.rearrange("p (a n) -> p a n", a=1)
            link(dve.tensor_tensor(logit[:, :, :], ps[:, 6, 0:T * E].rearrange("p (t e) -> p t e", e=E), row(b_router[:, :]).to_broadcast([P, T, E]), ALU.add))
            for t in range(T):
                last = dve.max(top[:, t, :], logit[:, t, :])
            link(last)
            dve.tensor_tensor(expd[:, :, :], top[:, :, 0:TOPK], top[:, :, 0:1].to_broadcast([P, T, TOPK]), ALU.subtract).then_inc(expd_done, 1)
            for t in range(T):
                last = dve.max_index(topi[:, t, :], top[:, t, :], logit[:, t, :])
            link(last)
            link(dve.tensor_copy(topf[:, :, :], topi[:, :, :]))
            for k in range(TOPK):
                last = dve.tensor_tensor(pick[:, k, :, :], row(iota[:, 0:E]).to_broadcast([P, T, E]), topf[:, :, k:k + 1].to_broadcast([P, T, E]), ALU.is_equal)
            link(last)
            link(dve.tensor_tensor(base[:, :, :], pick[:, 0, :, :], pick[:, 1, :, :], ALU.add))
            link(dve.tensor_tensor(prod[:, :, :], pick[:, 2, :, :], pick[:, 3, :, :], ALU.add))
            link(dve.tensor_tensor(chosen[:, :, :], base[:, :, :], prod[:, :, :], ALU.add))
            link(dve.memset(before[:, 0, :], 0.0))
            for t in range(T):
                ins = dve.tensor_tensor(before[:, t + 1, :], before[:, t, :], chosen[:, t, :], ALU.add)
                if t + 1 < T:
                    link(ins)
            ins.then_inc(chosen_done, 1)
            dve.wait_ge(exps_done, 1)
            link(dve.tensor_reduce(norm[:, :, 0:1], exps[:, :, :], AX.X, ALU.add))
            link(dve.reciprocal(norm[:, :, 1:2], norm[:, :, 0:1]))
            link(dve.tensor_tensor(K.weights[:, :, :], exps[:, :, :], norm[:, :, 1:2].to_broadcast([P, T, TOPK]), ALU.mult))
            dve.wait_ge(pos_done, 1)
            link(dve.tensor_copy(count[:, :], ps[:, 7, T * E:(T + 1) * E]))
            link(dve.tensor_scalar(nblk[:, 0, :], count[:, :], 0.0, None, ALU.is_gt))
            for m in range(1, SEQ // P):
                link(dve.scalar_tensor_tensor(nblk[:, m % 2, :], count[:, :], float(P * m), nblk[:, (m - 1) % 2, :], ALU.is_gt, ALU.add))
            blocks = nblk[:, (SEQ // P - 1) % 2, :]
            link(dve.tensor_copy(scan[:, 0, :], blocks))
            cur = 0
            for shift in (1, 2, 4, 8, 16):
                link(dve.tensor_copy(scan[:, 1 - cur, 0:shift], scan[:, cur, 0:shift]))
                link(dve.tensor_tensor(scan[:, 1 - cur, shift:], scan[:, cur, shift:], scan[:, cur, 0:E - shift], ALU.add))
                cur = 1 - cur
            ends = scan[:, cur, :]
            link(dve.tensor_tensor(start[:, :], ends, blocks, ALU.subtract))
            link(dve.scalar_tensor_tensor(base[:, :, :], row(start[:, :]).to_broadcast([P, T, E]), float(P), ps[:, 7, 0:T * E].rearrange("p (t e) -> p t e", e=E), ALU.mult, ALU.add))
            for k in range(TOPK):
                link(dve.tensor_tensor(prod[:, :, :], pick[:, k, :, :], base[:, :, :], ALU.mult))
                link(dve.tensor_reduce(slotf[:, k, :], prod[:, :, :], AX.X, ALU.add))
            link(dve.tensor_copy(K.slots[:, :, :], slotf[:, :, :]))
            link(dve.tensor_tensor(cmp[:, :, :], row(scan[0:1, cur, :]).to_broadcast([1, NTAB, E]), iota[0:1, 0:NTAB].rearrange("p (n a) -> p n a", a=1).to_broadcast([1, NTAB, E]), ALU.is_le))
            link(dve.tensor_reduce(tabf[:, 0, :], cmp[:, :, :], AX.X, ALU.add))
            link(dve.tensor_scalar(tabf[:, 1, :], tabf[:, 0, :], float(E - 1), None, ALU.min))
            link(dve.tensor_copy(K.table[:, 0:NTAB], tabf[:, 1, :]))
            dve.tensor_copy(K.table[:, 79:80], scan[0:1, cur, E - 1:E]).then_inc(route_done, 1)


def experts(K):
    nc, io, ps = K.nc, K.io, K.psum
    w1 = io["w_mlp1"][0].rearrange("e (k p) n -> e p k n", p=P)
    w2 = io["w_mlp2"][0].rearrange("e (k p) n -> e p k n", p=P)
    UP, DOWN = 2 * FF // UNIT, D // UNIT
    NU, RING, CH = UP + DOWN, 3, 2
    PAIRS = UNIT // 2
    KC = KD // CH
    ctx = ExitStack()
    with ctx:
        sb, sem = scope(nc, ctx)
        ring = sb("wring", [P, RING, KD, UNIT])
        w_hi, w_lo = sb("w_hi", [P, 2, KD, UNIT], F32R), sb("w_lo", [P, 2, KD, UNIT], F32R)
        xg = sb("xg", [P, D])
        x_hi, x_lo = sb("x_hi", [P, KD, P], F32R), sb("x_lo", [P, KD, P], F32R)
        a_hi, a_lo = sb("a_hi", [P, KD, P], F32R), sb("a_lo", [P, KD, P], F32R)
        glu, lin, sig, act_o = (sb(n, [P, 2, PAIRS]) for n in ("glu", "lin", "sig", "act_o"))
        y = sb("y", [P, D])
        idx, y_row, int_zero = sb("idx", [P, 2], I32), sb("y_row", [P, 1], I32), sb("int_zero", [P, 1], I32)
        poolgate = sb("poolgate", [P, 2])
        NB = 2 * FF + D
        braw, brest, bpart = sb("braw", [96, NB]), sb("brest", [96, NB]), sb("bpart", [96, NB], BF16)
        btab = sb("btab", [96, NB], BF16)
        onehot = sb("onehot", [96, E])
        sel_up, sel_down = sb("sel_up", [96, P], BF16), sb("sel_down", [96, P], BF16)

        b_loaded = sem("b_loaded4")
        w_loaded = [sem(f"w_loaded{r}") for r in range(RING)]
        hi_done, lo_done, pe_unit = sem("hi_done"), sem("lo_done"), sem("pe_unit")
        idx_loaded, gathered, gate_open = sem("idx_loaded"), sem("gathered"), sem("gate_open")
        xt_done, xhi_done, x_ready = sem("xt_done4"), sem("xhi_done"), sem("x_ready")
        sel_up_ready, sel_down_ready = sem("sel_up_ready"), sem("sel_down_ready")
        glu_done, sig_done, up_free, act_done = sem("glu_done"), sem("sig_done4"), sem("up_free"), sem("act_done")
        at_done, ahi_done, a_ready = sem("at_done"), sem("ahi_done"), sem("a_ready")
        y_copied, y_stored, y_free = sem("y_copied"), sem("y_stored"), sem("y_free")
        dve_own = sem("dve_own4")
        DVE_OWN = UP

        block = ctx.enter_context(nc.Block())
        limits = dict(min_val=1, max_val=MAXB)

        def wait_loaded(engine, b, n):
            engine.wait_ge(w_loaded[n % RING], 16 * ((NU // RING) * b + n // RING + 1))

        @block.sync
        def _(sp):
            def load(b, n, e):
                sp.wait_ge(lo_done, CH * (NU * b + n) + CH)
                src = w1[bass.ds(e, 1), :, :, n * UNIT:(n + 1) * UNIT] if n < UP else w2[bass.ds(e, 1), :, :, (n - UP) * UNIT:(n - UP + 1) * UNIT]
                sp.dma_start(ring[:, n % RING, :, :], src.rearrange("a p k n -> (a p) k n")).then_inc(w_loaded[n % RING], 16)

            blocks = sp.value_load(K.table[0:1, 79:80], **limits)
            first = sp.value_load(K.table[0:1, 0:1], min_val=0, max_val=E - 1)
            load(0, 0, first)
            with sp.Fori(0, blocks) as b:
                e = sp.value_load(K.table[0:1, bass.ds(b, 1)], min_val=0, max_val=E - 1)
                e_next = sp.value_load(K.table[0:1, bass.ds(b + 1, 1)], min_val=0, max_val=E - 1)
                for n in range(1, NU):
                    load(b, n, e)
                load(b + 1, 0, e_next)

        @block.gpsimd
        def _(pool):
            pool.sem_inc(y_free, 1)
            pool.memset(int_zero[:, :], 0).then_inc(gate_open, 1)
            pool.wait_ge(gate_open, 1)
            pool.memset(poolgate[:, :], 0.0).then_inc(gate_open, 1)
            for part in range(3):
                rows = slice(E * part, E * part + E)
                pool.dma_start(braw[rows, 0:2 * FF], io["b_mlp1"][0]).then_inc(b_loaded, 16)
                pool.dma_start(braw[rows, 2 * FF:], io["b_mlp2"][0]).then_inc(b_loaded, 16)
            pool.dma_start(onehot[:, :], io["k_onehot"]).then_inc(b_loaded, 16)
            pool.wait_ge(gate_open, 2)
            blocks = pool.value_load(K.table[0:1, 79:80], **limits)

            def gate():
                pool.tensor_tensor(poolgate[:, 1:2], poolgate[:, 0:1], poolgate[:, 0:1], ALU.add).then_inc(gate_open, 1)

            pool.dma_start(idx[:, :], K.slot_d[0:P, :]).then_inc(idx_loaded, 16)
            pool.wait_ge(idx_loaded, 16)
            pool.indirect_dma_start(xg[:, :], None, K.h2_d, bass.IndirectOffsetOnAxis(ap=idx[:, 0:1], axis=0)).then_inc(gathered, 16)
            pool.wait_ge(gathered, 16)
            with pool.Fori(0, blocks) as b:
                pool.wait_ge(gate_open, 3 * b + 2)
                pool.tensor_tensor(y_row[:, :], idx[:, 1:2], int_zero[:, :], ALU.add).then_inc(gate_open, 1)
                pool.wait_ge(gate_open, 3 * b + 3)
                pool.dma_start(idx[:, :], K.slot_d[bass.ds(b * P + P, P), :]).then_inc(idx_loaded, 16)
                pool.wait_ge(idx_loaded, 16 * b + 32)
                pool.wait_ge(xt_done, b + 1)
                gate()
                pool.indirect_dma_start(xg[:, :], None, K.h2_d, bass.IndirectOffsetOnAxis(ap=idx[:, 0:1], axis=0)).then_inc(gathered, 16)
                pool.wait_ge(gathered, 16 * b + 32)
                pool.wait_ge(gate_open, 3 * b + 4)
                pool.wait_ge(y_copied, DOWN * b + 2 * DOWN)
                gate()
                pool.indirect_dma_start(K.y_d, bass.IndirectOffsetOnAxis(ap=y_row[:, 0:1], axis=0), y[:, :], None).then_inc(y_stored, 16)
                pool.wait_ge(y_stored, 16 * b + 16)
                pool.sem_inc(y_free, 1)
            pool.wait_ge(y_stored, 16)

        @block.scalar
        def _(act):
            act.sem_inc(y_copied, 2)

            def split(b, n):
                wait_loaded(act, b, n)
                act.wait_ge(pe_unit, NU * b + n + 1)
                for c in range(CH):
                    k = slice(KC * c, KC * (c + 1))
                    act.activation(w_hi[:, n % 2, k, :], ring[:, n % RING, k, :], ACT.Copy).then_inc(hi_done, 1)

            def rows(b):
                act.wait_ge(xt_done, b + 1)
                act.activation(x_hi[:, :, :].rearrange("p k n -> p (k n)"), ps[:, 6:8, :].rearrange("p b n -> p (b n)"), ACT.Copy).then_inc(xhi_done, 1)

            def columns(b, n):
                act.wait_ge(at_done, UP * b + n + 1)
                act.activation(a_hi[:, 2 * n:2 * n + 2, :].rearrange("p k n -> p (k n)"), ps[:, 2 + n % 2, 0:2 * P], ACT.Copy).then_inc(ahi_done, 1)

            blocks = act.value_load(K.table[0:1, 79:80], **limits)
            split(0, 0)
            rows(0)
            with act.Fori(0, blocks) as b:
                for n in range(NU):
                    split(b + (n + 1) // NU, (n + 1) % NU)
                    if n < UP:
                        act.wait_ge(glu_done, UP * b + n + 1)
                        act.activation(sig[:, n % 2, :], glu[:, n % 2, :], ACT.Sigmoid, scale=ALPHA).then_inc(sig_done, 1)
                        if n:
                            columns(b, n - 1)
                    elif n == UP:
                        rows(b + 1)
                        columns(b, UP - 1)
                act.wait_ge(y_free, b + 1)
                for h in range(DOWN):
                    act.wait_ge(pe_unit, NU * b + UP + h + 3)
                    act.activation(y[:, h * UNIT:(h + 1) * UNIT], ps[:, 4 + h, :], ACT.Copy).then_inc(y_copied, 1)

        @block.vector
        def _(dve):
            dve.sem_inc(lo_done, RING * CH)
            dve.sem_inc(up_free, 2)
            dve.sem_inc(a_ready, 2)
            prep = linker(dve, dve_own)
            dve.wait_ge(b_loaded, 16 * 7)
            src = braw
            for part in range(3):
                rows = slice(E * part, E * part + E)
                prep(dve.tensor_copy(bpart[:, :], src[:, :]))
                prep(dve.tensor_copy(btab[rows, :], bpart[rows, :]))
                if part < 2:
                    prep(dve.tensor_tensor(brest[:, :], src[:, :], bpart[:, :], ALU.subtract))
                    src = brest
            BASE = prep.count[0]

            def split(b, n):
                for c in range(CH):
                    k = slice(KC * c, KC * (c + 1))
                    dve.wait_ge(hi_done, CH * (NU * b + n) + c + 1)
                    dve.tensor_tensor(w_lo[:, n % 2, k, :], ring[:, n % RING, k, :], w_hi[:, n % 2, k, :].bitcast(F32), ALU.subtract).then_inc(lo_done, 1)

            def rows(b):
                dve.wait_ge(xhi_done, b + 1)
                dve.tensor_tensor(x_lo[:, :, :].rearrange("p k n -> p (k n)"), ps[:, 6:8, :].rearrange("p b n -> p (b n)"),
                                  x_hi[:, :, :].bitcast(F32).rearrange("p k n -> p (k n)"), ALU.subtract).then_inc(x_ready, 1)

            def columns(b, n):
                dve.wait_ge(ahi_done, UP * b + n + 1)
                dve.tensor_tensor(a_lo[:, 2 * n:2 * n + 2, :].rearrange("p k n -> p (k n)"), ps[:, 2 + n % 2, 0:2 * P],
                                  a_hi[:, 2 * n:2 * n + 2, :].bitcast(F32).rearrange("p k n -> p (k n)"), ALU.subtract).then_inc(a_ready, 1)

            def select(sel, e, ready):
                col = onehot[:, bass.ds(e, 1)] if not isinstance(e, int) else onehot[:, e:e + 1]
                dve.tensor_copy(sel[:, :], col.to_broadcast([96, P])).then_inc(ready, 1)

            blocks = dve.value_load(K.table[0:1, 79:80], **limits)
            first = dve.value_load(K.table[0:1, 0:1], min_val=0, max_val=E - 1)
            select(sel_up, first, sel_up_ready)
            split(0, 0)
            rows(0)
            with dve.Fori(0, blocks) as b:
                link = linker(dve, dve_own, b * DVE_OWN + BASE)
                e = dve.value_load(K.table[0:1, bass.ds(b, 1)], min_val=0, max_val=E - 1)
                e_next = dve.value_load(K.table[0:1, bass.ds(b + 1, 1)], min_val=0, max_val=E - 1)
                for n in range(NU):
                    split(b + (n + 1) // NU, (n + 1) % NU)
                    if n == 0:
                        dve.wait_ge(pe_unit, NU * b + 2)
                        select(sel_down, e, sel_down_ready)
                    if n < UP:
                        pairs = ps[:, n % 2, :].rearrange("p (j two) -> p j two", two=2)
                        s = n % 2
                        dve.wait_ge(pe_unit, NU * b + n + 3)
                        if n >= 2:
                            dve.wait_ge(at_done, UP * b + n - 1)
                        dve.tensor_scalar(glu[:, s, :], pairs[:, :, 0], LIMIT, None, ALU.min).then_inc(glu_done, 1)
                        dve.tensor_scalar(lin[:, s, :], pairs[:, :, 1], LIMIT, -LIMIT, ALU.min, ALU.max).then_inc(up_free, 1)
                        dve.wait_ge(up_free, UP * b + n + 3)
                        link(dve.scalar_tensor_tensor(lin[:, s, :], lin[:, s, :], 1.0, glu[:, s, :], ALU.add, ALU.mult))
                        dve.wait_ge(sig_done, UP * b + n + 1)
                        dve.tensor_tensor(act_o[:, s, :], lin[:, s, :], sig[:, s, :], ALU.mult).then_inc(act_done, 1)
                        if n:
                            columns(b, n - 1)
                        if n == UP - 1:
                            select(sel_up, e_next, sel_up_ready)
                    elif n == UP:
                        rows(b + 1)
                        columns(b, UP - 1)
                assert link.count[0] == UP

        @block.tensor
        def _(pe):
            pe.sem_inc(pe_unit, 2)

            def rows(b):
                pe.wait_ge(gathered, 16 * b + 16)
                for k in range(KD):
                    last = pe.transpose(ps[:, 6 + k // 4, (k % 4) * P:(k % 4 + 1) * P], xg[:, k * P:(k + 1) * P], K.ident[:, :])
                last.then_inc(xt_done, 1)

            def columns(b, n):
                pe.wait_ge(act_done, UP * b + n + 1)
                pe.wait_ge(a_ready, UP * b + n + 1)
                for c in range(2):
                    last = pe.transpose(ps[:, 2 + n % 2, c * P:(c + 1) * P], act_o[:, n % 2, c * P:(c + 1) * P], K.ident[:, :])
                last.then_inc(at_done, 1)

            def product(b, n, bank, hi, lo, ready):
                for c in range(CH):
                    pe.wait_ge(lo_done, CH * (NU * b + n) + c + 1 + RING * CH)
                    for k in range(KC * c, KC * (c + 1)):
                        if ready:
                            ready(k)
                        pe.matmul(bank, hi[:, k, :], w_hi[:, n % 2, k, :], start=False, stop=False)
                        pe.matmul(bank, hi[:, k, :], w_lo[:, n % 2, k, :], start=False, stop=False)
                        last = pe.matmul(bank, lo[:, k, :], w_hi[:, n % 2, k, :], start=False, stop=(k == KD - 1))
                last.then_inc(pe_unit, 1)

            blocks = pe.value_load(K.table[0:1, 79:80], **limits)
            rows(0)
            with pe.Fori(0, blocks) as b:
                pe.wait_ge(sel_up_ready, b + 1)
                pe.wait_ge(x_ready, b + 1)
                for n in range(UP):
                    pe.wait_ge(up_free, UP * b + n + 1)
                    pe.matmul(ps[:, n % 2, :], sel_up[:, :], btab[:, n * UNIT:(n + 1) * UNIT], start=True, stop=False)
                    product(b, n, ps[:, n % 2, :], x_hi, x_lo, None)
                    if n:
                        columns(b, n - 1)
                rows(b + 1)
                columns(b, UP - 1)
                pe.wait_ge(sel_down_ready, b + 1)
                for h in range(DOWN):
                    pe.wait_ge(y_copied, DOWN * b + h + 1)
                    bank = ps[:, 4 + h, :]
                    pe.matmul(bank, sel_down[:, :], btab[:, 2 * FF + h * UNIT:2 * FF + (h + 1) * UNIT], start=True, stop=False)

                    def ready(k):
                        if k % 2 == 0:
                            pe.wait_ge(a_ready, UP * b + k // 2 + 3)
                    product(b, UP + h, bank, a_hi, a_lo, ready if h == 0 else None)


def combine(K):
    nc, io = K.nc, K.io
    ctx = ExitStack()
    with ctx:
        sb, sem = scope(nc, ctx)
        yg = sb("yg", [P, 2, TOPK, D])
        x1 = sb("x1r", [P, 2, D])
        acc, out = sb("acc", [P, 2, D]), sb("outt", [P, 2, D])
        squares = sb("squares5", [P, D])
        gate2, gain = sb("gate2", [P, D]), sb("gain5", [P, D])
        stat = sb("stat5", [P, T, 3])
        rows_loaded, ss_done = sem("rows_loaded5"), sem("ss_done5")
        gathered = [sem("gathered5_0"), sem("gathered5_1")]
        x_loaded = [sem("x_loaded5_0"), sem("x_loaded5_1")]
        stored = [sem("stored5_0"), sem("stored5_1")]
        acc_done, rms_done, out_done, dve_own, act_own = sem("acc_done"), sem("rms_done5"), sem("out_done"), sem("dve_own5"), sem("act_own5")
        y_rows = K.y_d[0:TOPK * SEQ, :].rearrange("(k t p) d -> t p k d", t=T, p=P)
        block = ctx.enter_context(nc.Block())

        @block.sync
        def _(sp):
            def store(t):
                sp.wait_ge(out_done, t + 1)
                sp.dma_start(io["out"][0][t * P:(t + 1) * P, :], out[:, t % 2, :]).then_inc(stored[t % 2], 16)

            for t in range(T):
                if t >= 2:
                    sp.wait_ge(out_done, t - 1)
                sp.dma_start(yg[:, t % 2, :, :], y_rows[t]).then_inc(gathered[t % 2], 16)
                sp.dma_start(x1[:, t % 2, :], K.x1_d[t * P:(t + 1) * P, :]).then_inc(x_loaded[t % 2], 16)
                if t >= 1:
                    store(t - 1)
            store(T - 1)
            for s in range(2):
                sp.wait_ge(stored[s], 16 * (T // 2))

        @block.gpsimd
        def _(pool):
            pool.dma_start(gate2[:, :], K.mod_d[0:1, 5 * D:6 * D].to_broadcast([P, D])).then_inc(rows_loaded, 16)
            pool.dma_start(gain[:, :], io["g_post_ffn"].to_broadcast([P, D])).then_inc(rows_loaded, 16)
            pool.wait_ge(rows_loaded, 32)

        @block.scalar
        def _(act):
            link = linker(act, act_own)
            for t in range(T):
                act.wait_ge(acc_done, t + 1)
                link(act.activation(squares[:, :], acc[:, t % 2, :], ACT.Square, accum_out=stat[:, t, 0:1]))
                act.activation(stat[:, t, 1:2], stat[:, t, 0:1], ACT.Sqrt, bias=K.eps[:, :], scale=1.0 / D).then_inc(rms_done, 1)

        @block.vector
        def _(dve):
            link = linker(dve, dve_own)

            def add(t):
                s = t % 2
                dve.wait_ge(gathered[s], 16 * (t // 2 + 1))
                link(dve.tensor_scalar(acc[:, s, :], yg[:, s, 0, :], K.weights[:, t, 0:1], None, ALU.mult))
                for k in range(1, TOPK):
                    ins = dve.scalar_tensor_tensor(acc[:, s, :], yg[:, s, k, :], K.weights[:, t, k:k + 1], acc[:, s, :], ALU.mult, ALU.add)
                    if k + 1 < TOPK:
                        link(ins)
                ins.then_inc(acc_done, 1)

            def finish(t):
                s = t % 2
                dve.wait_ge(rms_done, t + 1)
                link(dve.reciprocal(stat[:, t, 2:3], stat[:, t, 1:2]))
                if t >= 2:
                    dve.wait_ge(stored[s], 16 * (t // 2))
                link(dve.scalar_tensor_tensor(out[:, s, :], acc[:, s, :], stat[:, t, 2:3], gate2[:, :], ALU.mult, ALU.mult))
                dve.wait_ge(x_loaded[s], 16 * (t // 2 + 1))
                dve.tensor_tensor(out[:, s, :], out[:, s, :], x1[:, s, :], ALU.add).then_inc(out_done, 1)

            add(0)
            dve.wait_ge(rows_loaded, 32)
            link(dve.tensor_tensor(gate2[:, :], gate2[:, :], gain[:, :], ALU.mult))
            for t in range(T):
                if t + 1 < T:
                    add(t + 1)
                finish(t)


_INS = ["x", "c", "ctx", "c_ctx", "w_ada", "b_ada", "g_pre_mix", "g_post_mix", "g_pre_ffn", "g_post_ffn",
        "w_in", "g_grp_a", "g_grp_b", "sink_a", "rpb_b", "w_out", "w_router", "b_router",
        "w_mlp1", "b_mlp1", "w_mlp2", "b_mlp2"]


def kernel(**inputs):
    import concourse.bacc as bacc
    from concourse.bass_utils import run_bass_kernel_spmd

    nc = bacc.Bacc("TRN2", target_bir_lowering=False, num_devices=1)
    arrays, io = {}, {}
    given = {name: inputs[name] for name in _INS}
    given.update(constants())
    for name, a in given.items():
        a = np.ascontiguousarray(a)
        arrays["in_" + name] = a
        io[name] = nc.dram_tensor("in_" + name, a.shape, mybir.dt.from_np(a.dtype), kind="ExternalInput").ap()
    io["out"] = nc.dram_tensor("out_0", (1, SEQ, D), F32, kind="ExternalOutput").ap()
    Kernel(nc, io).build()
    r = run_bass_kernel_spmd(nc, [arrays], core_ids=[0])
    return r.results[0]["out_0"]
```

```python
import concourse.bass as bass
from concourse import mybir
from contextlib import ExitStack
import numpy as np

F32 = mybir.dt.float32
F32R = mybir.dt.float32r
BF16 = mybir.dt.bfloat16
I32 = mybir.dt.int32
U32 = mybir.dt.uint32
ALU = mybir.AluOpType
ACT = mybir.ActivationFunctionType
AX = mybir.AxisListType

P = 128
D = 1024
KD = D // P
SEQ, CTX = 1024, 256
T = SEQ // P
TC = CTX // P
HD = 64
NHA, NKVA, NHB = 8, 2, 8
NH = NHA + NHB
GRID_W, GRID_H = 64, SEQ // 64
NA_ROWS, NA_COLS = 8, 16
WINDOW = 128
IN_W = 2304
E, TOPK, FF = 32, 4, 1024
EPS = 1e-6
LIMIT, ALPHA = 7.0, 1.702
NEG = -1e30
UNIT = 512
LA = P + 2 * WINDOW
LBR = 10
LB = LBR * GRID_W
RPB_R, RPB_C = 2 * NA_ROWS - 1, 2 * NA_COLS - 1
BROWS = NHB * RPB_R + 4
BW = GRID_W + RPB_C - 1
STEPS = E + 1
PAIR_SLOTS, SINGLE_SLOTS = 2 * P * STEPS, P * STEPS
SLOTS = PAIR_SLOTS + SINGLE_SLOTS
PAIR_AT, SINGLE_AT = 0, STEPS
PAIR_COUNT, SINGLE_COUNT = 2 * STEPS, 2 * STEPS + 1
assert SEQ * TOPK // (P + 1) < E


def constants():
    f = np.float32
    out = {}
    out["k_ident"] = np.eye(P, dtype=f)
    d = np.arange(P)
    partner = np.where((d % 32) < 16, d + 16, d - 16)
    perm = np.zeros((P, P), f)
    perm[partner, d] = 1
    out["k_perm"] = perm
    pos = np.arange(SEQ)
    rows, cols = (pos // GRID_W).astype(f), (pos % GRID_W).astype(f)
    nf = HD // 4
    freqs = (f(10000.0) ** (-np.arange(nf, dtype=f) / f(nf))).astype(f)
    fr = freqs[d % 16]
    isrow = (d % HD) < 32
    ang = np.where(isrow[:, None], fr[:, None] * rows[None], fr[:, None] * cols[None]).astype(f)
    sign = np.where((d % 32) < 16, -1.0, 1.0).astype(f)
    out["k_cos"] = np.cos(ang).astype(f)
    out["k_sin"] = (np.sin(ang) * sign[:, None]).astype(f)
    mask_a = np.zeros((T, P, LA + CTX), f)
    mask_b = np.zeros((T, P, LB), f)
    tab = np.zeros((T, 4), np.int32)
    for i in range(T):
        k0 = min(max(i - 1, 0), T - 3) * P
        q = i * P + np.arange(P)
        k = k0 + np.arange(LA)
        mask_a[i, :, :LA] = np.where(np.abs(k[None] - q[:, None]) <= WINDOW, 0, NEG)
        base = min(max(2 * i - NA_ROWS // 2, 0), GRID_H - LBR)
        r, qc = q // GRID_W, q % GRID_W
        rs = np.clip(r - NA_ROWS // 2, 0, GRID_H - NA_ROWS)
        cs = np.clip(qc - NA_COLS // 2, 0, GRID_W - NA_COLS)
        kr, kc = base + np.arange(LBR), np.arange(GRID_W)
        ok = ((kr[None] >= rs[:, None]) & (kr[None] < rs[:, None] + NA_ROWS))[:, :, None] & \
             ((kc[None] >= cs[:, None]) & (kc[None] < cs[:, None] + NA_COLS))[:, None, :]
        mask_b[i] = np.where(ok, 0, NEG).reshape(P, LB)
        tab[i] = (k0, base * GRID_W, base - 2 * i + 7 + 2, base - 2 * i - 1 + 7 + 2)
    out["k_mask_a"], out["k_mask_b"] = mask_a, mask_b
    out["k_tiles"] = tab.reshape(1, 4 * T)
    out["k_tri"] = np.triu(np.ones((P, P), f), 1)
    out["k_iota"] = np.broadcast_to(np.arange(P, dtype=f), (P, P)).copy()
    out["k_zeros"] = np.zeros((1, BROWS * BW), f)
    out["k_onehot"] = (np.arange(96)[:, None] % E == np.arange(E)[None]).astype(f)
    token = np.arange(P)[:, None, None] + P * np.arange(T)[None, None]
    record = np.stack(np.broadcast_arrays(token, token + SEQ * np.arange(TOPK)[None, :, None]), axis=-1)
    out["k_record"] = record.reshape(P, TOPK * T * 2).astype(np.int32)
    spare = TOPK * SEQ + np.arange(SLOTS) % P
    out["k_empty"] = np.stack([0 * spare, spare], axis=-1).astype(np.int32)
    return out


def raw_ap(ap, offset, dims):
    return bass.AP(tensor=ap.tensor, offset=offset, ap=dims)


class Kernel:

    def __init__(self, nc, io, dbg=None):
        self.nc, self.io, self.dbg = nc, io, dbg or {}

    def build(self, upto=9):
        nc, io = self.nc, self.io
        with ExitStack() as ctx:
            self.semaphores = ctx.enter_context(ExitStack())
            self.psum = ctx.enter_context(nc.psum_tensor("psum", [P, 8, 512], F32))
            self.ident = ctx.enter_context(nc.sbuf_tensor("ident", [P, P], F32))
            self.eps = ctx.enter_context(nc.sbuf_tensor("eps", [P, 1], F32))
            self.colv = ctx.enter_context(nc.sbuf_tensor("colv", [P, 48], F32))
            self.weights = ctx.enter_context(nc.sbuf_tensor("route_w", [P, T, TOPK], F32))
            self.slots = ctx.enter_context(nc.sbuf_tensor("route_slot", [P, TOPK, T], I32))
            self.table = ctx.enter_context(nc.sbuf_tensor("block_table", [1, 2 * STEPS + 2], I32))
            dram = lambda n, s, d=F32: nc.dram_tensor(n, s, d, kind="Internal").ap()
            self.mod_d = dram("mod_d", (2, 6 * D))
            self.skew_d = dram("skew_d", (GRID_W, BROWS, BW))
            self.bias_d = dram("bias_d", (GRID_W, BROWS, GRID_W))
            self.mix_d = dram("mix_d", (SEQ, D))
            self.x1_d = dram("x1_d", (SEQ, D))
            self.h2_d = dram("h2_d", (SEQ, D))
            self.btab_d = dram("btab_d", (96, 2 * FF + D), BF16)
            self.slot_d = dram("slot_d", (SLOTS, 2), I32)
            self.y_d = dram("y_d", (TOPK * SEQ + P, D))
            with ExitStack() as early:
              self.ring = early.enter_context(nc.sbuf_tensor("ring", [P, 2, KD, UNIT], F32))
              with ExitStack() as qkv:
                  self.qa = qkv.enter_context(nc.sbuf_tensor("qaT", [P, 4, SEQ], F32))
                  self.ka = qkv.enter_context(nc.sbuf_tensor("kaT", [P, SEQ + CTX], F32))
                  self.qb = qkv.enter_context(nc.sbuf_tensor("qbT", [P, 4, SEQ], F32))
                  self.kb = qkv.enter_context(nc.sbuf_tensor("kbT", [P, 4, SEQ + CTX], F32))
                  self.v = qkv.enter_context(nc.sbuf_tensor("v", [P, T + TC, NKVA * HD + NHB * HD], F32))
                  front(self)
                  if upto >= 2:
                      attention(self)
              if upto >= 3:
                  middle(self)
            if upto >= 4:
                experts(self, 2, PAIR_AT, PAIR_COUNT, 0)
                experts(self, 1, SINGLE_AT, SINGLE_COUNT, PAIR_SLOTS)
            if upto >= 5:
                combine(self)


def scope(K, ctx):
    nc = K.nc
    sb = lambda name, shape, dt=F32: ctx.enter_context(nc.sbuf_tensor(name, shape, dt))
    sem = lambda name: K.semaphores.enter_context(nc.semaphore(name))
    return sb, sem


def linker(engine, sem, base=0):
    n = [0]

    def link(ins):
        n[0] += 1
        ins.then_inc(sem, 1)
        engine.wait_ge(sem, base + n[0])
    link.count = n
    return link


def front(K):
    nc, io, ps, ring = K.nc, K.io, K.psum, K.ring
    w_ada = io["w_ada"][0].rearrange("(k p) n -> p k n", p=P)
    w_in = io["w_in"][0].rearrange("(k p) n -> p k n", p=P)
    ctx = ExitStack()
    with ctx:
        sb, sem = scope(K, ctx)
        hT = sb("hT", [P, KD, SEQ + CTX])
        xin = sb("xin", [P, 2, D])
        modrow = sb("modrow", [2, 6 * D])
        cosT, sinT = sb("cosT", [P, SEQ]), sb("sinT", [P, SEQ])
        perm = sb("perm", [P, P])
        raw = sb("raw", [P, 2, UNIT])
        squares = raw[:, :, :].rearrange("p a n -> p (a n)")
        rot = sb("rot", [P, 2, UNIT])
        crow = sb("crow", [16, P])
        csig = sb("csig", [16, P])
        csilu = sb("csilu", [16, P])
        cT = sb("cT", [P, 16])
        modc = sb("modc", [48, P])
        aff = sb("aff", [P, 2, 2, KD])
        stat = sb("stat", [P, 2, 3])

        const_loaded, ident_loaded, c_loaded, b_loaded = sem("const_loaded"), sem("ident_loaded"), sem("c_loaded"), sem("b_loaded")
        mod_stored_late = sem("mod_stored_late")
        unit_loaded = [sem("unit_loaded0"), sem("unit_loaded1")]
        unit_used = sem("unit_used")
        x_loaded = [sem("x_loaded0"), sem("x_loaded1")]
        x_scaled, xt_done, ht_done = sem("x_scaled"), sem("xt_done"), sem("ht_done")
        ss_done, rms_done, rstd_done = sem("ss_done"), sem("rms_done"), sem("rstd_done")
        sig_done, silu_done, ct_done, ct_copied = sem("sig_done"), sem("silu_done"), sem("ct_done"), sem("ct_copied")
        ada_done, mod_done, mod_stored = sem("ada_done"), sem("mod_done"), sem("mod_stored")
        modc_loaded, modc_t, aff_done = sem("modc_loaded"), sem("modc_t"), sem("aff_done")
        group_done, group_copied = sem("group_done"), sem("group_copied")
        perm_done, rope_done = sem("perm_done"), sem("rope_done")
        eps_set, empty_stored, skew_zeroed, skew_stored = sem("eps_set"), sem("empty_stored"), sem("skew_zeroed"), sem("skew_stored")
        bias_stored, dve_own = sem("bias_stored"), sem("dve_own")

        units = [("ada", u) for u in range(4)] + [("in", u) for u in range(5)] + [("ada", u) for u in range(4, 12)]
        groups = []
        for u, tiles in enumerate([[("qa", j) for j in range(4)],
                                   [("ka", 0), ("va", 0), ("qb", 0), ("qb", 1)],
                                   [("qb", 2), ("qb", 3), ("kb", 0), ("kb", 1)],
                                   [("kb", 2), ("kb", 3), ("vb", 0)],
                                   [("vb", 1)]]):
            col = 0
            for kind, j in tiles:
                width = 2 * P if kind == "vb" else P
                if kind in ("va", "vb"):
                    groups += [(u, kind, j, col, tt, width) for tt in range(T + TC)]
                else:
                    groups += [(u, kind, j, col, hf, UNIT) for hf in range(2)]
                    if kind in ("ka", "kb"):
                        groups.append((u, kind, j, col, 2, CTX))
                col += width
        ropes = [g for g, x in enumerate(groups) if x[1] in ("qa", "ka") and x[4] < 2]

        block = ctx.enter_context(nc.Block())

        @block.sync
        def _(sp):
            sp.dma_start(crow[0:8, :], io["c"][0].rearrange("(k p) -> k p", p=P)).then_inc(c_loaded, 16)
            sp.dma_start(crow[8:16, :], io["c_ctx"].rearrange("(k p) -> k p", p=P)).then_inc(c_loaded, 16)
            sp.dma_start(K.ident[:, :], io["k_ident"]).then_inc(ident_loaded, 16)

            def load_x(t):
                if t >= 2:
                    sp.wait_ge(xt_done, t - 1)
                src = io["x"][0][t * P:(t + 1) * P, :] if t < T else io["ctx"][0][(t - T) * P:(t - T + 1) * P, :]
                sp.dma_start(xin[:, t % 2, :], src).then_inc(x_loaded[t % 2], 16)

            load_x(0)
            load_x(1)
            for n, (kind, u) in enumerate(units):
                if n >= 2:
                    sp.wait_ge(unit_used, n - 1)
                src = w_ada if kind == "ada" else w_in
                cols = min(UNIT, src.shape[2] - u * UNIT)
                sp.dma_start(ring[:, n % 2, :, 0:cols], src[:, :, u * UNIT:u * UNIT + cols]).then_inc(unit_loaded[n % 2], 16)
                if n == 5:
                    for t in range(2, T + TC):
                        load_x(t)
            sp.wait_ge(mod_done, 12)
            sp.dma_start(K.mod_d[:, 2 * D:], modrow[:, 2 * D:]).then_inc(mod_stored_late, 16)
            sp.wait_ge(mod_stored_late, 16)
            sp.wait_ge(bias_stored, 16)

        @block.gpsimd
        def _(pool):
            pool.memset(K.eps[:, :], EPS).then_inc(eps_set, 1)
            for dst, src in ((perm[:, :], io["k_perm"]), (cosT[:, :], io["k_cos"]), (sinT[:, :], io["k_sin"])):
                pool.dma_start(dst, src).then_inc(const_loaded, 16)
            for r in range(2):
                pool.dma_start(modrow[r:r + 1, :], io["b_ada"]).then_inc(b_loaded, 16)
            for r, name in ((32, "g_pre_mix"), (40, "g_grp_a"), (44, "g_grp_b")):
                n = io[name].shape[1] // P
                pool.dma_start(modc[r:r + n, :], io[name][0].rearrange("(k p) -> k p", p=P)).then_inc(modc_loaded, 16)
            pool.dma_start(K.slot_d, io["k_empty"]).then_inc(empty_stored, 16)
            pool.dma_start(K.skew_d.rearrange("q n k -> q (n k)"), io["k_zeros"].to_broadcast([GRID_W, BROWS * BW])).then_inc(skew_zeroed, 16)
            pool.wait_ge(skew_zeroed, 16)
            rpb = raw_ap(io["rpb_b"], 0, [[0, GRID_W], [RPB_C, NHB * RPB_R], [1, RPB_C]])
            pool.dma_start(raw_ap(K.skew_d, 2 * BW, [[BROWS * BW + 1, GRID_W], [BW, NHB * RPB_R], [1, RPB_C]]), rpb).then_inc(skew_stored, 16)
            pool.wait_ge(skew_stored, 16)
            pool.dma_start(K.bias_d, K.skew_d[:, :, NA_COLS - 1:NA_COLS - 1 + GRID_W]).then_inc(bias_stored, 16)
            pool.wait_ge(empty_stored, 16)
            pool.wait_ge(mod_done, 4)
            pool.dma_start(K.mod_d[:, 0:2 * D], modrow[:, 0:2 * D]).then_inc(mod_stored, 16)
            pool.wait_ge(mod_stored, 16)
            for r in range(2):
                pool.dma_start(modc[16 * r:16 * r + 16, :], K.mod_d[r, 0:2 * D].rearrange("(n p) -> n p", p=P)).then_inc(modc_loaded, 16)
            pool.wait_ge(modc_loaded, 80)

        @block.scalar
        def _(act):
            act.wait_ge(c_loaded, 32)
            act.activation(csig[:, :], crow[:, :], ACT.Sigmoid).then_inc(sig_done, 1)
            act.wait_ge(eps_set, 1)
            for t in range(T + TC):
                act.wait_ge(x_loaded[t % 2], 16 * (t // 2 + 1))
                if t:
                    act.wait_ge(ss_done, t)
                if t >= 2:
                    act.wait_ge(x_scaled, t - 1)
                act.activation(squares, xin[:, t % 2, :], ACT.Square, accum_out=stat[:, t % 2, 0:1]).then_inc(ss_done, 1)
                act.wait_ge(ss_done, t + 1)
                act.activation(stat[:, t % 2, 1:2], stat[:, t % 2, 0:1], ACT.Sqrt, bias=K.eps[:, :], scale=1.0 / D).then_inc(rms_done, 1)
            rope = 0
            for g, (u, kind, j, col, part, width) in enumerate(groups):
                bank = g % 4
                act.wait_ge(group_done, g + 1)
                if kind in ("qa", "ka") and part < 2:
                    if rope >= 2:
                        act.wait_ge(rope_done, rope - 1)
                    act.activation(raw[:, rope % 2, :], ps[:, bank, :], ACT.Copy, scale=HD ** -0.5 if kind == "qa" else 1.0).then_inc(group_copied, 1)
                    rope += 1
                    continue
                if kind == "ka":
                    dst = K.ka[:, SEQ:]
                elif kind == "qb":
                    dst = K.qb[:, j, part * UNIT:part * UNIT + width]
                elif kind == "kb":
                    dst = K.kb[:, j, part * UNIT:part * UNIT + width]
                elif kind == "va":
                    dst = K.v[:, part, 0:P]
                else:
                    dst = K.v[:, part, P + j * width:P + (j + 1) * width]
                act.activation(dst, ps[:, bank, 0:width], ACT.Copy, scale=HD ** -0.5 if kind == "qb" else 1.0).then_inc(group_copied, 1)

        @block.vector
        def _(dve):
            link = linker(dve, dve_own)
            dve.wait_ge(sig_done, 1)
            dve.tensor_tensor(csilu[:, :], crow[:, :], csig[:, :], ALU.mult).then_inc(silu_done, 1)
            dve.wait_ge(ct_done, 1)
            dve.tensor_copy(cT[:, :], ps[:, 2, 0:16]).then_inc(ct_copied, 1)
            dve.wait_ge(b_loaded, 32)

            def ada(u):
                dve.wait_ge(ada_done, u + 1)
                row = modrow[0:2, u * UNIT:(u + 1) * UNIT]
                dve.tensor_tensor(row, ps[0:2, u % 2, :], row, ALU.add).then_inc(mod_done, 1)

            def scale(t):
                dve.wait_ge(rms_done, t + 1)
                link(dve.reciprocal(stat[:, t % 2, 2:3], stat[:, t % 2, 1:2]))
                dve.tensor_scalar(xin[:, t % 2, :], xin[:, t % 2, :], stat[:, t % 2, 2:3], None, ALU.mult).then_inc(x_scaled, 1)

            for u in range(4):
                ada(u)
            scale(0)
            scale(1)
            dve.wait_ge(modc_t, 1)
            link(dve.tensor_copy(K.colv[:, :], ps[:, 2, 0:48]))
            for r in range(2):
                dve.scalar_tensor_tensor(aff[:, r, 0, :], K.colv[:, 16 * r + 8:16 * r + 16], 1.0, K.colv[:, 32:40], ALU.add, ALU.mult).then_inc(aff_done, 1)
                dve.tensor_copy(aff[:, r, 1, :], K.colv[:, 16 * r:16 * r + 8]).then_inc(aff_done, 1)
            dve.wait_ge(aff_done, 4)
            for t in range(T + TC):
                r = 0 if t < T else 1
                dve.wait_ge(xt_done, t + 1)
                for k in range(KD):
                    last = dve.tensor_scalar(hT[:, k, t * P:(t + 1) * P], ps[:, 4 + 2 * (t % 2) + k // 4, (k % 4) * P:(k % 4 + 1) * P],
                                             aff[:, r, 0, k:k + 1], aff[:, r, 1, k:k + 1], ALU.mult, ALU.add)
                last.then_inc(ht_done, 1)
                if t + 2 < T + TC:
                    scale(t + 2)
            dve.wait_ge(const_loaded, 48)
            for n, g in enumerate(ropes):
                _, kind, j, _, hf, _ = groups[g]
                cols = slice(hf * UNIT, (hf + 1) * UNIT)
                dve.wait_ge(group_copied, g + 1)
                link(dve.tensor_tensor(rot[:, 0, :], raw[:, n % 2, :], cosT[:, cols], ALU.mult))
                dve.wait_ge(perm_done, n + 1)
                link(dve.tensor_tensor(rot[:, 1, :], ps[:, 4 + n % 2, :], sinT[:, cols], ALU.mult))
                if kind == "qa":
                    for half in range(2):
                        head, src = 2 * j + half, slice(HD * half, HD * half + HD)
                        g0 = HD * (head // (NHA // NKVA))
                        last = dve.tensor_tensor(K.qa[g0:g0 + HD, head % 4, cols], rot[src, 0, :], rot[src, 1, :], ALU.add)
                else:
                    last = dve.tensor_tensor(K.ka[:, cols], rot[:, 0, :], rot[:, 1, :], ALU.add)
                last.then_inc(rope_done, 1)
                dve.wait_ge(rope_done, n + 1)
            for u in range(4, 12):
                ada(u)

        @block.tensor
        def _(pe):
            pe.wait_ge(silu_done, 1)
            pe.wait_ge(const_loaded, 48)
            pe.wait_ge(ident_loaded, 16)
            pe.transpose(ps[:, 2, 0:16], csilu[:, :], K.ident[0:16, 0:16]).then_inc(ct_done, 1)
            pe.wait_ge(ct_copied, 1)
            cols = cT[:, :].rearrange("p (v k) -> p k v", v=2)

            def ada(n, u):
                pe.wait_ge(unit_loaded[n % 2], 16 * (n // 2 + 1))
                if u >= 2:
                    pe.wait_ge(mod_done, u - 1)
                for k in range(KD):
                    last = pe.matmul(ps[0:2, u % 2, :], cols[:, k, :], ring[:, n % 2, k, :], start=(k == 0), stop=(k == KD - 1))
                last.then_inc(ada_done, 1)
                pe.wait_ge(ada_done, u + 1)
                pe.sem_inc(unit_used, 1)

            for n in range(4):
                ada(n, units[n][1])
            pe.wait_ge(modc_loaded, 80)
            pe.transpose(ps[:, 2, 0:48], modc[:, :], K.ident[0:48, 0:48]).then_inc(modc_t, 1)
            for t in range(T + TC):
                pe.wait_ge(x_scaled, t + 1)
                if t >= 2:
                    pe.wait_ge(ht_done, t - 1)
                for k in range(KD):
                    last = pe.transpose(ps[:, 4 + 2 * (t % 2) + k // 4, (k % 4) * P:(k % 4 + 1) * P], xin[:, t % 2, k * P:(k + 1) * P], K.ident[:, :])
                last.then_inc(xt_done, 1)
            pe.wait_ge(ht_done, T + TC)
            pe.wait_ge(mod_done, 4)
            pe.wait_ge(aff_done, 4)
            rope = 0

            def rotate(n, g):
                pe.wait_ge(group_copied, g + 1)
                if n >= 2:
                    pe.wait_ge(rope_done, n - 1)
                pe.matmul(ps[:, 4 + n % 2, :], perm[:, :], raw[:, n % 2, :], start=True, stop=True).then_inc(perm_done, 1)

            pending = None
            for g, (u, kind, j, col, part, width) in enumerate(groups):
                n = 4 + u
                slot = n % 2
                if g == 0 or groups[g - 1][0] != u:
                    pe.wait_ge(unit_loaded[slot], 16 * (n // 2 + 1))
                if g >= 4:
                    pe.wait_ge(group_copied, g - 3)
                for k in range(KD):
                    if kind in ("va", "vb"):
                        lhs, rhs = hT[:, k, part * P:(part + 1) * P], ring[:, slot, k, col:col + width]
                    else:
                        lhs, rhs = ring[:, slot, k, col:col + P], hT[:, k, part * UNIT:part * UNIT + width]
                    last = pe.matmul(ps[:, g % 4, 0:width], lhs, rhs, start=(k == 0), stop=(k == KD - 1))
                last.then_inc(group_done, 1)
                if g + 1 == len(groups) or groups[g + 1][0] != u:
                    pe.wait_ge(group_done, g + 1)
                    pe.sem_inc(unit_used, 1)
                if pending is not None:
                    rotate(*pending)
                    pending = None
                if g in ropes:
                    pending = (ropes.index(g), g)
            pe.wait_ge(group_copied, len(groups))
            for n in range(9, 17):
                ada(n, units[n][1])


def attention(K):
    nc, io, ps, ring = K.nc, K.io, K.psum, K.ring
    w_out = io["w_out"][0].rearrange("(k p) n -> p k n", p=P)
    ctx = ExitStack()
    with ctx:
        sb, sem = scope(K, ctx)
        qz = sb("qz", [P, NH, P])
        bias = sb("bias", [P, NHB, LB])
        mask_a, mask_b = sb("mask_a", [P, LA + CTX]), sb("mask_b", [P, LB])
        zeros = sb("zeros", [P, CTX])
        S = sb("S", [P, 2, LB + CTX])
        PT = sb("PT", [P, 2, 7 * P])
        o = sb("o", [P, 2, NHA * HD])
        squares = sb("squares", [P, NHA * HD])
        sink = sb("sink", [P, NHA])
        negm, den, sinkd, sinke, rden = sb("negm", [P, NH]), sb("den", [P, NH]), sb("sinkd", [P, NHA]), sb("sinke", [P, NHA]), sb("rden", [P, NH])
        mx = sb("mx", [P, NH, 2])
        stat = sb("stat2", [P, 2, 3])
        gate = sb("gate", [P, 1])
        tiles = sb("tiles", [1, 4 * T], I32)

        tiles_loaded, sink_loaded, zeros_set, qz_set = sem("tiles_loaded"), sem("sink_loaded"), sem("zeros_set"), sem("qz_set")
        mask_a_loaded, bias_loaded, wout_loaded = sem("mask_a_loaded"), sem("bias_loaded"), sem("wout_loaded")
        mask_a_free, bias_free, q_free, o_free = sem("mask_a_free"), sem("bias_free"), sem("q_free"), sem("o_free")
        q_ready, bias_ready = sem("q_ready"), sem("bias_ready")
        s_done, s_masked, p_done, pt_done, pt_low, pt_high, pv_done = (sem(n) for n in ("s_done", "s_masked", "p_done", "pt_done", "pt_low", "pt_high", "pv_done"))
        sinkd_done, sinke_done, o_scaled, rms_done, o_done, o_stored = (sem(n) for n in ("sinkd_done", "sinke_done", "o_scaled", "rms2_done", "o_done", "o_stored"))
        dve_own, act_own = sem("dve_own2"), sem("act_own2")
        DVE_OWN, ACT_OWN = NH + 5, 2

        block = ctx.enter_context(nc.Block())

        @block.sync
        def _(sp):
            sp.dma_start(tiles[:, :], io["k_tiles"]).then_inc(tiles_loaded, 16)
            for n in range(2):
                sp.dma_start(ring[:, n, :, :], w_out[:, :, n * UNIT:(n + 1) * UNIT]).then_inc(wout_loaded, 16)
            sp.wait_ge(tiles_loaded, 16)
            with sp.Fori(0, T) as i:
                sp.wait_ge(mask_a_free, i + 1)
                sp.dma_start(mask_a[:, :], io["k_mask_a"][bass.ds(i, 1), :, :].rearrange("a p n -> (a p) n")).then_inc(mask_a_loaded, 16)
                first = [sp.value_load(tiles[0:1, bass.ds(i * 4 + 2 + half, 1)], min_val=0, max_val=BROWS - LBR - 15 * (NHB - 1)) for half in range(2)]
                sp.wait_ge(bias_free, i + 1)
                for half in range(2):
                    src = K.bias_d.rearrange("q n k -> q (n k)")
                    src = bass.AP(tensor=src.tensor, offset=first[half] * GRID_W, ap=[[BROWS * GRID_W, GRID_W], [RPB_R * GRID_W, NHB], [1, LB]])
                    sp.dma_start(bias[GRID_W * half:GRID_W * (half + 1), :, :], src).then_inc(bias_loaded, 16)
                sp.dma_start(mask_b[:, :], io["k_mask_b"][bass.ds(i, 1), :, :].rearrange("a p n -> (a p) n")).then_inc(bias_loaded, 16)
                sp.wait_ge(o_done, 2 * i + 2)
                sp.dma_start(K.mix_d[bass.ds(i * P, P), :], o[:, :, :].rearrange("p a n -> p (a n)")).then_inc(o_stored, 16)
                sp.wait_ge(o_stored, 16 * i + 16)
                sp.sem_inc(o_free, 1)
            sp.wait_ge(o_stored, 16 * T)
            sp.wait_ge(wout_loaded, 32)

        @block.gpsimd
        def _(pool):
            pool.memset(zeros[:, :], 0.0).then_inc(zeros_set, 1)
            pool.memset(qz[:, :, :], 0.0).then_inc(qz_set, 1)
            pool.dma_start(sink[:, :], io["sink_a"].to_broadcast([P, NHA])).then_inc(sink_loaded, 16)
            pool.wait_ge(qz_set, 1)
            with pool.Fori(0, T) as i:
                pool.wait_ge(q_free, i + 1)
                for half in range(2):
                    part = slice(HD * half, HD * half + HD)
                    pool.tensor_copy(qz[part, 4 * half:4 * half + 4, :], K.qa[part, :, bass.ds(i * P, P)])
                    last = pool.tensor_copy(qz[part, NHA + half:NH:2, :], K.qb[part, :, bass.ds(i * P, P)])
                last.then_inc(q_ready, 1)
                pool.wait_ge(q_ready, i + 1)
                pool.wait_ge(bias_loaded, 48 * i + 48)
                pool.tensor_tensor(bias[:, :, :], bias[:, :, :], mask_b[:, :].rearrange("p (a n) -> p a n", a=1).to_broadcast([P, NHB, LB]), ALU.add).then_inc(bias_ready, 1)
            pool.wait_ge(sink_loaded, 16)

        def keys(s):
            return LA + CTX if s < NHA else LB + CTX

        @block.tensor
        def _(pe):
            pe.sem_inc(q_free, 1)
            pe.wait_ge(tiles_loaded, 16)
            with pe.Fori(0, T) as i:
                k_a = pe.value_load(tiles[0:1, bass.ds(i * 4, 1)], min_val=0, max_val=SEQ - LA)
                k_b = pe.value_load(tiles[0:1, bass.ds(i * 4 + 1, 1)], min_val=0, max_val=SEQ - LB)
                pe.wait_ge(q_ready, i + 1)

                def scores(s):
                    if s >= 2:
                        pe.wait_ge(s_masked, i * NH + s - 1)
                    bank = 2 * (s % 2)
                    q = qz[:, s, :]
                    flat = ps[:, bank:bank + 2, :].rearrange("p b n -> p (b n)")
                    if s < NHA:
                        pe.matmul(flat[:, 128:512], q, K.ka[:, bass.ds(k_a, LA)], start=True, stop=True)
                        pe.matmul(flat[:, 512:768], q, K.ka[:, SEQ:], start=True, stop=True).then_inc(s_done, 1)
                    else:
                        kt = K.kb[:, (s - NHA) // 2, :]
                        pe.matmul(flat[:, 0:512], q, kt[:, bass.ds(k_b, 512)], start=True, stop=True)
                        pe.matmul(flat[:, 512:640], q, kt[:, bass.ds(k_b + 512, 128)], start=True, stop=True)
                        pe.matmul(flat[:, 640:896], q, kt[:, SEQ:], start=True, stop=True).then_inc(s_done, 1)

                def transposes(s):
                    if s >= 1:
                        pe.wait_ge(pt_low, i * NH + s)
                        pe.wait_ge(pt_high, i * NH + s)
                    pe.wait_ge(p_done, i * NH + s + 1)
                    for c in range(keys(s) // P):
                        last = pe.transpose(ps[:, 4 + c // 4, (c % 4) * P:(c % 4 + 1) * P], S[:, s % 2, c * P:(c + 1) * P], K.ident[:, :])
                    last.then_inc(pt_done, 1)

                def values(s):
                    pe.wait_ge(pt_low, i * NH + s + 1)
                    pe.wait_ge(pt_high, i * NH + s + 1)
                    chunks = keys(s) // P
                    head = s % NHA
                    col = HD * (head // (NHA // NKVA)) if s < NHA else P + HD * head
                    local = chunks - TC
                    start = k_a if s < NHA else k_b
                    for c in range(chunks):
                        row = (start >> 7) + c if c < local else None
                        v = K.v[:, bass.ds(row, 1), col:col + HD].rearrange("p a n -> p (a n)") if c < local else K.v[:, T + c - local, col:col + HD]
                        last = pe.matmul(ps[:, 6 + s // NHA, head * HD:(head + 1) * HD], PT[:, s % 2, c * P:(c + 1) * P], v, start=(c == 0), stop=(c == chunks - 1))
                    last.then_inc(pv_done, 1)

                scores(0)
                for s in range(NH):
                    if s + 1 < NH:
                        scores(s + 1)
                    if s + 1 == NH - 1:
                        pass
                    transposes(s)
                    if s >= 1:
                        values(s - 1)
                values(NH - 1)
                pe.wait_ge(pv_done, i * NH + NH)
                pe.sem_inc(q_free, 1)
                pe.wait_ge(o_scaled, 2 * i + 2)

        @block.scalar
        def _(act):
            with act.Fori(0, T) as i:
                link = linker(act, act_own, i * ACT_OWN)

                def probs(s):
                    act.wait_ge(s_masked, i * NH + s + 1)
                    act.activation(S[:, s % 2, 0:keys(s)], S[:, s % 2, 0:keys(s)], ACT.Exp, bias=negm[:, s:s + 1], accum_out=den[:, s:s + 1]).then_inc(p_done, 1)

                def evacuate(s):
                    act.wait_ge(pt_done, i * NH + s + 1)
                    if s >= 2:
                        act.wait_ge(pv_done, i * NH + s - 1)
                    act.activation(PT[:, s % 2, 0:512], ps[:, 4, :], ACT.Copy).then_inc(pt_low, 1)

                def rms(g):
                    act.wait_ge(o_scaled, 2 * i + g + 1)
                    link(act.activation(squares[:, :], o[:, g, :], ACT.Square, accum_out=stat[:, g, 0:1]))
                    act.activation(stat[:, g, 1:2], stat[:, g, 0:1], ACT.Sqrt, bias=K.eps[:, :], scale=1.0 / (NHA * HD)).then_inc(rms_done, 1)

                for s in range(NH):
                    probs(s)
                    if s >= 1:
                        evacuate(s - 1)
                    if s == NHA:
                        act.wait_ge(sinkd_done, i + 1)
                        act.activation(sinke[:, :], sinkd[:, :], ACT.Exp).then_inc(sinke_done, 1)
                evacuate(NH - 1)
                rms(0)
                rms(1)

        @block.vector
        def _(dve):
            dve.sem_inc(mask_a_free, 1)
            dve.sem_inc(bias_free, 1)
            dve.sem_inc(o_free, 1)
            dve.wait_ge(sink_loaded, 16)
            dve.wait_ge(zeros_set, 1)
            with dve.Fori(0, T) as i:
                link = linker(dve, dve_own, i * DVE_OWN)

                def mask(s):
                    dve.wait_ge(s_done, i * NH + s + 1)
                    if s >= 2:
                        dve.wait_ge(pt_done, i * NH + s - 1)
                    flat = ps[:, 2 * (s % 2):2 * (s % 2) + 2, :].rearrange("p b n -> p (b n)")
                    dve.memset(gate[:, :], 0.0)
                    if s < NHA:
                        link(dve.tensor_tensor_reduce(S[:, s % 2, 0:keys(s)], flat[:, 128:768], mask_a[:, :], 1.0, sink[:, s:s + 1], ALU.add, ALU.max, mx[:, s, 0:1]))
                        dve.tensor_scalar(negm[:, s:s + 1], mx[:, s, 0:1], -1.0, None, ALU.mult).then_inc(s_masked, 1)
                    else:
                        dve.tensor_tensor_reduce(S[:, s % 2, 0:LB], flat[:, 0:LB], bias[:, s - NHA, :], 1.0, NEG, ALU.add, ALU.max, mx[:, s, 0:1])
                        link(dve.tensor_tensor_reduce(S[:, s % 2, LB:LB + CTX], flat[:, LB:LB + CTX], zeros[:, :], 1.0, NEG, ALU.add, ALU.max, mx[:, s, 1:2]))
                        dve.tensor_scalar(negm[:, s:s + 1], mx[:, s, 0:1], mx[:, s, 1:2], -1.0, ALU.max, ALU.mult).then_inc(s_masked, 1)

                def evacuate(s):
                    dve.wait_ge(pt_done, i * NH + s + 1)
                    if s >= 2:
                        dve.wait_ge(pv_done, i * NH + s - 1)
                    dve.tensor_copy(PT[:, s % 2, 512:keys(s)], ps[:, 5, 0:keys(s) - 512]).then_inc(pt_high, 1)

                def output(g):
                    heads = slice(g * NHA, (g + 1) * NHA)
                    if g == 0:
                        dve.wait_ge(sinke_done, i + 1)
                        link(dve.tensor_tensor(den[:, heads], den[:, heads], sinke[:, :], ALU.add))
                        dve.wait_ge(o_free, i + 1)
                    link(dve.reciprocal(rden[:, heads], den[:, heads]))
                    dve.wait_ge(pv_done, i * NH + (g + 1) * NHA)
                    r = rden[:, heads].rearrange("p (h a) -> p h a", a=1).to_broadcast([P, NHA, HD])
                    dve.tensor_tensor(o[:, g, :].rearrange("p (h d) -> p h d", h=NHA), ps[:, 6 + g, :].rearrange("p (h d) -> p h d", h=NHA), r, ALU.mult).then_inc(o_scaled, 1)

                def norm(g):
                    dve.wait_ge(rms_done, 2 * i + g + 1)
                    link(dve.reciprocal(stat[:, g, 2:3], stat[:, g, 1:2]))
                    dve.tensor_scalar(o[:, g, :], o[:, g, :], stat[:, g, 2:3], None, ALU.mult).then_inc(o_done, 1)

                dve.wait_ge(mask_a_loaded, 16 * i + 16)
                for s in range(NH):
                    if s == NHA:
                        dve.sem_inc(mask_a_free, 1)
                        dve.wait_ge(p_done, i * NH + NHA)
                        dve.tensor_tensor(sinkd[:, :], sink[:, :], negm[:, 0:NHA], ALU.add).then_inc(sinkd_done, 1)
                        dve.wait_ge(bias_ready, i + 1)
                    mask(s)
                    if s >= 1:
                        evacuate(s - 1)
                    if s == NHA + 2:
                        output(0)
                dve.sem_inc(bias_free, 1)
                evacuate(NH - 1)
                dve.wait_ge(p_done, i * NH + NH)
                output(1)
                norm(0)
                norm(1)
                assert link.count[0] == DVE_OWN, link.count


def middle(K):
    nc, io, ps, ring = K.nc, K.io, K.psum, K.ring
    ctx = ExitStack()
    with ctx:
        sb, sem = scope(K, ctx)
        mix, xin = sb("mix", [P, 2, D]), sb("xres", [P, 2, D])
        mixT, h2T = sb("mixT", [P, KD, P]), sb("h2T", [P, KD, P])
        mixT2, h2T2 = sb("mixT2", [P, KD, P]), sb("h2T2", [P, KD, P])
        x1, h2 = sb("x1", [P, 2, D]), sb("h2", [P, 2, D])
        squares = sb("squares3", [P, D])
        gate1, scale2, shift2, gain = sb("gate1", [P, D]), sb("scale2", [P, D]), sb("shift2", [P, D]), sb("gain", [P, 2, D])
        w_router, b_router = sb("w_router", [P, KD, E]), sb("b_router", [P, E])
        stat = sb("stat3", [P, T, 6])
        tri, iota, ones = sb("tri", [P, P]), sb("iota", [P, P]), sb("ones", [P, P])
        record = sb("record", [P, TOPK, T, 2], I32)
        logit = sb("logit", [P, T, E])
        top, topi, topf = sb("top", [P, T, 8]), sb("topi", [P, T, 8], U32), sb("topf", [P, T, 8])
        pick = sb("pick", [P, TOPK, T, E])
        chosen, before = sb("chosen", [P, T, E]), sb("before", [P, T + 1, E])
        base, prod = sb("base", [P, T, E]), sb("prod", [P, T, E])
        nsteps, over = sb("nsteps", [P, 2, E]), sb("over", [P, 2, E])
        scan = sb("scan", [P, 2, 2, E])
        start, count = sb("start", [P, 2, E]), sb("count", [P, E])
        shifted = sb("shifted", [P, T, E])
        braw, brest, bpart = sb("braw", [96, 2 * FF + D]), sb("brest", [96, 2 * FF + D]), sb("bpart", [96, 2 * FF + D], BF16)
        slotf = sb("slotf", [P, TOPK, T])
        expd, exps, norm = sb("expd", [P, T, TOPK]), sb("exps", [P, T, TOPK]), sb("norm", [P, T, 2])
        cmp, tabf = sb("cmp", [1, STEPS, E]), sb("tabf", [1, 2, STEPS])

        btab = sb("btab", [96, 2 * FF + D], BF16)
        braw_loaded, btab_done, btab_stored = sem("braw_loaded"), sem("btab_done"), sem("btab_stored")
        rows_loaded, tabs_loaded, ones_set = sem("rows_loaded"), sem("tabs_loaded"), sem("ones_set")
        mix_loaded = [sem("mix_loaded0"), sem("mix_loaded1")]
        xr_loaded = [sem("xr_loaded0"), sem("xr_loaded1")]
        stored = [sem("stored0"), sem("stored1")]
        mt_done, mt_copied, proj_done, x1_done, h2_done, h2_shifted = (sem(n) for n in ("mt_done", "mt_copied", "proj_done", "x1_done", "h2_done", "h2_shifted"))
        h2t_done, h2t_copied, logit_done, rms1_done, rms2_done = (sem(n) for n in ("h2t_done", "h2t_copied", "logit_done", "rms1_done", "rms2b_done"))
        chosen_done, pos_done, expd_done, exps_done, route_done, scattered = (sem(n) for n in ("chosen_done", "pos_done", "expd_done", "exps_done", "route_done", "scattered"))
        dve_own, act_own = sem("dve_own3"), sem("act_own3")
        mts, h2ts = [mixT, mixT2], [h2T, h2T2]

        block = ctx.enter_context(nc.Block())

        @block.sync
        def _(sp):
            def load(t):
                if t >= 2:
                    sp.wait_ge(mt_done, t - 1)
                    sp.wait_ge(x1_done, t - 1)
                sp.dma_start(mix[:, t % 2, :], K.mix_d[t * P:(t + 1) * P, :]).then_inc(mix_loaded[t % 2], 16)
                sp.dma_start(xin[:, t % 2, :], io["x"][0][t * P:(t + 1) * P, :]).then_inc(xr_loaded[t % 2], 16)

            load(0)
            load(1)
            for t in range(T):
                sp.wait_ge(h2_shifted, t + 1)
                sp.dma_start(K.x1_d[t * P:(t + 1) * P, :], x1[:, t % 2, :]).then_inc(stored[t % 2], 16)
                sp.dma_start(K.h2_d[t * P:(t + 1) * P, :], h2[:, t % 2, :]).then_inc(stored[t % 2], 16)
                if t + 2 < T:
                    load(t + 2)
            sp.wait_ge(btab_done, 3)
            sp.dma_start(K.btab_d, btab[:, :]).then_inc(btab_stored, 16)
            sp.wait_ge(btab_stored, 16)
            for s in range(2):
                sp.wait_ge(stored[s], 32 * (T // 2))

        @block.gpsimd
        def _(pool):
            pool.memset(ones[:, :], 1.0).then_inc(ones_set, 1)
            for dst, src in ((gate1, K.mod_d[0:1, 2 * D:3 * D]), (shift2, K.mod_d[0:1, 3 * D:4 * D]), (scale2, K.mod_d[0:1, 4 * D:5 * D])):
                pool.dma_start(dst[:, :], src.to_broadcast([P, D])).then_inc(rows_loaded, 16)
            pool.dma_start(gain[:, 0, :], io["g_post_mix"].to_broadcast([P, D])).then_inc(rows_loaded, 16)
            pool.dma_start(gain[:, 1, :], io["g_pre_ffn"].to_broadcast([P, D])).then_inc(rows_loaded, 16)
            pool.dma_start(w_router[:, :, :], io["w_router"][0].rearrange("(k p) n -> p k n", p=P)).then_inc(tabs_loaded, 16)
            pool.dma_start(b_router[:, :], io["b_router"].to_broadcast([P, E])).then_inc(tabs_loaded, 16)
            pool.dma_start(tri[:, :], io["k_tri"]).then_inc(tabs_loaded, 16)
            pool.dma_start(iota[:, :], io["k_iota"]).then_inc(tabs_loaded, 16)
            pool.dma_start(record[:, :, :, :].rearrange("p k t a -> p (k t a)"), io["k_record"]).then_inc(tabs_loaded, 16)
            for part in range(3):
                rows = slice(E * part, E * part + E)
                pool.dma_start(braw[rows, 0:2 * FF], io["b_mlp1"][0]).then_inc(braw_loaded, 16)
                pool.dma_start(braw[rows, 2 * FF:], io["b_mlp2"][0]).then_inc(braw_loaded, 16)
            pool.wait_ge(rows_loaded, 80)
            for t in range(T):
                pool.wait_ge(h2_done, t + 1)
                pool.tensor_tensor(h2[:, t % 2, :], h2[:, t % 2, :], shift2[:, :], ALU.add).then_inc(h2_shifted, 1)
            pool.wait_ge(tabs_loaded, 80)
            pool.wait_ge(route_done, 1)
            for k in range(TOPK):
                for t in range(T):
                    pool.indirect_dma_start(K.slot_d, bass.IndirectOffsetOnAxis(ap=K.slots[:, k, t:t + 1], axis=0), record[:, k, t, :], None).then_inc(scattered, 16)
            pool.wait_ge(scattered, 16 * TOPK * T)

        @block.tensor
        def _(pe):
            def to_columns(t):
                pe.wait_ge(mix_loaded[t % 2], 16 * (t // 2 + 1))
                if t:
                    pe.wait_ge(mt_copied, t)
                for k in range(KD):
                    last = pe.transpose(ps[:, k // 4, (k % 4) * P:(k % 4 + 1) * P], mix[:, t % 2, k * P:(k + 1) * P], K.ident[:, :])
                last.then_inc(mt_done, 1)

            def project(t):
                pe.wait_ge(mt_copied, t + 1)
                if t:
                    pe.wait_ge(x1_done, t)
                for n in range(2):
                    for k in range(KD):
                        last = pe.matmul(ps[:, 2 + n, :], mts[t % 2][:, k, :], ring[:, n, k, :], start=(k == 0), stop=(k == KD - 1))
                last.then_inc(proj_done, 1)

            def route(t):
                pe.wait_ge(h2_shifted, t + 1)
                if t:
                    pe.wait_ge(h2t_copied, t)
                for k in range(KD):
                    last = pe.transpose(ps[:, 4 + k // 4, (k % 4) * P:(k % 4 + 1) * P], h2[:, t % 2, k * P:(k + 1) * P], K.ident[:, :])
                last.then_inc(h2t_done, 1)
                pe.wait_ge(h2t_copied, t + 1)
                for k in range(KD):
                    last = pe.matmul(ps[:, 6, t * E:(t + 1) * E], h2ts[t % 2][:, k, :], w_router[:, k, :], start=(k == 0), stop=(k == KD - 1))
                last.then_inc(logit_done, 1)

            pe.wait_ge(tabs_loaded, 80)
            to_columns(0)
            for t in range(T):
                if t + 1 < T:
                    to_columns(t + 1)
                project(t)
                if t:
                    route(t - 1)
            route(T - 1)
            pe.wait_ge(ones_set, 1)
            pe.wait_ge(chosen_done, 1)
            flat = lambda x: x.rearrange("p t e -> p (t e)")
            pe.matmul(ps[:, 7, 0:T * E], tri[:, :], flat(chosen[:, :, :]), start=True, stop=False)
            pe.matmul(ps[:, 7, 0:T * E], ones[:, :], flat(before[:, 0:T, :]), start=False, stop=True)
            pe.matmul(ps[:, 7, T * E:(T + 1) * E], ones[:, :], before[:, T, :], start=True, stop=True).then_inc(pos_done, 1)

        @block.scalar
        def _(act):
            link = linker(act, act_own)

            def copy_h2(t):
                act.wait_ge(h2t_done, t + 1)
                if t >= 2:
                    act.wait_ge(logit_done, t - 1)
                act.activation(h2ts[t % 2][:, :, :].rearrange("p k n -> p (k n)"), ps[:, 4:6, :].rearrange("p b n -> p (b n)"), ACT.Copy).then_inc(h2t_copied, 1)

            for t in range(T):
                act.wait_ge(proj_done, t + 1)
                link(act.activation(squares[:, :], ps[:, 2:4, :].rearrange("p b n -> p (b n)"), ACT.Square, accum_out=stat[:, t, 0:1]))
                act.activation(stat[:, t, 1:2], stat[:, t, 0:1], ACT.Sqrt, bias=K.eps[:, :], scale=1.0 / D).then_inc(rms1_done, 1)
                act.wait_ge(x1_done, t + 1)
                link(act.activation(squares[:, :], x1[:, t % 2, :], ACT.Square, accum_out=stat[:, t, 3:4]))
                act.activation(stat[:, t, 4:5], stat[:, t, 3:4], ACT.Sqrt, bias=K.eps[:, :], scale=1.0 / D).then_inc(rms2_done, 1)
                if t:
                    copy_h2(t - 1)
            copy_h2(T - 1)
            act.wait_ge(expd_done, 1)
            act.activation(exps[:, :, :], expd[:, :, :], ACT.Exp).then_inc(exps_done, 1)

        @block.vector
        def _(dve):
            link = linker(dve, dve_own)
            dve.wait_ge(rows_loaded, 80)
            link(dve.tensor_tensor(gate1[:, :], gate1[:, :], gain[:, 0, :], ALU.mult))
            link(dve.scalar_tensor_tensor(scale2[:, :], scale2[:, :], 1.0, gain[:, 1, :], ALU.add, ALU.mult))

            def copy_mix(t):
                dve.wait_ge(mt_done, t + 1)
                if t >= 2:
                    dve.wait_ge(proj_done, t - 1)
                for k in range(KD):
                    last = dve.tensor_scalar(mts[t % 2][:, k, :], ps[:, k // 4, (k % 4) * P:(k % 4 + 1) * P], K.colv[:, 40 + k:41 + k], None, ALU.mult)
                last.then_inc(mt_copied, 1)

            copy_mix(0)
            for t in range(T):
                if t + 1 < T:
                    copy_mix(t + 1)
                s = t % 2
                dve.wait_ge(rms1_done, t + 1)
                link(dve.reciprocal(stat[:, t, 2:3], stat[:, t, 1:2]))
                if t >= 2:
                    dve.wait_ge(stored[s], 32 * (t // 2))
                    dve.wait_ge(h2t_done, t - 1)
                link(dve.scalar_tensor_tensor(x1[:, s, :], ps[:, 2:4, :].rearrange("p b n -> p (b n)"), stat[:, t, 2:3], gate1[:, :], ALU.mult, ALU.mult))
                dve.wait_ge(xr_loaded[s], 16 * (t // 2 + 1))
                dve.tensor_tensor(x1[:, s, :], x1[:, s, :], xin[:, s, :], ALU.add).then_inc(x1_done, 1)
                dve.wait_ge(rms2_done, t + 1)
                link(dve.reciprocal(stat[:, t, 5:6], stat[:, t, 4:5]))
                dve.scalar_tensor_tensor(h2[:, s, :], x1[:, s, :], stat[:, t, 5:6], scale2[:, :], ALU.mult, ALU.mult).then_inc(h2_done, 1)
            dve.wait_ge(logit_done, T)
            dve.wait_ge(tabs_loaded, 80)
            row = lambda x: x.rearrange("p (a n) -> p a n", a=1)
            link(dve.tensor_tensor(logit[:, :, :], ps[:, 6, 0:T * E].rearrange("p (t e) -> p t e", e=E), row(b_router[:, :]).to_broadcast([P, T, E]), ALU.add))
            for t in range(T):
                last = dve.max(top[:, t, :], logit[:, t, :])
            link(last)
            dve.tensor_tensor(expd[:, :, :], top[:, :, 0:TOPK], top[:, :, 0:1].to_broadcast([P, T, TOPK]), ALU.subtract).then_inc(expd_done, 1)
            for t in range(T):
                last = dve.max_index(topi[:, t, :], top[:, t, :], logit[:, t, :])
            link(last)
            link(dve.tensor_copy(topf[:, :, :], topi[:, :, :]))
            for k in range(TOPK):
                last = dve.tensor_tensor(pick[:, k, :, :], row(iota[:, 0:E]).to_broadcast([P, T, E]), topf[:, :, k:k + 1].to_broadcast([P, T, E]), ALU.is_equal)
            link(last)
            link(dve.tensor_tensor(base[:, :, :], pick[:, 0, :, :], pick[:, 1, :, :], ALU.add))
            link(dve.tensor_tensor(prod[:, :, :], pick[:, 2, :, :], pick[:, 3, :, :], ALU.add))
            link(dve.tensor_tensor(chosen[:, :, :], base[:, :, :], prod[:, :, :], ALU.add))
            link(dve.memset(before[:, 0, :], 0.0))
            for t in range(T):
                ins = dve.tensor_tensor(before[:, t + 1, :], before[:, t, :], chosen[:, t, :], ALU.add)
                if t + 1 < T:
                    link(ins)
            ins.then_inc(chosen_done, 1)
            dve.wait_ge(exps_done, 1)
            link(dve.tensor_reduce(norm[:, :, 0:1], exps[:, :, :], AX.X, ALU.add))
            link(dve.reciprocal(norm[:, :, 1:2], norm[:, :, 0:1]))
            link(dve.tensor_tensor(K.weights[:, :, :], exps[:, :, :], norm[:, :, 1:2].to_broadcast([P, T, TOPK]), ALU.mult))
            dve.wait_ge(pos_done, 1)
            link(dve.tensor_copy(count[:, :], ps[:, 7, T * E:(T + 1) * E]))
            link(dve.tensor_scalar(over[:, 0, :], count[:, :], 0.0, None, ALU.is_gt))
            for m in range(1, SEQ // P):
                link(dve.scalar_tensor_tensor(over[:, m % 2, :], count[:, :], float(P * m), over[:, (m - 1) % 2, :], ALU.is_gt, ALU.add))
            blocks = over[:, (SEQ // P - 1) % 2, :]
            for m in range(0, SEQ // (2 * P)):
                if m == 0:
                    link(dve.tensor_scalar(nsteps[:, m % 2, :], count[:, :], float(P), None, ALU.is_gt))
                else:
                    link(dve.scalar_tensor_tensor(nsteps[:, m % 2, :], count[:, :], float(P * (2 * m + 1)), nsteps[:, (m - 1) % 2, :], ALU.is_gt, ALU.add))
            link(dve.tensor_copy(nsteps[:, 0, :], nsteps[:, 1, :]))
            link(dve.scalar_tensor_tensor(nsteps[:, 1, :], nsteps[:, 0, :], -2.0, blocks, ALU.mult, ALU.add))
            link(dve.tensor_copy(scan[:, 0, :, :], nsteps[:, :, :]))
            cur = 0
            for shift in (1, 2, 4, 8, 16):
                link(dve.tensor_copy(scan[:, 1 - cur, :, 0:shift], scan[:, cur, :, 0:shift]))
                link(dve.tensor_tensor(scan[:, 1 - cur, :, shift:], scan[:, cur, :, shift:], scan[:, cur, :, 0:E - shift], ALU.add))
                cur = 1 - cur
            ends = scan[:, cur, :, :]
            link(dve.tensor_tensor(start[:, :, :], ends, nsteps[:, :, :], ALU.subtract))
            rank = ps[:, 7, 0:T * E].rearrange("p (t e) -> p t e", e=E)
            wide = lambda x: row(x).to_broadcast([P, T, E])
            link(dve.scalar_tensor_tensor(base[:, :, :], wide(start[:, 0, :]), float(2 * P), rank, ALU.mult, ALU.add))
            link(dve.tensor_scalar(start[:, 1, :], start[:, 1, :], float(P), float(PAIR_SLOTS), ALU.mult, ALU.add))
            link(dve.scalar_tensor_tensor(start[:, 1, :], scan[:, cur, 0, :], -2.0 * P, start[:, 1, :], ALU.mult, ALU.add))
            link(dve.scalar_tensor_tensor(shifted[:, :, :], wide(nsteps[:, 0, :]), float(2 * P), rank, ALU.mult, ALU.is_le))
            link(dve.tensor_tensor(shifted[:, :, :], shifted[:, :, :], wide(start[:, 1, :]), ALU.mult))
            link(dve.tensor_tensor(base[:, :, :], base[:, :, :], shifted[:, :, :], ALU.add))
            for k in range(TOPK):
                link(dve.tensor_tensor(prod[:, :, :], pick[:, k, :, :], base[:, :, :], ALU.mult))
                link(dve.tensor_reduce(slotf[:, k, :], prod[:, :, :], AX.X, ALU.add))
            link(dve.tensor_copy(K.slots[:, :, :], slotf[:, :, :]))
            for kind, at in ((0, PAIR_AT), (1, SINGLE_AT)):
                link(dve.tensor_tensor(cmp[:, :, :], row(scan[0:1, cur, kind, :]).to_broadcast([1, STEPS, E]), iota[0:1, 0:STEPS].rearrange("p (n a) -> p n a", a=1).to_broadcast([1, STEPS, E]), ALU.is_le))
                link(dve.tensor_reduce(tabf[:, 0, :], cmp[:, :, :], AX.X, ALU.add))
                link(dve.tensor_scalar(tabf[:, 1, :], tabf[:, 0, :], float(E - 1), None, ALU.min))
                link(dve.tensor_copy(K.table[:, at:at + STEPS], tabf[:, 1, :]))
            dve.tensor_copy(K.table[:, PAIR_COUNT:SINGLE_COUNT + 1], scan[0:1, cur, :, E - 1]).then_inc(route_done, 1)
            dve.wait_ge(braw_loaded, 16 * 6)
            src = braw
            for part in range(3):
                rows = slice(E * part, E * part + E)
                link(dve.tensor_copy(bpart[:, :], src[:, :]))
                dve.tensor_copy(btab[rows, :], bpart[rows, :]).then_inc(btab_done, 1)
                if part < 2:
                    link(dve.tensor_tensor(brest[:, :], src[:, :], bpart[:, :], ALU.subtract))
                    src = brest
                    dve.wait_ge(btab_done, part + 1)


def experts(K, R, steps_at, count_at, slot_base):
    nc, io, ps = K.nc, K.io, K.psum
    w1 = io["w_mlp1"][0].rearrange("e (k p) n -> e p k n", p=P)
    w2 = io["w_mlp2"][0].rearrange("e (k p) n -> e p k n", p=P)
    UP, DOWN = 2 * FF // UNIT, D // UNIT
    NU, RING, CH = UP + DOWN, 3, 2
    PAIRS = UNIT // 2
    KC = KD // CH
    UPS, DOWNS = UP * R, DOWN * R
    ctx = ExitStack()
    with ctx:
        sb = lambda name, shape, dt=F32: ctx.enter_context(nc.sbuf_tensor(f"{name}_{R}", shape, dt))
        sem = lambda name: K.semaphores.enter_context(nc.semaphore(f"{name}_{R}"))
        ring = sb("wring", [P, RING, KD, UNIT])
        w_hi, w_lo = sb("w_hi", [P, 2, KD, UNIT], F32R), sb("w_lo", [P, 2, KD, UNIT], F32R)
        xg = sb("xg", [P, R, D])
        x_hi, x_lo = sb("x_hi", [P, R, KD, P], F32R), sb("x_lo", [P, R, KD, P], F32R)
        a_hi, a_lo = sb("a_hi", [P, R, KD, P], F32R), sb("a_lo", [P, R, KD, P], F32R)
        glu, lin, sig, act_o = (sb(n, [P, 2, PAIRS]) for n in ("glu", "lin", "sig", "act_o"))
        y = sb("y", [P, R, D])
        record, y_row, int_zero = sb("record", [P, R, 2], I32), sb("y_row", [P, R], I32), sb("int_zero", [P, R], I32)
        poolgate = sb("poolgate", [P, 2])
        onehot = sb("onehot", [96, E])
        btab = sb("btab", [96, 2 * FF + D], BF16)
        sel_up, sel_down = sb("sel_up", [96, P], BF16), sb("sel_down", [96, P], BF16)

        bias_loaded = sem("bias_loaded")
        w_loaded = [sem(f"w_loaded{r}") for r in range(RING)]
        hi_done, lo_done, prod_done = sem("hi_done"), sem("lo_done"), sem("prod_done")
        record_loaded, gathered, gate_open = sem("record_loaded"), sem("gathered"), sem("gate_open")
        xt_done, xhi_done, x_ready = sem("xt_done"), sem("xhi_done"), sem("x_ready")
        sel_up_ready, sel_down_ready = sem("sel_up_ready"), sem("sel_down_ready")
        glu_done, sig_done, up_free, act_done = sem("glu_done"), sem("sig_done"), sem("up_free"), sem("act_done")
        at_done, ahi_done, a_ready = sem("at_done"), sem("ahi_done"), sem("a_ready")
        y_copied, y_stored, y_free = sem("y_copied"), sem("y_stored"), sem("y_free")
        dve_own = sem("dve_own")

        block = ctx.enter_context(nc.Block())

        def step_count(engine):
            return engine.value_load(K.table[0:1, count_at:count_at + 1], min_val=0, max_val=E)

        def expert_of(engine, step):
            at = slice(steps_at, steps_at + 1) if isinstance(step, int) else bass.ds(step + steps_at, 1)
            return engine.value_load(K.table[0:1, at], min_val=0, max_val=E - 1)

        def wait_loaded(engine, b, n):
            engine.wait_ge(w_loaded[n % RING], 16 * ((NU // RING) * b + n // RING + 1))

        def wait_product(engine, b, n, r):
            engine.wait_ge(prod_done, R * (NU * b + n) + 2 * R + r + 1)

        @block.sync
        def _(sp):
            def load(b, n, e):
                sp.wait_ge(lo_done, CH * (NU * b + n) + CH)
                src = w1[bass.ds(e, 1), :, :, n * UNIT:(n + 1) * UNIT] if n < UP else w2[bass.ds(e, 1), :, :, (n - UP) * UNIT:(n - UP + 1) * UNIT]
                sp.dma_start(ring[:, n % RING, :, :], src.rearrange("a p k n -> (a p) k n")).then_inc(w_loaded[n % RING], 16)

            steps = step_count(sp)
            load(0, 0, expert_of(sp, 0))
            with sp.Fori(0, steps) as b:
                e, e_next = expert_of(sp, b), expert_of(sp, b + 1)
                for n in range(1, NU):
                    load(b, n, e)
                load(b + 1, 0, e_next)

        @block.gpsimd
        def _(pool):
            pool.sem_inc(y_free, 1)
            pool.memset(int_zero[:, :], 0).then_inc(gate_open, 1)
            pool.wait_ge(gate_open, 1)
            pool.memset(poolgate[:, :], 0.0).then_inc(gate_open, 1)
            pool.dma_start(onehot[:, :], io["k_onehot"]).then_inc(bias_loaded, 16)
            pool.dma_start(btab[:, :], K.btab_d).then_inc(bias_loaded, 16)
            pool.wait_ge(gate_open, 2)
            steps = step_count(pool)

            def gate():
                pool.tensor_tensor(poolgate[:, 1:2], poolgate[:, 0:1], poolgate[:, 0:1], ALU.add).then_inc(gate_open, 1)

            def gather():
                for r in range(R):
                    pool.indirect_dma_start(xg[:, r, :], None, K.h2_d, bass.IndirectOffsetOnAxis(ap=record[:, r, 0:1], axis=0)).then_inc(gathered, 16)

            pool.dma_start(record[:, :, :], K.slot_d[slot_base:slot_base + R * P, :].rearrange("(r p) a -> p r a", p=P)).then_inc(record_loaded, 16)
            pool.wait_ge(record_loaded, 16)
            gather()
            pool.wait_ge(gathered, 16 * R)
            with pool.Fori(0, steps) as b:
                pool.wait_ge(gate_open, 3 * b + 2)
                pool.tensor_tensor(y_row[:, :], record[:, :, 1], int_zero[:, :], ALU.add).then_inc(gate_open, 1)
                pool.wait_ge(gate_open, 3 * b + 3)
                pool.dma_start(record[:, :, :], K.slot_d[bass.ds(b * (R * P) + (slot_base + R * P), R * P), :].rearrange("(r p) a -> p r a", p=P)).then_inc(record_loaded, 16)
                pool.wait_ge(record_loaded, 16 * b + 32)
                pool.wait_ge(xt_done, R * b + R)
                gate()
                gather()
                pool.wait_ge(gathered, 16 * R * b + 32 * R)
                pool.wait_ge(gate_open, 3 * b + 4)
                pool.wait_ge(y_copied, DOWNS * b + DOWNS + 2)
                gate()
                for r in range(R):
                    pool.indirect_dma_start(K.y_d, bass.IndirectOffsetOnAxis(ap=y_row[:, r:r + 1], axis=0), y[:, r, :], None).then_inc(y_stored, 16)
                pool.wait_ge(y_stored, 16 * R * b + 16 * R)
                pool.sem_inc(y_free, 1)
            pool.wait_ge(bias_loaded, 32)

        @block.scalar
        def _(act):
            act.sem_inc(y_copied, 2)

            def split(b, n):
                wait_loaded(act, b, n)
                act.wait_ge(prod_done, R * (NU * b + n) + R)
                for c in range(CH):
                    k = slice(KC * c, KC * (c + 1))
                    act.activation(w_hi[:, n % 2, k, :], ring[:, n % RING, k, :], ACT.Copy).then_inc(hi_done, 1)

            def rows(b, r):
                act.wait_ge(xt_done, R * b + r + 1)
                act.activation(x_hi[:, r, :, :].rearrange("p k n -> p (k n)"), ps[:, 6:8, :].rearrange("p b n -> p (b n)"), ACT.Copy).then_inc(xhi_done, 1)

            def columns(b, j):
                act.wait_ge(at_done, UPS * b + j + 1)
                n, r = divmod(j, R)
                act.activation(a_hi[:, r, 2 * n:2 * n + 2, :].rearrange("p k n -> p (k n)"), ps[:, 2 + j % 2, 0:2 * P], ACT.Copy).then_inc(ahi_done, 1)

            steps = step_count(act)
            split(0, 0)
            for r in range(R):
                rows(0, r)
            with act.Fori(0, steps) as b:
                for n in range(NU):
                    split(b + (n + 1) // NU, (n + 1) % NU)
                    if n < UP:
                        for j in range(n * R, n * R + R):
                            act.wait_ge(glu_done, UPS * b + j + 1)
                            act.activation(sig[:, j % 2, :], glu[:, j % 2, :], ACT.Sigmoid, scale=ALPHA).then_inc(sig_done, 1)
                            if j:
                                columns(b, j - 1)
                        continue
                    if n == UP:
                        rows(b + 1, 0)
                        columns(b, UPS - 1)
                        act.wait_ge(y_free, b + 1)
                    h = n - UP
                    for r in range(R):
                        wait_product(act, b, n, r)
                        act.activation(y[:, r, h * UNIT:(h + 1) * UNIT], ps[:, 4 + (h * R + r) % 2, :], ACT.Copy).then_inc(y_copied, 1)
                        if n == UP and r + 1 < R:
                            rows(b + 1, r + 1)

        @block.vector
        def _(dve):
            dve.sem_inc(lo_done, RING * CH)
            dve.sem_inc(up_free, 2)
            dve.sem_inc(a_ready, 2)

            def split(b, n):
                for c in range(CH):
                    k = slice(KC * c, KC * (c + 1))
                    dve.wait_ge(hi_done, CH * (NU * b + n) + c + 1)
                    dve.tensor_tensor(w_lo[:, n % 2, k, :], ring[:, n % RING, k, :], w_hi[:, n % 2, k, :].bitcast(F32), ALU.subtract).then_inc(lo_done, 1)

            def rows(b, r):
                dve.wait_ge(xhi_done, R * b + r + 1)
                dve.tensor_tensor(x_lo[:, r, :, :].rearrange("p k n -> p (k n)"), ps[:, 6:8, :].rearrange("p b n -> p (b n)"),
                                  x_hi[:, r, :, :].bitcast(F32).rearrange("p k n -> p (k n)"), ALU.subtract).then_inc(x_ready, 1)

            def columns(b, j):
                dve.wait_ge(ahi_done, UPS * b + j + 1)
                n, r = divmod(j, R)
                dve.tensor_tensor(a_lo[:, r, 2 * n:2 * n + 2, :].rearrange("p k n -> p (k n)"), ps[:, 2 + j % 2, 0:2 * P],
                                  a_hi[:, r, 2 * n:2 * n + 2, :].bitcast(F32).rearrange("p k n -> p (k n)"), ALU.subtract).then_inc(a_ready, 1)

            def select(sel, e, ready):
                col = onehot[:, bass.ds(e, 1)]
                dve.tensor_copy(sel[:, :], col.to_broadcast([96, P])).then_inc(ready, 1)

            steps = step_count(dve)
            dve.wait_ge(bias_loaded, 32)
            select(sel_up, expert_of(dve, 0), sel_up_ready)
            split(0, 0)
            for r in range(R):
                rows(0, r)
            with dve.Fori(0, steps) as b:
                link = linker(dve, dve_own, b * UPS)
                e, e_next = expert_of(dve, b), expert_of(dve, b + 1)
                for n in range(NU):
                    split(b + (n + 1) // NU, (n + 1) % NU)
                    if n == 0:
                        dve.wait_ge(prod_done, R * NU * b + 2 * R)
                        select(sel_down, e, sel_down_ready)
                    if n < UP:
                        for j in range(n * R, n * R + R):
                            s = j % 2
                            pairs = ps[:, s, :].rearrange("p (j two) -> p j two", two=2)
                            wait_product(dve, b, n, j - n * R)
                            if j >= 2:
                                dve.wait_ge(at_done, UPS * b + j - 1)
                            dve.tensor_scalar(glu[:, s, :], pairs[:, :, 0], LIMIT, None, ALU.min).then_inc(glu_done, 1)
                            dve.tensor_scalar(lin[:, s, :], pairs[:, :, 1], LIMIT, -LIMIT, ALU.min, ALU.max).then_inc(up_free, 1)
                            dve.wait_ge(up_free, UPS * b + j + 3)
                            link(dve.scalar_tensor_tensor(lin[:, s, :], lin[:, s, :], 1.0, glu[:, s, :], ALU.add, ALU.mult))
                            dve.wait_ge(sig_done, UPS * b + j + 1)
                            dve.tensor_tensor(act_o[:, s, :], lin[:, s, :], sig[:, s, :], ALU.mult).then_inc(act_done, 1)
                            if j:
                                columns(b, j - 1)
                        if n == UP - 1:
                            select(sel_up, e_next, sel_up_ready)
                    elif n == UP:
                        rows(b + 1, 0)
                        columns(b, UPS - 1)
                        for r in range(1, R):
                            rows(b + 1, r)
                assert link.count[0] == UPS

        @block.tensor
        def _(pe):
            pe.sem_inc(prod_done, 2 * R)

            def rows(b, r):
                pe.wait_ge(gathered, 16 * R * b + 16 * R)
                if not isinstance(b, int) or r:
                    pe.wait_ge(x_ready, R * b + r)
                for k in range(KD):
                    last = pe.transpose(ps[:, 6 + k // 4, (k % 4) * P:(k % 4 + 1) * P], xg[:, r, k * P:(k + 1) * P], K.ident[:, :])
                last.then_inc(xt_done, 1)

            def columns(b, j):
                pe.wait_ge(act_done, UPS * b + j + 1)
                pe.wait_ge(a_ready, UPS * b + j + 1)
                for c in range(2):
                    last = pe.transpose(ps[:, 2 + j % 2, c * P:(c + 1) * P], act_o[:, j % 2, c * P:(c + 1) * P], K.ident[:, :])
                last.then_inc(at_done, 1)

            def product(b, n, r, bank, hi, lo, ready):
                for c in range(CH):
                    if r == 0:
                        pe.wait_ge(lo_done, CH * (NU * b + n) + c + 1 + RING * CH)
                    for k in range(KC * c, KC * (c + 1)):
                        if ready:
                            ready(k, r)
                        pe.matmul(bank, hi[:, r, k, :], w_hi[:, n % 2, k, :], start=False, stop=False)
                        pe.matmul(bank, hi[:, r, k, :], w_lo[:, n % 2, k, :], start=False, stop=False)
                        last = pe.matmul(bank, lo[:, r, k, :], w_hi[:, n % 2, k, :], start=False, stop=(k == KD - 1))
                last.then_inc(prod_done, 1)

            steps = step_count(pe)
            for r in range(R):
                rows(0, r)
            with pe.Fori(0, steps) as b:
                pe.wait_ge(sel_up_ready, b + 1)
                for j in range(UPS):
                    n, r = divmod(j, R)
                    if n == 0:
                        pe.wait_ge(x_ready, R * b + r + 1)
                    pe.wait_ge(up_free, UPS * b + j + 1)
                    pe.matmul(ps[:, j % 2, :], sel_up[:, :], btab[:, n * UNIT:(n + 1) * UNIT], start=True, stop=False)
                    product(b, n, r, ps[:, j % 2, :], x_hi, x_lo, None)
                    if j:
                        columns(b, j - 1)
                rows(b + 1, 0)
                columns(b, UPS - 1)
                pe.wait_ge(sel_down_ready, b + 1)

                def ready(k, r):
                    if k % 2 == 0:
                        pe.wait_ge(a_ready, UPS * b + (k // 2) * R + r + 3)

                for i in range(DOWNS):
                    h, r = divmod(i, R)
                    pe.wait_ge(y_copied, DOWNS * b + i + 1)
                    bank = ps[:, 4 + i % 2, :]
                    pe.matmul(bank, sel_down[:, :], btab[:, 2 * FF + h * UNIT:2 * FF + (h + 1) * UNIT], start=True, stop=False)
                    product(b, UP + h, r, bank, a_hi, a_lo, ready if h == 0 else None)
                    if h == 0 and r + 1 < R:
                        rows(b + 1, r + 1)


def combine(K):
    nc, io = K.nc, K.io
    ctx = ExitStack()
    with ctx:
        sb, sem = scope(K, ctx)
        yg = sb("yg", [P, 2, TOPK, D])
        x1 = sb("x1r", [P, 2, D])
        acc, out = sb("acc", [P, 2, D]), sb("outt", [P, 2, D])
        squares = sb("squares5", [P, D])
        gate2, gain = sb("gate2", [P, D]), sb("gain5", [P, D])
        stat = sb("stat5", [P, T, 3])
        rows_loaded = sem("rows_loaded5")
        tile_loaded = [sem("tile_loaded5_0"), sem("tile_loaded5_1")]
        stored = [sem("stored5_0"), sem("stored5_1")]
        acc_done, rms_done, out_done, dve_own, act_own = sem("acc_done"), sem("rms_done5"), sem("out_done"), sem("dve_own5"), sem("act_own5")
        y_rows = K.y_d[0:TOPK * SEQ, :].rearrange("(k t p) d -> t p k d", t=T, p=P)
        block = ctx.enter_context(nc.Block())

        @block.sync
        def _(sp):
            def store(t):
                sp.wait_ge(out_done, t + 1)
                sp.dma_start(io["out"][0][t * P:(t + 1) * P, :], out[:, t % 2, :]).then_inc(stored[t % 2], 16)

            for t in range(T):
                if t >= 2:
                    sp.wait_ge(out_done, t - 1)
                sp.dma_start(yg[:, t % 2, :, :], y_rows[t]).then_inc(tile_loaded[t % 2], 16)
                sp.dma_start(x1[:, t % 2, :], K.x1_d[t * P:(t + 1) * P, :]).then_inc(tile_loaded[t % 2], 16)
                if t >= 1:
                    store(t - 1)
            store(T - 1)
            for s in range(2):
                sp.wait_ge(stored[s], 16 * (T // 2))

        @block.gpsimd
        def _(pool):
            pool.dma_start(gate2[:, :], K.mod_d[0:1, 5 * D:6 * D].to_broadcast([P, D])).then_inc(rows_loaded, 16)
            pool.dma_start(gain[:, :], io["g_post_ffn"].to_broadcast([P, D])).then_inc(rows_loaded, 16)
            pool.wait_ge(rows_loaded, 32)

        @block.scalar
        def _(act):
            link = linker(act, act_own)
            for t in range(T):
                act.wait_ge(acc_done, t + 1)
                link(act.activation(squares[:, :], acc[:, t % 2, :], ACT.Square, accum_out=stat[:, t, 0:1]))
                act.activation(stat[:, t, 1:2], stat[:, t, 0:1], ACT.Sqrt, bias=K.eps[:, :], scale=1.0 / D).then_inc(rms_done, 1)

        @block.vector
        def _(dve):
            link = linker(dve, dve_own)

            def add(t):
                s = t % 2
                dve.wait_ge(tile_loaded[s], 32 * (t // 2 + 1))
                link(dve.tensor_scalar(acc[:, s, :], yg[:, s, 0, :], K.weights[:, t, 0:1], None, ALU.mult))
                for k in range(1, TOPK):
                    ins = dve.scalar_tensor_tensor(acc[:, s, :], yg[:, s, k, :], K.weights[:, t, k:k + 1], acc[:, s, :], ALU.mult, ALU.add)
                    if k + 1 < TOPK:
                        link(ins)
                ins.then_inc(acc_done, 1)

            def finish(t):
                s = t % 2
                dve.wait_ge(rms_done, t + 1)
                link(dve.reciprocal(stat[:, t, 2:3], stat[:, t, 1:2]))
                if t >= 2:
                    dve.wait_ge(stored[s], 16 * (t // 2))
                link(dve.scalar_tensor_tensor(out[:, s, :], acc[:, s, :], stat[:, t, 2:3], gate2[:, :], ALU.mult, ALU.mult))
                dve.tensor_tensor(out[:, s, :], out[:, s, :], x1[:, s, :], ALU.add).then_inc(out_done, 1)

            add(0)
            dve.wait_ge(rows_loaded, 32)
            link(dve.tensor_tensor(gate2[:, :], gate2[:, :], gain[:, :], ALU.mult))
            for t in range(T):
                if t + 1 < T:
                    add(t + 1)
                finish(t)


_INS = ["x", "c", "ctx", "c_ctx", "w_ada", "b_ada", "g_pre_mix", "g_post_mix", "g_pre_ffn", "g_post_ffn",
        "w_in", "g_grp_a", "g_grp_b", "sink_a", "rpb_b", "w_out", "w_router", "b_router",
        "w_mlp1", "b_mlp1", "w_mlp2", "b_mlp2"]


def kernel(**inputs):
    import concourse.bacc as bacc
    from concourse.bass_utils import run_bass_kernel_spmd

    nc = bacc.Bacc("TRN2", target_bir_lowering=False, num_devices=1)
    arrays, io = {}, {}
    given = {name: inputs[name] for name in _INS}
    given.update(constants())
    for name, a in given.items():
        a = np.ascontiguousarray(a)
        arrays["in_" + name] = a
        io[name] = nc.dram_tensor("in_" + name, a.shape, mybir.dt.from_np(a.dtype), kind="ExternalInput").ap()
    io["out"] = nc.dram_tensor("out_0", (1, SEQ, D), F32, kind="ExternalOutput").ap()
    Kernel(nc, io).build()
    r = run_bass_kernel_spmd(nc, [arrays], core_ids=[0])
    return r.results[0]["out_0"]
```

```python
import concourse.bass as bass
from concourse import mybir
from contextlib import ExitStack
import numpy as np

F32 = mybir.dt.float32
F32R = mybir.dt.float32r
BF16 = mybir.dt.bfloat16
I32 = mybir.dt.int32
U32 = mybir.dt.uint32
ALU = mybir.AluOpType
ACT = mybir.ActivationFunctionType
AX = mybir.AxisListType

P = 128
D = 1024
KD = D // P
SEQ, CTX = 1024, 256
T = SEQ // P
TC = CTX // P
HD = 64
NHA, NKVA, NHB = 8, 2, 8
NH = NHA + NHB
GRID_W, GRID_H = 64, SEQ // 64
NA_ROWS, NA_COLS = 8, 16
WINDOW = 128
IN_W = 2304
E, TOPK, FF = 32, 4, 1024
EPS = 1e-6
LIMIT, ALPHA = 7.0, 1.702
NEG = -1e30
UNIT = 512
LA = P + 2 * WINDOW
LBR = 10
LB = LBR * GRID_W
TCOLS = 5
RPB_R, RPB_C = 2 * NA_ROWS - 1, 2 * NA_COLS - 1
BROWS = NHB * RPB_R + 4
BW = GRID_W + RPB_C - 1
STEPS = E + 1
PAIR_SLOTS, SINGLE_SLOTS = 2 * P * STEPS, P * STEPS
SLOTS = PAIR_SLOTS + SINGLE_SLOTS
PAIR_AT, SINGLE_AT = 0, STEPS
PAIR_COUNT, SINGLE_COUNT = 2 * STEPS, 2 * STEPS + 1
assert SEQ * TOPK // (P + 1) < E


def constants():
    f = np.float32
    out = {}
    out["k_ident"] = np.eye(P, dtype=f)
    d = np.arange(P)
    partner = np.where((d % 32) < 16, d + 16, d - 16)
    perm = np.zeros((P, P), f)
    perm[partner, d] = 1
    out["k_perm"] = perm
    pos = np.arange(SEQ)
    rows, cols = (pos // GRID_W).astype(f), (pos % GRID_W).astype(f)
    nf = HD // 4
    freqs = (f(10000.0) ** (-np.arange(nf, dtype=f) / f(nf))).astype(f)
    fr = freqs[d % 16]
    isrow = (d % HD) < 32
    ang = np.where(isrow[:, None], fr[:, None] * rows[None], fr[:, None] * cols[None]).astype(f)
    sign = np.where((d % 32) < 16, -1.0, 1.0).astype(f)
    out["k_cos"] = np.cos(ang).astype(f)
    out["k_sin"] = (np.sin(ang) * sign[:, None]).astype(f)
    mask_a = np.zeros((T, P, LA + CTX), f)
    mask_b = np.zeros((T, P, LB), f)
    tab = np.zeros((T + 1, TCOLS), np.int32)
    for i in range(T):
        k0 = min(max(i - 1, 0), T - 3) * P
        q = i * P + np.arange(P)
        k = k0 + np.arange(LA)
        mask_a[i, :, :LA] = np.where(np.abs(k[None] - q[:, None]) <= WINDOW, 0, NEG)
        base = min(max(2 * i - NA_ROWS // 2, 0), GRID_H - LBR)
        r, qc = q // GRID_W, q % GRID_W
        rs = np.clip(r - NA_ROWS // 2, 0, GRID_H - NA_ROWS)
        cs = np.clip(qc - NA_COLS // 2, 0, GRID_W - NA_COLS)
        kr, kc = base + np.arange(LBR), np.arange(GRID_W)
        ok = ((kr[None] >= rs[:, None]) & (kr[None] < rs[:, None] + NA_ROWS))[:, :, None] & \
             ((kc[None] >= cs[:, None]) & (kc[None] < cs[:, None] + NA_COLS))[:, None, :]
        mask_b[i] = np.where(ok, 0, NEG).reshape(P, LB)
        tab[i] = (k0, base * GRID_W, base - 2 * i + 7 + 2, base - 2 * i - 1 + 7 + 2, i * P)
    tab[T] = tab[T - 1]
    out["k_mask_a"], out["k_mask_b"] = mask_a, mask_b
    out["k_tiles"] = tab.reshape(1, -1)
    out["k_tri"] = np.triu(np.ones((P, P), f), 1)
    out["k_iota"] = np.broadcast_to(np.arange(P, dtype=f), (P, P)).copy()
    out["k_zeros"] = np.zeros((1, BROWS * BW), f)
    out["k_onehot"] = (np.arange(96)[:, None] % E == np.arange(E)[None]).astype(f)
    token = np.arange(P)[:, None, None] + P * np.arange(T)[None, None]
    record = np.stack(np.broadcast_arrays(token, token + SEQ * np.arange(TOPK)[None, :, None]), axis=-1)
    out["k_record"] = record.reshape(P, TOPK * T * 2).astype(np.int32)
    spare = TOPK * SEQ + np.arange(SLOTS) % P
    out["k_empty"] = np.stack([0 * spare, spare], axis=-1).astype(np.int32)
    return out


def raw_ap(ap, offset, dims):
    return bass.AP(tensor=ap.tensor, offset=offset, ap=dims)


class Kernel:

    def __init__(self, nc, io):
        self.nc, self.io = nc, io

    def build(self):
        nc, io = self.nc, self.io
        with ExitStack() as ctx:
            self.semaphores = ctx.enter_context(ExitStack())
            self.psum = ctx.enter_context(nc.psum_tensor("psum", [P, 8, 512], F32))
            self.ident = ctx.enter_context(nc.sbuf_tensor("ident", [P, P], F32))
            self.eps = ctx.enter_context(nc.sbuf_tensor("eps", [P, 1], F32))
            self.colv = ctx.enter_context(nc.sbuf_tensor("colv", [P, 48], F32))
            self.weights = ctx.enter_context(nc.sbuf_tensor("route_w", [P, T, TOPK], F32))
            self.slots = ctx.enter_context(nc.sbuf_tensor("route_slot", [P, TOPK, T], I32))
            self.table = ctx.enter_context(nc.sbuf_tensor("step_table", [1, 2 * STEPS + 2], I32))
            dram = lambda n, s, d=F32: nc.dram_tensor(n, s, d, kind="Internal").ap()
            self.mod_d = dram("mod_d", (2, 6 * D))
            self.skew_d = dram("skew_d", (GRID_W, BROWS, BW))
            self.bias_d = dram("bias_d", (GRID_W, BROWS, GRID_W))
            self.mix_d = dram("mix_d", (SEQ, D))
            self.x1_d = dram("x1_d", (SEQ, D))
            self.h2_d = dram("h2_d", (SEQ, D))
            self.btab_d = dram("btab_d", (96, 2 * FF + D), BF16)
            self.slot_d = dram("slot_d", (SLOTS, 2), I32)
            self.y_d = dram("y_d", (TOPK * SEQ + P, D))
            with ExitStack() as until_middle:
                self.ring = until_middle.enter_context(nc.sbuf_tensor("ring", [P, 2, KD, UNIT], F32))
                with ExitStack() as until_attention:
                    qkv = lambda name, shape: until_attention.enter_context(nc.sbuf_tensor(name, shape, F32))
                    self.qa = qkv("qaT", [P, NHA // 2, SEQ])
                    self.ka = qkv("kaT", [P, SEQ + CTX])
                    self.qb = qkv("qbT", [P, NHB // 2, SEQ])
                    self.kb = qkv("kbT", [P, NHB // 2, SEQ + CTX])
                    self.v = qkv("v", [P, T + TC, NKVA * HD + NHB * HD])
                    front(self)
                    attention(self)
                middle(self)
            experts(self, 2, PAIR_AT, PAIR_COUNT, 0)
            experts(self, 1, SINGLE_AT, SINGLE_COUNT, PAIR_SLOTS)
            combine(self)


def scope(K, ctx):
    nc = K.nc
    sb = lambda name, shape, dt=F32: ctx.enter_context(nc.sbuf_tensor(name, shape, dt))
    sem = lambda name: K.semaphores.enter_context(nc.semaphore(name))
    return sb, sem


def linker(engine, sem, base=0):
    n = [0]

    def link(ins):
        n[0] += 1
        ins.then_inc(sem, 1)
        engine.wait_ge(sem, base + n[0])
    link.count = n
    return link


def front(K):
    nc, io, ps, ring = K.nc, K.io, K.psum, K.ring
    w_ada = io["w_ada"][0].rearrange("(k p) n -> p k n", p=P)
    w_in = io["w_in"][0].rearrange("(k p) n -> p k n", p=P)
    ctx = ExitStack()
    with ctx:
        sb, sem = scope(K, ctx)
        hT = sb("hT", [P, KD, SEQ + CTX])
        xin = sb("xin", [P, 2, D])
        modrow = sb("modrow", [2, 6 * D])
        cosT, sinT = sb("cosT", [P, SEQ]), sb("sinT", [P, SEQ])
        perm = sb("perm", [P, P])
        raw = sb("raw", [P, 2, UNIT])
        squares = raw[:, :, :].rearrange("p a n -> p (a n)")
        rot = sb("rot", [P, 2, UNIT])
        crow = sb("crow", [16, P])
        csig = sb("csig", [16, P])
        csilu = sb("csilu", [16, P])
        cT = sb("cT", [P, 16])
        modc = sb("modc", [48, P])
        aff = sb("aff", [P, 2, 2, KD])
        stat = sb("stat", [P, 2, 3])

        const_loaded, c_loaded, b_loaded = sem("const_loaded"), sem("c_loaded"), sem("b_loaded")
        mod_stored_late = sem("mod_stored_late")
        unit_loaded = [sem("unit_loaded0"), sem("unit_loaded1")]
        unit_used = sem("unit_used")
        x_loaded = [sem("x_loaded0"), sem("x_loaded1")]
        x_scaled, xt_done, ht_done = sem("x_scaled"), sem("xt_done"), sem("ht_done")
        ss_done, rms_done = sem("ss_done"), sem("rms_done")
        sig_done, silu_done, ct_done, ct_copied = sem("sig_done"), sem("silu_done"), sem("ct_done"), sem("ct_copied")
        ada_done, mod_done, mod_stored = sem("ada_done"), sem("mod_done"), sem("mod_stored")
        modc_loaded, modc_t, aff_done = sem("modc_loaded"), sem("modc_t"), sem("aff_done")
        group_done, group_copied = sem("group_done"), sem("group_copied")
        perm_done, rope_done = sem("perm_done"), sem("rope_done")
        eps_set, empty_stored, skew_zeroed, skew_stored = sem("eps_set"), sem("empty_stored"), sem("skew_zeroed"), sem("skew_stored")
        bias_stored, dve_own = sem("bias_stored"), sem("dve_own")

        ADA = 6 * D // UNIT
        units = [("ada", u) for u in range(ADA)] + [("in", u) for u in range(5)]
        EARLY = ADA - 4
        groups = []
        for u, tiles in enumerate([[("qa", j) for j in range(4)],
                                   [("ka", 0), ("va", 0), ("qb", 0), ("qb", 1)],
                                   [("qb", 2), ("qb", 3), ("kb", 0), ("kb", 1)],
                                   [("kb", 2), ("kb", 3), ("vb", 0)],
                                   [("vb", 1)]]):
            col = 0
            for kind, j in tiles:
                width = 2 * P if kind == "vb" else P
                if kind in ("va", "vb"):
                    groups += [(u, kind, j, col, tt, width) for tt in range(T + TC)]
                else:
                    groups += [(u, kind, j, col, hf, UNIT) for hf in range(2)]
                    if kind in ("ka", "kb"):
                        groups.append((u, kind, j, col, 2, CTX))
                col += width
        ropes = [g for g, x in enumerate(groups) if x[1] in ("qa", "ka") and x[4] < 2]

        block = ctx.enter_context(nc.Block())

        @block.sync
        def _(sp):
            sp.dma_start(crow[0:8, :], io["c"][0].rearrange("(k p) -> k p", p=P)).then_inc(c_loaded, 16)
            sp.dma_start(crow[8:16, :], io["c_ctx"].rearrange("(k p) -> k p", p=P)).then_inc(c_loaded, 16)
            sp.dma_start(K.ident[:, :], io["k_ident"]).then_inc(c_loaded, 16)

            def load_x(t):
                if t >= 2:
                    sp.wait_ge(xt_done, t - 1)
                src = io["x"][0][t * P:(t + 1) * P, :] if t < T else io["ctx"][0][(t - T) * P:(t - T + 1) * P, :]
                sp.dma_start(xin[:, t % 2, :], src).then_inc(x_loaded[t % 2], 16)

            load_x(0)
            load_x(1)
            for n, (kind, u) in enumerate(units):
                if n >= 2:
                    sp.wait_ge(unit_used, n - 1)
                src = w_ada if kind == "ada" else w_in
                cols = min(UNIT, src.shape[2] - u * UNIT)
                sp.dma_start(ring[:, n % 2, :, 0:cols], src[:, :, u * UNIT:u * UNIT + cols]).then_inc(unit_loaded[n % 2], 16)
                if n >= EARLY and 2 * (n - EARLY) + 3 < T + TC:
                    load_x(2 * (n - EARLY) + 2)
                    load_x(2 * (n - EARLY) + 3)
            sp.wait_ge(mod_done, ADA)
            sp.dma_start(K.mod_d[:, 2 * D:], modrow[:, 2 * D:]).then_inc(mod_stored_late, 16)
            sp.wait_ge(mod_stored_late, 16)
            sp.wait_ge(bias_stored, 16)

        @block.gpsimd
        def _(pool):
            pool.memset(K.eps[:, :], EPS).then_inc(eps_set, 1)
            for dst, src in ((perm[:, :], io["k_perm"]), (cosT[:, :], io["k_cos"]), (sinT[:, :], io["k_sin"])):
                pool.dma_start(dst, src).then_inc(const_loaded, 16)
            for r in range(2):
                pool.dma_start(modrow[r:r + 1, :], io["b_ada"]).then_inc(b_loaded, 16)
            for r, name in ((32, "g_pre_mix"), (40, "g_grp_a"), (44, "g_grp_b")):
                n = io[name].shape[1] // P
                pool.dma_start(modc[r:r + n, :], io[name][0].rearrange("(k p) -> k p", p=P)).then_inc(modc_loaded, 16)
            pool.dma_start(K.slot_d, io["k_empty"]).then_inc(empty_stored, 16)
            pool.dma_start(K.skew_d.rearrange("q n k -> q (n k)"), io["k_zeros"].to_broadcast([GRID_W, BROWS * BW])).then_inc(skew_zeroed, 16)
            pool.wait_ge(skew_zeroed, 16)
            rpb = raw_ap(io["rpb_b"], 0, [[0, GRID_W], [RPB_C, NHB * RPB_R], [1, RPB_C]])
            pool.dma_start(raw_ap(K.skew_d, 2 * BW, [[BROWS * BW + 1, GRID_W], [BW, NHB * RPB_R], [1, RPB_C]]), rpb).then_inc(skew_stored, 16)
            pool.wait_ge(skew_stored, 16)
            pool.dma_start(K.bias_d, K.skew_d[:, :, NA_COLS - 1:NA_COLS - 1 + GRID_W]).then_inc(bias_stored, 16)
            pool.wait_ge(empty_stored, 16)
            pool.wait_ge(mod_done, 4)
            pool.dma_start(K.mod_d[:, 0:2 * D], modrow[:, 0:2 * D]).then_inc(mod_stored, 16)
            pool.wait_ge(mod_stored, 16)
            for r in range(2):
                pool.dma_start(modc[16 * r:16 * r + 16, :], K.mod_d[r, 0:2 * D].rearrange("(n p) -> n p", p=P)).then_inc(modc_loaded, 16)
            pool.wait_ge(modc_loaded, 80)

        @block.scalar
        def _(act):
            act.wait_ge(c_loaded, 48)
            act.activation(csig[:, :], crow[:, :], ACT.Sigmoid).then_inc(sig_done, 1)
            act.wait_ge(eps_set, 1)
            for t in range(T + TC):
                act.wait_ge(x_loaded[t % 2], 16 * (t // 2 + 1))
                if t:
                    act.wait_ge(ss_done, t)
                if t >= 2:
                    act.wait_ge(x_scaled, t - 1)
                act.activation(squares, xin[:, t % 2, :], ACT.Square, accum_out=stat[:, t % 2, 0:1]).then_inc(ss_done, 1)
                act.wait_ge(ss_done, t + 1)
                act.activation(stat[:, t % 2, 1:2], stat[:, t % 2, 0:1], ACT.Sqrt, bias=K.eps[:, :], scale=1.0 / D).then_inc(rms_done, 1)
            rope = 0
            for g, (u, kind, j, col, part, width) in enumerate(groups):
                bank = g % 4
                act.wait_ge(group_done, g + 1)
                if kind in ("qa", "ka") and part < 2:
                    if rope >= 2:
                        act.wait_ge(rope_done, rope - 1)
                    act.activation(raw[:, rope % 2, :], ps[:, bank, :], ACT.Copy, scale=HD ** -0.5 if kind == "qa" else 1.0).then_inc(group_copied, 1)
                    rope += 1
                    continue
                if kind == "ka":
                    dst = K.ka[:, SEQ:]
                elif kind == "qb":
                    dst = K.qb[:, j, part * UNIT:part * UNIT + width]
                elif kind == "kb":
                    dst = K.kb[:, j, part * UNIT:part * UNIT + width]
                elif kind == "va":
                    dst = K.v[:, part, 0:P]
                else:
                    dst = K.v[:, part, P + j * width:P + (j + 1) * width]
                act.activation(dst, ps[:, bank, 0:width], ACT.Copy, scale=HD ** -0.5 if kind == "qb" else 1.0).then_inc(group_copied, 1)

        @block.vector
        def _(dve):
            link = linker(dve, dve_own)
            dve.wait_ge(sig_done, 1)
            dve.tensor_tensor(csilu[:, :], crow[:, :], csig[:, :], ALU.mult).then_inc(silu_done, 1)
            dve.wait_ge(ct_done, 1)
            dve.tensor_copy(cT[:, :], ps[:, 2, 0:16]).then_inc(ct_copied, 1)
            dve.wait_ge(b_loaded, 32)

            def ada(u):
                dve.wait_ge(ada_done, u + 1)
                row = modrow[0:2, u * UNIT:(u + 1) * UNIT]
                dve.tensor_tensor(row, ps[0:2, u % 2, :], row, ALU.add).then_inc(mod_done, 1)

            def scale(t):
                dve.wait_ge(rms_done, t + 1)
                link(dve.reciprocal(stat[:, t % 2, 2:3], stat[:, t % 2, 1:2]))
                dve.tensor_scalar(xin[:, t % 2, :], xin[:, t % 2, :], stat[:, t % 2, 2:3], None, ALU.mult).then_inc(x_scaled, 1)

            for u in range(4):
                ada(u)
            scale(0)
            scale(1)
            for u in range(4, EARLY):
                ada(u)
            dve.wait_ge(modc_t, 1)
            link(dve.tensor_copy(K.colv[:, :], ps[:, 2, 0:48]))
            for r in range(2):
                dve.scalar_tensor_tensor(aff[:, r, 0, :], K.colv[:, 16 * r + 8:16 * r + 16], 1.0, K.colv[:, 32:40], ALU.add, ALU.mult).then_inc(aff_done, 1)
                dve.tensor_copy(aff[:, r, 1, :], K.colv[:, 16 * r:16 * r + 8]).then_inc(aff_done, 1)
            dve.wait_ge(aff_done, 4)
            for t in range(T + TC):
                r = 0 if t < T else 1
                dve.wait_ge(xt_done, t + 1)
                for k in range(KD):
                    last = dve.tensor_scalar(hT[:, k, t * P:(t + 1) * P], ps[:, 4 + 2 * (t % 2) + k // 4, (k % 4) * P:(k % 4 + 1) * P],
                                             aff[:, r, 0, k:k + 1], aff[:, r, 1, k:k + 1], ALU.mult, ALU.add)
                last.then_inc(ht_done, 1)
                if t + 2 < T + TC:
                    scale(t + 2)
                if t % 2 and EARLY + t // 2 < ADA:
                    ada(EARLY + t // 2)
            dve.wait_ge(const_loaded, 48)
            for n, g in enumerate(ropes):
                _, kind, j, _, hf, _ = groups[g]
                cols = slice(hf * UNIT, (hf + 1) * UNIT)
                dve.wait_ge(group_copied, g + 1)
                link(dve.tensor_tensor(rot[:, 0, :], raw[:, n % 2, :], cosT[:, cols], ALU.mult))
                dve.wait_ge(perm_done, n + 1)
                link(dve.tensor_tensor(rot[:, 1, :], ps[:, 4 + n % 2, :], sinT[:, cols], ALU.mult))
                if kind == "qa":
                    for half in range(2):
                        head, src = 2 * j + half, slice(HD * half, HD * half + HD)
                        g0 = HD * (head // (NHA // NKVA))
                        last = dve.tensor_tensor(K.qa[g0:g0 + HD, head % 4, cols], rot[src, 0, :], rot[src, 1, :], ALU.add)
                else:
                    last = dve.tensor_tensor(K.ka[:, cols], rot[:, 0, :], rot[:, 1, :], ALU.add)
                last.then_inc(rope_done, 1)
                dve.wait_ge(rope_done, n + 1)

        @block.tensor
        def _(pe):
            pe.wait_ge(silu_done, 1)
            pe.wait_ge(const_loaded, 48)
            pe.wait_ge(c_loaded, 48)
            pe.transpose(ps[:, 2, 0:16], csilu[:, :], K.ident[0:16, 0:16]).then_inc(ct_done, 1)
            pe.wait_ge(ct_copied, 1)
            cols = cT[:, :].rearrange("p (v k) -> p k v", v=2)

            def ada(n, u):
                pe.wait_ge(unit_loaded[n % 2], 16 * (n // 2 + 1))
                if u >= 2:
                    pe.wait_ge(mod_done, u - 1)
                for k in range(KD):
                    last = pe.matmul(ps[0:2, u % 2, :], cols[:, k, :], ring[:, n % 2, k, :], start=(k == 0), stop=(k == KD - 1))
                last.then_inc(ada_done, 1)
                pe.wait_ge(ada_done, u + 1)
                pe.sem_inc(unit_used, 1)

            for n in range(EARLY):
                ada(n, units[n][1])
            pe.wait_ge(modc_loaded, 80)
            pe.transpose(ps[:, 2, 0:48], modc[:, :], K.ident[0:48, 0:48]).then_inc(modc_t, 1)
            for t in range(T + TC):
                pe.wait_ge(x_scaled, t + 1)
                if t >= 2:
                    pe.wait_ge(ht_done, t - 1)
                for k in range(KD):
                    last = pe.transpose(ps[:, 4 + 2 * (t % 2) + k // 4, (k % 4) * P:(k % 4 + 1) * P], xin[:, t % 2, k * P:(k + 1) * P], K.ident[:, :])
                last.then_inc(xt_done, 1)
                if t % 2 and EARLY + t // 2 < ADA:
                    ada(EARLY + t // 2, units[EARLY + t // 2][1])
            pe.wait_ge(ht_done, T + TC)
            pe.wait_ge(mod_done, ADA)
            pe.wait_ge(aff_done, 4)
            rope = 0

            def rotate(n, g):
                pe.wait_ge(group_copied, g + 1)
                if n >= 2:
                    pe.wait_ge(rope_done, n - 1)
                pe.matmul(ps[:, 4 + n % 2, :], perm[:, :], raw[:, n % 2, :], start=True, stop=True).then_inc(perm_done, 1)

            pending = None
            for g, (u, kind, j, col, part, width) in enumerate(groups):
                n = ADA + u
                slot = n % 2
                if g == 0 or groups[g - 1][0] != u:
                    pe.wait_ge(unit_loaded[slot], 16 * (n // 2 + 1))
                if g >= 4:
                    pe.wait_ge(group_copied, g - 3)
                for k in range(KD):
                    if kind in ("va", "vb"):
                        lhs, rhs = hT[:, k, part * P:(part + 1) * P], ring[:, slot, k, col:col + width]
                    else:
                        lhs, rhs = ring[:, slot, k, col:col + P], hT[:, k, part * UNIT:part * UNIT + width]
                    last = pe.matmul(ps[:, g % 4, 0:width], lhs, rhs, start=(k == 0), stop=(k == KD - 1))
                last.then_inc(group_done, 1)
                if g + 1 == len(groups) or groups[g + 1][0] != u:
                    pe.wait_ge(group_done, g + 1)
                    pe.sem_inc(unit_used, 1)
                if pending is not None:
                    rotate(*pending)
                    pending = None
                if g in ropes:
                    pending = (ropes.index(g), g)


def attention(K):
    nc, io, ps, ring = K.nc, K.io, K.psum, K.ring
    w_out = io["w_out"][0].rearrange("(k p) n -> p k n", p=P)
    ctx = ExitStack()
    with ctx:
        sb, sem = scope(K, ctx)
        qz = sb("qz", [P, NH, P])
        bias = sb("bias", [P, NHB, LB])
        mask_a, mask_b = sb("mask_a", [P, LA + CTX]), sb("mask_b", [P, LB])
        zeros = sb("zeros", [P, CTX])
        S = sb("S", [P, 2, LB + CTX])
        PT = sb("PT", [P, 2, 7 * P])
        o = sb("o", [P, 2, NHA * HD])
        squares = sb("squares", [P, NHA * HD])
        sink = sb("sink", [P, NHA])
        negm, den, sinkd, sinke, rden = sb("negm", [P, NH]), sb("den", [P, NH]), sb("sinkd", [P, NHA]), sb("sinke", [P, NHA]), sb("rden", [P, NH])
        mx = sb("mx", [P, NH, 2])
        stat = sb("stat2", [P, 2, 3])
        gate = sb("gate", [P, 1])
        tiles = sb("tiles", [1, (T + 1) * TCOLS], I32)

        tiles_loaded, sink_loaded, zeros_set = sem("tiles_loaded"), sem("sink_loaded"), sem("zeros_set")
        mask_a_loaded, bias_loaded = sem("mask_a_loaded"), sem("bias_loaded")
        mask_a_free, bias_free, o_free = sem("mask_a_free"), sem("bias_free"), sem("o_free")
        qa_free, qb_free, qa_ready, qb_ready, bias_ready = sem("qa_free"), sem("qb_free"), sem("qa_ready"), sem("qb_ready"), sem("bias_ready")
        s_done, s_masked, p_done, pt_done, pt_low, pt_high, pv_done = (sem(n) for n in ("s_done", "s_masked", "p_done", "pt_done", "pt_low", "pt_high", "pv_done"))
        sinkd_done, sinke_done, o_scaled, rms_done, o_done, o_stored = (sem(n) for n in ("sinkd_done", "sinke_done", "o_scaled", "rms2_done", "o_done", "o_stored"))
        dve_own, act_own = sem("dve_own2"), sem("act_own2")
        DVE_OWN, ACT_OWN = NH + 5, 2

        block = ctx.enter_context(nc.Block())

        @block.sync
        def _(sp):
            sp.dma_start(tiles[:, :], io["k_tiles"]).then_inc(tiles_loaded, 16)
            sp.wait_ge(tiles_loaded, 16)
            for n in range(2):
                sp.dma_start(ring[:, n, :, :], w_out[:, :, n * UNIT:(n + 1) * UNIT]).then_inc(tiles_loaded, 16)

            def store(i):
                sp.wait_ge(o_done, 2 * i + 3)
                sp.dma_start(K.mix_d[bass.ds(i * P, P), :], o[:, :, :].rearrange("p a n -> p (a n)")).then_inc(o_stored, 16)
                sp.wait_ge(o_stored, 16 * i + 16)
                sp.sem_inc(o_free, 1)

            def load(i):
                sp.wait_ge(mask_a_free, i + 1)
                sp.dma_start(mask_a[:, :], io["k_mask_a"][bass.ds(i, 1), :, :].rearrange("a p n -> (a p) n")).then_inc(mask_a_loaded, 16)
                first = [sp.value_load(tiles[0:1, bass.ds(i * TCOLS + 2 + half, 1)], min_val=0, max_val=BROWS - LBR - 15 * (NHB - 1)) for half in range(2)]
                sp.wait_ge(bias_free, i + 1)
                for half in range(2):
                    src = K.bias_d.rearrange("q n k -> q (n k)")
                    src = bass.AP(tensor=src.tensor, offset=first[half] * GRID_W, ap=[[BROWS * GRID_W, GRID_W], [RPB_R * GRID_W, NHB], [1, LB]])
                    sp.dma_start(bias[GRID_W * half:GRID_W * (half + 1), :, :], src).then_inc(bias_loaded, 16)
                sp.dma_start(mask_b[:, :], io["k_mask_b"][bass.ds(i, 1), :, :].rearrange("a p n -> (a p) n")).then_inc(bias_loaded, 16)

            load(0)
            with sp.Fori(0, T - 1) as i:
                load(i + 1)
                store(i)
            store(T - 1)
            sp.wait_ge(tiles_loaded, 48)

        @block.gpsimd
        def _(pool):
            pool.memset(zeros[:, :], 0.0).then_inc(zeros_set, 1)
            pool.memset(qz[:, :, :], 0.0).then_inc(zeros_set, 1)
            pool.dma_start(sink[:, :], io["sink_a"].to_broadcast([P, NHA])).then_inc(sink_loaded, 16)
            pool.wait_ge(zeros_set, 2)
            pool.wait_ge(tiles_loaded, 16)

            def queries(first, source, start, ready):
                for half in range(2):
                    part = slice(HD * half, HD * half + HD)
                    heads = slice(4 * half, 4 * half + 4) if first == 0 else slice(NHA + half, NH, 2)
                    last = pool.tensor_copy(qz[part, heads, :], source[part, :, bass.ds(start, P)])
                last.then_inc(ready, 1)

            queries(0, K.qa, 0, qa_ready)
            with pool.Fori(0, T) as i:
                next_start = pool.value_load(tiles[0:1, bass.ds(i * TCOLS + (2 * TCOLS - 1), 1)], min_val=0, max_val=SEQ - P)
                pool.wait_ge(qa_ready, i + 1)
                pool.wait_ge(qb_free, i + 1)
                queries(NHA, K.qb, i * P, qb_ready)
                pool.wait_ge(qb_ready, i + 1)
                pool.wait_ge(bias_loaded, 48 * i + 48)
                pool.tensor_tensor(bias[:, :, :], bias[:, :, :], mask_b[:, :].rearrange("p (a n) -> p a n", a=1).to_broadcast([P, NHB, LB]), ALU.add).then_inc(bias_ready, 1)
                pool.wait_ge(bias_ready, i + 1)
                pool.wait_ge(qa_free, i + 1)
                queries(0, K.qa, next_start, qa_ready)
            pool.wait_ge(sink_loaded, 16)

        def keys(s):
            return LA + CTX if s < NHA else LB + CTX

        @block.tensor
        def _(pe):
            pe.sem_inc(qb_free, 1)
            pe.wait_ge(tiles_loaded, 16)
            with pe.Fori(0, T) as i:
                k_a = pe.value_load(tiles[0:1, bass.ds(i * TCOLS, 1)], min_val=0, max_val=SEQ - LA)
                k_b = pe.value_load(tiles[0:1, bass.ds(i * TCOLS + 1, 1)], min_val=0, max_val=SEQ - LB)

                def scores(s):
                    if s >= 2:
                        pe.wait_ge(s_masked, i * NH + s - 1)
                    if s % NHA == 0:
                        pe.wait_ge(qb_ready if s else qa_ready, i + 1)
                    bank = 2 * (s % 2)
                    q = qz[:, s, :]
                    flat = ps[:, bank:bank + 2, :].rearrange("p b n -> p (b n)")
                    if s < NHA:
                        pe.matmul(flat[:, 128:512], q, K.ka[:, bass.ds(k_a, LA)], start=True, stop=True)
                        pe.matmul(flat[:, 512:768], q, K.ka[:, SEQ:], start=True, stop=True).then_inc(s_done, 1)
                    else:
                        kt = K.kb[:, (s - NHA) // 2, :]
                        pe.matmul(flat[:, 0:512], q, kt[:, bass.ds(k_b, 512)], start=True, stop=True)
                        pe.matmul(flat[:, 512:640], q, kt[:, bass.ds(k_b + 512, 128)], start=True, stop=True)
                        pe.matmul(flat[:, 640:896], q, kt[:, SEQ:], start=True, stop=True).then_inc(s_done, 1)

                def transposes(s):
                    if s >= 1:
                        pe.wait_ge(pt_low, i * NH + s)
                        pe.wait_ge(pt_high, i * NH + s)
                    pe.wait_ge(p_done, i * NH + s + 1)
                    for c in range(keys(s) // P):
                        last = pe.transpose(ps[:, 4 + c // 4, (c % 4) * P:(c % 4 + 1) * P], S[:, s % 2, c * P:(c + 1) * P], K.ident[:, :])
                    last.then_inc(pt_done, 1)

                def values(s):
                    pe.wait_ge(pt_low, i * NH + s + 1)
                    pe.wait_ge(pt_high, i * NH + s + 1)
                    if s % NHA == 0:
                        pe.wait_ge(o_scaled, 2 * i + 1 + s // NHA)
                    chunks = keys(s) // P
                    head = s % NHA
                    col = HD * (head // (NHA // NKVA)) if s < NHA else P + HD * head
                    local = chunks - TC
                    start = k_a if s < NHA else k_b
                    for c in range(chunks):
                        row = (start >> 7) + c if c < local else None
                        v = K.v[:, bass.ds(row, 1), col:col + HD].rearrange("p a n -> p (a n)") if c < local else K.v[:, T + c - local, col:col + HD]
                        last = pe.matmul(ps[:, 6 + s // NHA, head * HD:(head + 1) * HD], PT[:, s % 2, c * P:(c + 1) * P], v, start=(c == 0), stop=(c == chunks - 1))
                    last.then_inc(pv_done, 1)

                scores(0)
                for s in range(NH):
                    if s + 1 < NH:
                        scores(s + 1)
                    if s in (NHA, NH - 1):
                        pe.wait_ge(s_done, i * NH + s + 1)
                        pe.sem_inc(qa_free if s == NHA else qb_free, 1)
                    transposes(s)
                    if s >= 1:
                        values(s - 1)
                values(NH - 1)

        @block.scalar
        def _(act):
            act.sem_inc(rms_done, 2)
            with act.Fori(0, T) as i:
                link = linker(act, act_own, i * ACT_OWN)

                def probs(s):
                    act.wait_ge(s_masked, i * NH + s + 1)
                    act.activation(S[:, s % 2, 0:keys(s)], S[:, s % 2, 0:keys(s)], ACT.Exp, bias=negm[:, s:s + 1], accum_out=den[:, s:s + 1]).then_inc(p_done, 1)

                def evacuate(s):
                    act.wait_ge(pt_done, i * NH + s + 1)
                    if s >= 2:
                        act.wait_ge(pv_done, i * NH + s - 1)
                    act.activation(PT[:, s % 2, 0:512], ps[:, 4, :], ACT.Copy).then_inc(pt_low, 1)

                def rms(g):
                    act.wait_ge(o_scaled, 2 * i + g + 3)
                    link(act.activation(squares[:, :], o[:, g, :], ACT.Square, accum_out=stat[:, g, 0:1]))
                    act.activation(stat[:, g, 1:2], stat[:, g, 0:1], ACT.Sqrt, bias=K.eps[:, :], scale=1.0 / (NHA * HD)).then_inc(rms_done, 1)

                for s in range(NH):
                    probs(s)
                    if s >= 1:
                        evacuate(s - 1)
                    if s == NHA:
                        act.wait_ge(sinkd_done, i + 1)
                        act.activation(sinke[:, :], sinkd[:, :], ACT.Exp).then_inc(sinke_done, 1)
                    if s == NHA + 4:
                        rms(0)
                evacuate(NH - 1)
                rms(1)

        @block.vector
        def _(dve):
            dve.sem_inc(mask_a_free, 1)
            dve.sem_inc(bias_free, 1)
            dve.sem_inc(o_free, 1)
            dve.sem_inc(o_scaled, 2)
            dve.wait_ge(sink_loaded, 16)
            dve.wait_ge(zeros_set, 2)
            before = linker(dve, dve_own)
            before(dve.memset(o[:, 1, :], 0.0))
            before(dve.memset(stat[:, 1, 1:2], 1.0))

            def norm(i, g, link):
                dve.wait_ge(rms_done, 2 * i + g + 3)
                link(dve.reciprocal(stat[:, g, 2:3], stat[:, g, 1:2]))
                dve.tensor_scalar(o[:, g, :], o[:, g, :], stat[:, g, 2:3], None, ALU.mult).then_inc(o_done, 1)

            with dve.Fori(0, T) as i:
                link = linker(dve, dve_own, i * DVE_OWN + before.count[0])

                def mask(s):
                    dve.wait_ge(s_done, i * NH + s + 1)
                    if s >= 2:
                        dve.wait_ge(pt_done, i * NH + s - 1)
                    flat = ps[:, 2 * (s % 2):2 * (s % 2) + 2, :].rearrange("p b n -> p (b n)")
                    dve.memset(gate[:, :], 0.0)
                    if s < NHA:
                        link(dve.tensor_tensor_reduce(S[:, s % 2, 0:keys(s)], flat[:, 128:768], mask_a[:, :], 1.0, sink[:, s:s + 1], ALU.add, ALU.max, mx[:, s, 0:1]))
                        dve.tensor_scalar(negm[:, s:s + 1], mx[:, s, 0:1], -1.0, None, ALU.mult).then_inc(s_masked, 1)
                    else:
                        dve.tensor_tensor_reduce(S[:, s % 2, 0:LB], flat[:, 0:LB], bias[:, s - NHA, :], 1.0, NEG, ALU.add, ALU.max, mx[:, s, 0:1])
                        link(dve.tensor_tensor_reduce(S[:, s % 2, LB:LB + CTX], flat[:, LB:LB + CTX], zeros[:, :], 1.0, NEG, ALU.add, ALU.max, mx[:, s, 1:2]))
                        dve.tensor_scalar(negm[:, s:s + 1], mx[:, s, 0:1], mx[:, s, 1:2], -1.0, ALU.max, ALU.mult).then_inc(s_masked, 1)

                def evacuate(s):
                    dve.wait_ge(pt_done, i * NH + s + 1)
                    if s >= 2:
                        dve.wait_ge(pv_done, i * NH + s - 1)
                    dve.tensor_copy(PT[:, s % 2, 512:keys(s)], ps[:, 5, 0:keys(s) - 512]).then_inc(pt_high, 1)

                def output(g):
                    heads = slice(g * NHA, (g + 1) * NHA)
                    if g == 0:
                        dve.wait_ge(sinke_done, i + 1)
                        link(dve.tensor_tensor(den[:, heads], den[:, heads], sinke[:, :], ALU.add))
                        dve.wait_ge(o_free, i + 1)
                    link(dve.reciprocal(rden[:, heads], den[:, heads]))
                    dve.wait_ge(pv_done, i * NH + (g + 1) * NHA)
                    r = rden[:, heads].rearrange("p (h a) -> p h a", a=1).to_broadcast([P, NHA, HD])
                    dve.tensor_tensor(o[:, g, :].rearrange("p (h d) -> p h d", h=NHA), ps[:, 6 + g, :].rearrange("p (h d) -> p h d", h=NHA), r, ALU.mult).then_inc(o_scaled, 1)


                dve.wait_ge(mask_a_loaded, 16 * i + 16)
                for s in range(NH):
                    if s == NHA:
                        dve.sem_inc(mask_a_free, 1)
                        dve.wait_ge(p_done, i * NH + NHA)
                        dve.tensor_tensor(sinkd[:, :], sink[:, :], negm[:, 0:NHA], ALU.add).then_inc(sinkd_done, 1)
                        dve.wait_ge(bias_ready, i + 1)
                    mask(s)
                    if s == 1:
                        norm(i - 1, 1, link)
                    if s >= 1:
                        evacuate(s - 1)
                    if s == NHA + 2:
                        output(0)
                    if s == NHA + 5:
                        norm(i, 0, link)
                dve.sem_inc(bias_free, 1)
                evacuate(NH - 1)
                dve.wait_ge(p_done, i * NH + NH)
                output(1)
                assert link.count[0] == DVE_OWN, link.count
            norm(T - 1, 1, linker(dve, dve_own, T * DVE_OWN + before.count[0]))


def middle(K):
    nc, io, ps, ring = K.nc, K.io, K.psum, K.ring
    ctx = ExitStack()
    with ctx:
        sb, sem = scope(K, ctx)
        mix, xin = sb("mix", [P, 2, D]), sb("xres", [P, 2, D])
        mixT, h2T = sb("mixT", [P, KD, P]), sb("h2T", [P, KD, P])
        mixT2, h2T2 = sb("mixT2", [P, KD, P]), sb("h2T2", [P, KD, P])
        x1, h2 = sb("x1", [P, 2, D]), sb("h2", [P, 2, D])
        squares = sb("squares3", [P, D])
        gate1, scale2, shift2, gain = sb("gate1", [P, D]), sb("scale2", [P, D]), sb("shift2", [P, D]), sb("gain", [P, 2, D])
        w_router, b_router = sb("w_router", [P, KD, E]), sb("b_router", [P, E])
        stat = sb("stat3", [P, T, 6])
        tri, iota, ones = sb("tri", [P, P]), sb("iota", [P, P]), sb("ones", [P, P])
        record = sb("record", [P, TOPK, T, 2], I32)
        logit = sb("logit", [P, T, E])
        top, topi, topf = sb("top", [P, T, 8]), sb("topi", [P, T, 8], U32), sb("topf", [P, T, 8])
        pick = sb("pick", [P, TOPK, T, E])
        chosen, before = sb("chosen", [P, T, E]), sb("before", [P, T + 1, E])
        base, prod = sb("base", [P, T, E]), sb("prod", [P, T, E])
        nsteps, over = sb("nsteps", [P, 2, E]), sb("over", [P, 2, E])
        scan = sb("scan", [P, 2, 2, E])
        start, count = sb("start", [P, 2, E]), sb("count", [P, E])
        shifted = sb("shifted", [P, T, E])
        braw, brest, bpart = sb("braw", [96, 2 * FF + D]), sb("brest", [96, 2 * FF + D]), sb("bpart", [96, 2 * FF + D], BF16)
        slotf = sb("slotf", [P, TOPK, T])
        expd, exps, norm = sb("expd", [P, T, TOPK]), sb("exps", [P, T, TOPK]), sb("norm", [P, T, 2])
        cmp, tabf = sb("cmp", [1, STEPS, E]), sb("tabf", [1, 2, STEPS])

        btab = sb("btab", [96, 2 * FF + D], BF16)
        btab_done, btab_stored = sem("btab_done"), sem("btab_stored")
        rows_loaded, tabs_loaded, ones_set = sem("rows_loaded"), sem("tabs_loaded"), sem("ones_set")
        mix_loaded = [sem("mix_loaded0"), sem("mix_loaded1")]
        xr_loaded = [sem("xr_loaded0"), sem("xr_loaded1")]
        stored = [sem("stored0"), sem("stored1")]
        mt_done, mt_copied, proj_done, x1_done, h2_done, h2_shifted = (sem(n) for n in ("mt_done", "mt_copied", "proj_done", "x1_done", "h2_done", "h2_shifted"))
        h2t_done, h2t_copied, logit_done, rms1_done, rms2_done = (sem(n) for n in ("h2t_done", "h2t_copied", "logit_done", "rms1_done", "rms2b_done"))
        chosen_done, pos_done, expd_done, exps_done, slots_done, scattered = (sem(n) for n in ("chosen_done", "pos_done", "expd_done", "exps_done", "slots_done", "scattered"))
        dve_own, act_own = sem("dve_own3"), sem("act_own3")
        TABS = 5 + 2 * 3
        mts, h2ts = [mixT, mixT2], [h2T, h2T2]

        block = ctx.enter_context(nc.Block())

        @block.sync
        def _(sp):
            def load(t):
                if t >= 2:
                    sp.wait_ge(mt_done, t - 1)
                    sp.wait_ge(x1_done, t - 1)
                sp.dma_start(mix[:, t % 2, :], K.mix_d[t * P:(t + 1) * P, :]).then_inc(mix_loaded[t % 2], 16)
                sp.dma_start(xin[:, t % 2, :], io["x"][0][t * P:(t + 1) * P, :]).then_inc(xr_loaded[t % 2], 16)

            for t in range(T):
                load(t)
            sp.wait_ge(btab_done, 3)
            sp.dma_start(K.btab_d, btab[:, :]).then_inc(btab_stored, 16)
            sp.wait_ge(btab_stored, 16)

        @block.gpsimd
        def _(pool):
            pool.memset(ones[:, :], 1.0).then_inc(ones_set, 1)
            for dst, src in ((gate1, K.mod_d[0:1, 2 * D:3 * D]), (shift2, K.mod_d[0:1, 3 * D:4 * D]), (scale2, K.mod_d[0:1, 4 * D:5 * D])):
                pool.dma_start(dst[:, :], src.to_broadcast([P, D])).then_inc(rows_loaded, 16)
            pool.dma_start(gain[:, 0, :], io["g_post_mix"].to_broadcast([P, D])).then_inc(rows_loaded, 16)
            pool.dma_start(gain[:, 1, :], io["g_pre_ffn"].to_broadcast([P, D])).then_inc(rows_loaded, 16)
            pool.dma_start(w_router[:, :, :], io["w_router"][0].rearrange("(k p) n -> p k n", p=P)).then_inc(tabs_loaded, 16)
            pool.dma_start(b_router[:, :], io["b_router"].to_broadcast([P, E])).then_inc(tabs_loaded, 16)
            pool.dma_start(tri[:, :], io["k_tri"]).then_inc(tabs_loaded, 16)
            pool.dma_start(iota[:, :], io["k_iota"]).then_inc(tabs_loaded, 16)
            pool.dma_start(record[:, :, :, :].rearrange("p k t a -> p (k t a)"), io["k_record"]).then_inc(tabs_loaded, 16)
            for part in range(3):
                rows = slice(E * part, E * part + E)
                pool.dma_start(braw[rows, 0:2 * FF], io["b_mlp1"][0]).then_inc(tabs_loaded, 16)
                pool.dma_start(braw[rows, 2 * FF:], io["b_mlp2"][0]).then_inc(tabs_loaded, 16)
            pool.wait_ge(rows_loaded, 80)
            for t in range(T):
                pool.wait_ge(h2_done, t + 1)
                pool.tensor_tensor(h2[:, t % 2, :], h2[:, t % 2, :], shift2[:, :], ALU.add).then_inc(h2_shifted, 1)
                pool.dma_start(K.x1_d[t * P:(t + 1) * P, :], x1[:, t % 2, :]).then_inc(stored[t % 2], 16)
                pool.wait_ge(h2_shifted, t + 1)
                pool.dma_start(K.h2_d[t * P:(t + 1) * P, :], h2[:, t % 2, :]).then_inc(stored[t % 2], 16)
            pool.wait_ge(tabs_loaded, 16 * TABS)
            for s in range(2):
                pool.wait_ge(stored[s], 32 * (T // 2))
            pool.wait_ge(slots_done, 1)
            for k in range(TOPK):
                for t in range(T):
                    pool.indirect_dma_start(K.slot_d, bass.IndirectOffsetOnAxis(ap=K.slots[:, k, t:t + 1], axis=0), record[:, k, t, :], None).then_inc(scattered, 16)
            pool.wait_ge(scattered, 16 * TOPK * T)

        @block.tensor
        def _(pe):
            def to_columns(t):
                pe.wait_ge(mix_loaded[t % 2], 16 * (t // 2 + 1))
                if t:
                    pe.wait_ge(mt_copied, t)
                if t >= 3:
                    pe.wait_ge(h2t_copied, t - 2)
                for k in range(KD):
                    last = pe.transpose(ps[:, k // 4, (k % 4) * P:(k % 4 + 1) * P], mix[:, t % 2, k * P:(k + 1) * P], K.ident[:, :])
                last.then_inc(mt_done, 1)

            def project(t):
                pe.wait_ge(mt_copied, t + 1)
                if t >= 2:
                    pe.wait_ge(x1_done, t - 1)
                for n in range(2):
                    for k in range(KD):
                        last = pe.matmul(ps[:, 2 + 2 * (t % 2) + n, :], mts[t % 2][:, k, :], ring[:, n, k, :], start=(k == 0), stop=(k == KD - 1))
                last.then_inc(proj_done, 1)

            def route(t):
                pe.wait_ge(h2_shifted, t + 1)
                pe.wait_ge(mt_copied, min(t + 3, T))
                for k in range(KD):
                    last = pe.transpose(ps[:, k // 4, (k % 4) * P:(k % 4 + 1) * P], h2[:, t % 2, k * P:(k + 1) * P], K.ident[:, :])
                last.then_inc(h2t_done, 1)
                pe.wait_ge(h2t_copied, t + 1)
                for k in range(KD):
                    last = pe.matmul(ps[:, 6, t * E:(t + 1) * E], h2ts[t % 2][:, k, :], w_router[:, k, :], start=(k == 0), stop=(k == KD - 1))
                last.then_inc(logit_done, 1)

            to_columns(0)
            to_columns(1)
            project(0)
            pe.wait_ge(tabs_loaded, 16 * TABS)
            for t in range(T):
                if t + 2 < T:
                    to_columns(t + 2)
                if t + 1 < T:
                    project(t + 1)
                route(t)
            pe.wait_ge(ones_set, 1)
            pe.wait_ge(chosen_done, 1)
            flat = lambda x: x.rearrange("p t e -> p (t e)")
            pe.matmul(ps[:, 7, 0:T * E], tri[:, :], flat(chosen[:, :, :]), start=True, stop=False)
            pe.matmul(ps[:, 7, 0:T * E], ones[:, :], flat(before[:, 0:T, :]), start=False, stop=True)
            pe.matmul(ps[:, 7, T * E:(T + 1) * E], ones[:, :], before[:, T, :], start=True, stop=True).then_inc(pos_done, 1)

        @block.scalar
        def _(act):
            link = linker(act, act_own)

            def copy_h2(t):
                act.wait_ge(h2t_done, t + 1)
                if t >= 2:
                    act.wait_ge(logit_done, t - 1)
                act.activation(h2ts[t % 2][:, :, :].rearrange("p k n -> p (k n)"), ps[:, 0:2, :].rearrange("p b n -> p (b n)"), ACT.Copy).then_inc(h2t_copied, 1)

            for t in range(T):
                act.wait_ge(proj_done, t + 1)
                bank = 2 + 2 * (t % 2)
                link(act.activation(squares[:, :], ps[:, bank:bank + 2, :].rearrange("p b n -> p (b n)"), ACT.Square, accum_out=stat[:, t, 0:1]))
                act.activation(stat[:, t, 1:2], stat[:, t, 0:1], ACT.Sqrt, bias=K.eps[:, :], scale=1.0 / D).then_inc(rms1_done, 1)
                if t:
                    copy_h2(t - 1)
                act.wait_ge(x1_done, t + 1)
                link(act.activation(squares[:, :], x1[:, t % 2, :], ACT.Square, accum_out=stat[:, t, 3:4]))
                act.activation(stat[:, t, 4:5], stat[:, t, 3:4], ACT.Sqrt, bias=K.eps[:, :], scale=1.0 / D).then_inc(rms2_done, 1)
            copy_h2(T - 1)
            act.wait_ge(expd_done, 1)
            act.activation(exps[:, :, :], expd[:, :, :], ACT.Exp).then_inc(exps_done, 1)

        @block.vector
        def _(dve):
            link = linker(dve, dve_own)
            dve.wait_ge(rows_loaded, 80)
            link(dve.tensor_tensor(gate1[:, :], gate1[:, :], gain[:, 0, :], ALU.mult))
            link(dve.scalar_tensor_tensor(scale2[:, :], scale2[:, :], 1.0, gain[:, 1, :], ALU.add, ALU.mult))

            def copy_mix(t):
                dve.wait_ge(mt_done, t + 1)
                if t >= 2:
                    dve.wait_ge(proj_done, t - 1)
                for k in range(KD):
                    last = dve.tensor_scalar(mts[t % 2][:, k, :], ps[:, k // 4, (k % 4) * P:(k % 4 + 1) * P], K.colv[:, 40 + k:41 + k], None, ALU.mult)
                last.then_inc(mt_copied, 1)

            copy_mix(0)
            for t in range(T):
                if t + 1 < T:
                    copy_mix(t + 1)
                s = t % 2
                dve.wait_ge(rms1_done, t + 1)
                link(dve.reciprocal(stat[:, t, 2:3], stat[:, t, 1:2]))
                if t >= 2:
                    dve.wait_ge(stored[s], 32 * (t // 2))
                    dve.wait_ge(h2t_done, t - 1)
                link(dve.scalar_tensor_tensor(x1[:, s, :], ps[:, 2 + 2 * s:4 + 2 * s, :].rearrange("p b n -> p (b n)"), stat[:, t, 2:3], gate1[:, :], ALU.mult, ALU.mult))
                dve.wait_ge(xr_loaded[s], 16 * (t // 2 + 1))
                dve.tensor_tensor(x1[:, s, :], x1[:, s, :], xin[:, s, :], ALU.add).then_inc(x1_done, 1)
                dve.wait_ge(rms2_done, t + 1)
                link(dve.reciprocal(stat[:, t, 5:6], stat[:, t, 4:5]))
                dve.scalar_tensor_tensor(h2[:, s, :], x1[:, s, :], stat[:, t, 5:6], scale2[:, :], ALU.mult, ALU.mult).then_inc(h2_done, 1)
            dve.wait_ge(logit_done, T)
            dve.wait_ge(tabs_loaded, 16 * TABS)
            row = lambda x: x.rearrange("p (a n) -> p a n", a=1)
            link(dve.tensor_tensor(logit[:, :, :], ps[:, 6, 0:T * E].rearrange("p (t e) -> p t e", e=E), row(b_router[:, :]).to_broadcast([P, T, E]), ALU.add))
            for t in range(T):
                last = dve.max(top[:, t, :], logit[:, t, :])
            link(last)
            dve.tensor_tensor(expd[:, :, :], top[:, :, 0:TOPK], top[:, :, 0:1].to_broadcast([P, T, TOPK]), ALU.subtract).then_inc(expd_done, 1)
            for t in range(T):
                last = dve.max_index(topi[:, t, :], top[:, t, :], logit[:, t, :])
            link(last)
            link(dve.tensor_copy(topf[:, :, :], topi[:, :, :]))
            for k in range(TOPK):
                last = dve.tensor_tensor(pick[:, k, :, :], row(iota[:, 0:E]).to_broadcast([P, T, E]), topf[:, :, k:k + 1].to_broadcast([P, T, E]), ALU.is_equal)
            link(last)
            link(dve.tensor_tensor(base[:, :, :], pick[:, 0, :, :], pick[:, 1, :, :], ALU.add))
            link(dve.tensor_tensor(prod[:, :, :], pick[:, 2, :, :], pick[:, 3, :, :], ALU.add))
            link(dve.tensor_tensor(chosen[:, :, :], base[:, :, :], prod[:, :, :], ALU.add))
            link(dve.memset(before[:, 0, :], 0.0))
            for t in range(T):
                ins = dve.tensor_tensor(before[:, t + 1, :], before[:, t, :], chosen[:, t, :], ALU.add)
                if t + 1 < T:
                    link(ins)
            ins.then_inc(chosen_done, 1)
            dve.wait_ge(exps_done, 1)
            link(dve.tensor_reduce(norm[:, :, 0:1], exps[:, :, :], AX.X, ALU.add))
            link(dve.reciprocal(norm[:, :, 1:2], norm[:, :, 0:1]))
            link(dve.tensor_tensor(K.weights[:, :, :], exps[:, :, :], norm[:, :, 1:2].to_broadcast([P, T, TOPK]), ALU.mult))
            dve.wait_ge(pos_done, 1)
            link(dve.tensor_copy(count[:, :], ps[:, 7, T * E:(T + 1) * E]))
            link(dve.tensor_scalar(over[:, 0, :], count[:, :], 0.0, None, ALU.is_gt))
            for m in range(1, SEQ // P):
                link(dve.scalar_tensor_tensor(over[:, m % 2, :], count[:, :], float(P * m), over[:, (m - 1) % 2, :], ALU.is_gt, ALU.add))
            blocks = over[:, (SEQ // P - 1) % 2, :]
            for m in range(0, SEQ // (2 * P)):
                if m == 0:
                    link(dve.tensor_scalar(nsteps[:, m % 2, :], count[:, :], float(P), None, ALU.is_gt))
                else:
                    link(dve.scalar_tensor_tensor(nsteps[:, m % 2, :], count[:, :], float(P * (2 * m + 1)), nsteps[:, (m - 1) % 2, :], ALU.is_gt, ALU.add))
            link(dve.tensor_copy(nsteps[:, 0, :], nsteps[:, 1, :]))
            link(dve.scalar_tensor_tensor(nsteps[:, 1, :], nsteps[:, 0, :], -2.0, blocks, ALU.mult, ALU.add))
            link(dve.tensor_copy(scan[:, 0, :, :], nsteps[:, :, :]))
            cur = 0
            for shift in (1, 2, 4, 8, 16):
                link(dve.tensor_copy(scan[:, 1 - cur, :, 0:shift], scan[:, cur, :, 0:shift]))
                link(dve.tensor_tensor(scan[:, 1 - cur, :, shift:], scan[:, cur, :, shift:], scan[:, cur, :, 0:E - shift], ALU.add))
                cur = 1 - cur
            ends = scan[:, cur, :, :]
            link(dve.tensor_tensor(start[:, :, :], ends, nsteps[:, :, :], ALU.subtract))
            rank = ps[:, 7, 0:T * E].rearrange("p (t e) -> p t e", e=E)
            wide = lambda x: row(x).to_broadcast([P, T, E])
            link(dve.scalar_tensor_tensor(base[:, :, :], wide(start[:, 0, :]), float(2 * P), rank, ALU.mult, ALU.add))
            link(dve.tensor_scalar(start[:, 1, :], start[:, 1, :], float(P), float(PAIR_SLOTS), ALU.mult, ALU.add))
            link(dve.scalar_tensor_tensor(start[:, 1, :], scan[:, cur, 0, :], -2.0 * P, start[:, 1, :], ALU.mult, ALU.add))
            link(dve.scalar_tensor_tensor(shifted[:, :, :], wide(nsteps[:, 0, :]), float(2 * P), rank, ALU.mult, ALU.is_le))
            link(dve.tensor_tensor(shifted[:, :, :], shifted[:, :, :], wide(start[:, 1, :]), ALU.mult))
            link(dve.tensor_tensor(base[:, :, :], base[:, :, :], shifted[:, :, :], ALU.add))
            for k in range(TOPK):
                link(dve.tensor_tensor(prod[:, :, :], pick[:, k, :, :], base[:, :, :], ALU.mult))
                link(dve.tensor_reduce(slotf[:, k, :], prod[:, :, :], AX.X, ALU.add))
            dve.tensor_copy(K.slots[:, :, :], slotf[:, :, :]).then_inc(slots_done, 1)
            for kind, at in ((0, PAIR_AT), (1, SINGLE_AT)):
                link(dve.tensor_tensor(cmp[:, :, :], row(scan[0:1, cur, kind, :]).to_broadcast([1, STEPS, E]), iota[0:1, 0:STEPS].rearrange("p (n a) -> p n a", a=1).to_broadcast([1, STEPS, E]), ALU.is_le))
                link(dve.tensor_reduce(tabf[:, 0, :], cmp[:, :, :], AX.X, ALU.add))
                link(dve.tensor_scalar(tabf[:, 1, :], tabf[:, 0, :], float(E - 1), None, ALU.min))
                link(dve.tensor_copy(K.table[:, at:at + STEPS], tabf[:, 1, :]))
            dve.tensor_copy(K.table[:, PAIR_COUNT:SINGLE_COUNT + 1], scan[0:1, cur, :, E - 1])
            src = braw
            for part in range(3):
                rows = slice(E * part, E * part + E)
                link(dve.tensor_copy(bpart[:, :], src[:, :]))
                dve.tensor_copy(btab[rows, :], bpart[rows, :]).then_inc(btab_done, 1)
                if part < 2:
                    link(dve.tensor_tensor(brest[:, :], src[:, :], bpart[:, :], ALU.subtract))
                    src = brest
                    dve.wait_ge(btab_done, part + 1)


def experts(K, R, steps_at, count_at, slot_base):
    nc, io, ps = K.nc, K.io, K.psum
    w1 = io["w_mlp1"][0].rearrange("e (k p) n -> e p k n", p=P)
    w2 = io["w_mlp2"][0].rearrange("e (k p) n -> e p k n", p=P)
    UP, DOWN = 2 * FF // UNIT, D // UNIT
    NU, RING, CH = UP + DOWN, 3, 2
    HI, LO = 3, 2
    PAIRS = UNIT // 2
    KC = KD // CH
    KP = KD - 1
    UPS, DOWNS = UP * R, DOWN * R
    ctx = ExitStack()
    with ctx:
        sb = lambda name, shape, dt=F32: ctx.enter_context(nc.sbuf_tensor(f"{name}_{R}", shape, dt))
        sem = lambda name: K.semaphores.enter_context(nc.semaphore(f"{name}_{R}"))
        ring = sb("wring", [P, RING, KD, UNIT])
        w_hi, w_lo = sb("w_hi", [P, HI, KD, UNIT], F32R), sb("w_lo", [P, LO, KD, UNIT], F32R)
        xg = sb("xg", [P, R, D])
        x_hi, x_lo = sb("x_hi", [P, R, KD, P], F32R), sb("x_lo", [P, R, KD, P], F32R)
        a_hi, a_lo = sb("a_hi", [P, R, KD, P], F32R), sb("a_lo", [P, R, KD, P], F32R)
        glu, lin, sig, act_o = (sb(n, [P, 2, PAIRS]) for n in ("glu", "lin", "sig", "act_o"))
        y = sb("y", [P, R, D])
        record, y_row, int_zero = sb("record", [P, R, 2], I32), sb("y_row", [P, R], I32), sb("int_zero", [P, R], I32)
        poolgate = sb("poolgate", [P, 2])
        onehot = sb("onehot", [96, E])
        btab = sb("btab", [96, 2 * FF + D], BF16)
        sel_up, sel_down = sb("sel_up", [96, P], BF16), sb("sel_down", [96, P], BF16)

        bias_loaded = sem("bias_loaded")
        w_loaded = [sem(f"w_loaded{r}") for r in range(RING)]
        hi_done, lo_done, pool_lo_done, prod_done = sem("hi_done"), sem("lo_done"), sem("pool_lo_done"), sem("prod_done")
        record_loaded, gathered, gate_open = sem("record_loaded"), sem("gathered"), sem("gate_open")
        xt_done, xhi_done, x_ready = sem("xt_done"), sem("xhi_done"), sem("x_ready")
        sel_up_ready, sel_down_ready = sem("sel_up_ready"), sem("sel_down_ready")
        glu_done, sig_done, up_free, act_done = sem("glu_done"), sem("sig_done"), sem("up_free"), sem("act_done")
        at_done, ahi_done, a_ready = sem("at_done"), sem("ahi_done"), sem("a_ready")
        y_copied, y_stored, y_free = sem("y_copied"), sem("y_stored"), sem("y_free")
        dve_own = sem("dve_own")

        block = ctx.enter_context(nc.Block())

        def step_count(engine):
            return engine.value_load(K.table[0:1, count_at:count_at + 1], min_val=0, max_val=E)

        def expert_of(engine, step):
            at = slice(steps_at, steps_at + 1) if isinstance(step, int) else bass.ds(step + steps_at, 1)
            return engine.value_load(K.table[0:1, at], min_val=0, max_val=E - 1)

        def wait_loaded(engine, b, n):
            engine.wait_ge(w_loaded[n % RING], 16 * ((NU // RING) * b + n // RING + 1))

        def wait_product(engine, b, n, r):
            engine.wait_ge(prod_done, R * (NU * b + n) + 2 * R + r + 1)

        @block.sync
        def _(sp):
            def load(b, n, e):
                split_before = CH * (NU * b + n) + CH
                if not isinstance(b, int):
                    split_before = sp.snap(split_before)
                sp.wait_ge(lo_done, split_before)
                sp.wait_ge(pool_lo_done, split_before)
                src = w1[bass.ds(e, 1), :, :, n * UNIT:(n + 1) * UNIT] if n < UP else w2[bass.ds(e, 1), :, :, (n - UP) * UNIT:(n - UP + 1) * UNIT]
                sp.dma_start(ring[:, n % RING, :, :], src.rearrange("a p k n -> (a p) k n")).then_inc(w_loaded[n % RING], 16)

            steps = step_count(sp)
            first = expert_of(sp, 0)
            load(0, 0, first)
            sp.wait_ge(gathered, 16 * R)
            load(0, 1, first)
            with sp.Fori(0, steps) as b:
                e, e_next = expert_of(sp, b), expert_of(sp, b + 1)
                for n in range(2, NU):
                    load(b, n, e)
                load(b + 1, 0, e_next)
                load(b + 1, 1, e_next)

        @block.gpsimd
        def _(pool):
            def gather():
                for r in range(R):
                    pool.indirect_dma_start(xg[:, r, :], None, K.h2_d, bass.IndirectOffsetOnAxis(ap=record[:, r, 0:1], axis=0)).then_inc(gathered, 16)

            pool.dma_start(record[:, :, :], K.slot_d[slot_base:slot_base + R * P, :].rearrange("(r p) a -> p r a", p=P)).then_inc(record_loaded, 16)
            pool.wait_ge(record_loaded, 16)
            gather()
            pool.sem_inc(y_free, 1)
            pool.memset(int_zero[:, :], 0).then_inc(gate_open, 1)
            pool.wait_ge(gate_open, 1)
            pool.memset(poolgate[:, :], 0.0).then_inc(gate_open, 1)
            pool.dma_start(onehot[:, :], io["k_onehot"]).then_inc(bias_loaded, 16)
            pool.dma_start(btab[:, :], K.btab_d).then_inc(bias_loaded, 16)
            pool.wait_ge(gate_open, 2)
            steps = step_count(pool)

            def gate():
                pool.tensor_tensor(poolgate[:, 1:2], poolgate[:, 0:1], poolgate[:, 0:1], ALU.add).then_inc(gate_open, 1)

            def split(b, n):
                pool.wait_ge(prod_done, R * (NU * b + n) + R)
                pool.wait_ge(hi_done, CH * (NU * b + n) + CH)
                pool.tensor_tensor(w_lo[:, n % LO, KP:, :], ring[:, n % RING, KP:, :], w_hi[:, n % HI, KP:, :].bitcast(F32), ALU.subtract).then_inc(pool_lo_done, CH)

            pool.sem_inc(pool_lo_done, RING * CH)
            pool.wait_ge(gathered, 16 * R)
            split(0, 0)
            split(0, 1)
            with pool.Fori(0, steps) as b:
                pool.wait_ge(gate_open, 3 * b + 2)
                pool.tensor_tensor(y_row[:, :], record[:, :, 1], int_zero[:, :], ALU.add).then_inc(gate_open, 1)
                pool.wait_ge(gate_open, 3 * b + 3)
                pool.dma_start(record[:, :, :], K.slot_d[bass.ds(b * (R * P) + (slot_base + R * P), R * P), :].rearrange("(r p) a -> p r a", p=P)).then_inc(record_loaded, 16)
                split(b, 2)
                pool.wait_ge(record_loaded, 16 * b + 32)
                pool.wait_ge(xt_done, R * b + R)
                gate()
                gather()
                for n in range(3, NU):
                    split(b, n)
                split(b + 1, 0)
                pool.wait_ge(gathered, 16 * R * b + 32 * R)
                pool.wait_ge(gate_open, 3 * b + 4)
                pool.wait_ge(y_copied, DOWNS * b + DOWNS + 2)
                gate()
                for r in range(R):
                    pool.indirect_dma_start(K.y_d, bass.IndirectOffsetOnAxis(ap=y_row[:, r:r + 1], axis=0), y[:, r, :], None).then_inc(y_stored, 16)
                split(b + 1, 1)
                pool.wait_ge(y_stored, 16 * R * b + 16 * R)
                pool.sem_inc(y_free, 1)
            pool.wait_ge(bias_loaded, 32)

        @block.scalar
        def _(act):
            act.sem_inc(y_copied, 2)

            def split(b, n):
                wait_loaded(act, b, n)
                if not isinstance(b, int):
                    act.wait_ge(prod_done, R * (NU * b + n))
                for c in range(CH):
                    k = slice(KC * c, KC * (c + 1))
                    act.activation(w_hi[:, n % HI, k, :], ring[:, n % RING, k, :], ACT.Copy).then_inc(hi_done, 1)

            def rows(b, r):
                act.wait_ge(xt_done, R * b + r + 1)
                act.activation(x_hi[:, r, :, :].rearrange("p k n -> p (k n)"), ps[:, 6:8, :].rearrange("p b n -> p (b n)"), ACT.Copy).then_inc(xhi_done, 1)

            def columns(b, j):
                act.wait_ge(at_done, UPS * b + j + 1)
                n, r = divmod(j, R)
                act.activation(a_hi[:, r, 2 * n:2 * n + 2, :].rearrange("p k n -> p (k n)"), ps[:, 2 + j % 2, 0:2 * P], ACT.Copy).then_inc(ahi_done, 1)

            steps = step_count(act)
            for r in range(R):
                rows(0, r)
            split(0, 0)
            split(0, 1)
            with act.Fori(0, steps) as b:
                for n in range(NU):
                    if n == UP:
                        columns(b, UPS - 1)
                    split(b + (n + 2) // NU, (n + 2) % NU)
                    if n < UP:
                        for j in range(n * R, n * R + R):
                            act.wait_ge(glu_done, UPS * b + j + 1)
                            act.activation(sig[:, j % 2, :], glu[:, j % 2, :], ACT.Sigmoid, scale=ALPHA).then_inc(sig_done, 1)
                            if j:
                                columns(b, j - 1)
                        continue
                    if n == UP:
                        rows(b + 1, 0)
                        act.wait_ge(y_free, b + 1)
                    h = n - UP
                    for r in range(R):
                        wait_product(act, b, n, r)
                        act.activation(y[:, r, h * UNIT:(h + 1) * UNIT], ps[:, 4 + (h * R + r) % 2, :], ACT.Copy).then_inc(y_copied, 1)
                        if n == UP and r + 1 < R:
                            rows(b + 1, r + 1)

        @block.vector
        def _(dve):
            dve.sem_inc(lo_done, RING * CH)
            dve.sem_inc(up_free, 2)
            dve.sem_inc(a_ready, 2)

            def split(b, n):
                dve.wait_ge(prod_done, R * (NU * b + n) + R)
                for c in range(CH):
                    k = slice(KC * c, min(KC * (c + 1), KP))
                    dve.wait_ge(hi_done, CH * (NU * b + n) + c + 1)
                    dve.tensor_tensor(w_lo[:, n % LO, k, :], ring[:, n % RING, k, :], w_hi[:, n % HI, k, :].bitcast(F32), ALU.subtract).then_inc(lo_done, 1)

            def rows(b, r):
                dve.wait_ge(xhi_done, R * b + r + 1)
                dve.tensor_tensor(x_lo[:, r, :, :].rearrange("p k n -> p (k n)"), ps[:, 6:8, :].rearrange("p b n -> p (b n)"),
                                  x_hi[:, r, :, :].bitcast(F32).rearrange("p k n -> p (k n)"), ALU.subtract).then_inc(x_ready, 1)

            def columns(b, j):
                dve.wait_ge(ahi_done, UPS * b + j + 1)
                n, r = divmod(j, R)
                dve.tensor_tensor(a_lo[:, r, 2 * n:2 * n + 2, :].rearrange("p k n -> p (k n)"), ps[:, 2 + j % 2, 0:2 * P],
                                  a_hi[:, r, 2 * n:2 * n + 2, :].bitcast(F32).rearrange("p k n -> p (k n)"), ALU.subtract).then_inc(a_ready, 1)

            def select(sel, e, ready):
                col = onehot[:, bass.ds(e, 1)]
                dve.tensor_copy(sel[:, :], col.to_broadcast([96, P])).then_inc(ready, 1)

            steps = step_count(dve)
            for r in range(R):
                rows(0, r)
            dve.wait_ge(bias_loaded, 32)
            select(sel_up, expert_of(dve, 0), sel_up_ready)
            split(0, 0)
            with dve.Fori(0, steps) as b:
                link = linker(dve, dve_own, b * UPS)
                e, e_next = expert_of(dve, b), expert_of(dve, b + 1)
                for n in range(NU):
                    if n == UP:
                        columns(b, UPS - 1)
                    split(b + (n + 1) // NU, (n + 1) % NU)
                    if n == 0:
                        dve.wait_ge(prod_done, R * NU * b + 2 * R)
                        select(sel_down, e, sel_down_ready)
                    if n < UP:
                        for j in range(n * R, n * R + R):
                            s = j % 2
                            pairs = ps[:, s, :].rearrange("p (j two) -> p j two", two=2)
                            wait_product(dve, b, n, j - n * R)
                            if j >= 2:
                                dve.wait_ge(at_done, UPS * b + j - 1)
                            dve.tensor_scalar(glu[:, s, :], pairs[:, :, 0], LIMIT, None, ALU.min).then_inc(glu_done, 1)
                            dve.tensor_scalar(lin[:, s, :], pairs[:, :, 1], LIMIT, -LIMIT, ALU.min, ALU.max).then_inc(up_free, 1)
                            dve.wait_ge(up_free, UPS * b + j + 3)
                            link(dve.scalar_tensor_tensor(lin[:, s, :], lin[:, s, :], 1.0, glu[:, s, :], ALU.add, ALU.mult))
                            dve.wait_ge(sig_done, UPS * b + j + 1)
                            dve.tensor_tensor(act_o[:, s, :], lin[:, s, :], sig[:, s, :], ALU.mult).then_inc(act_done, 1)
                            if j:
                                columns(b, j - 1)
                        if n == UP - 1:
                            select(sel_up, e_next, sel_up_ready)
                    elif n == UP:
                        for r in range(R):
                            rows(b + 1, r)
                assert link.count[0] == UPS

        @block.tensor
        def _(pe):
            pe.sem_inc(prod_done, 2 * R)

            def rows(b, r):
                pe.wait_ge(gathered, 16 * R * b + 16 * R)
                if not isinstance(b, int) or r:
                    pe.wait_ge(x_ready, R * b + r)
                for k in range(KD):
                    last = pe.transpose(ps[:, 6 + k // 4, (k % 4) * P:(k % 4 + 1) * P], xg[:, r, k * P:(k + 1) * P], K.ident[:, :])
                last.then_inc(xt_done, 1)

            def columns(b, j):
                pe.wait_ge(act_done, UPS * b + j + 1)
                pe.wait_ge(a_ready, UPS * b + j + 1)
                for c in range(2):
                    last = pe.transpose(ps[:, 2 + j % 2, c * P:(c + 1) * P], act_o[:, j % 2, c * P:(c + 1) * P], K.ident[:, :])
                last.then_inc(at_done, 1)

            def product(b, n, r, bank, hi, lo, ready):
                for c in range(CH):
                    if r == 0:
                        pe.wait_ge(lo_done, CH * (NU * b + n) + c + 1 + RING * CH)
                    for k in range(KC * c, KC * (c + 1)):
                        if r == 0 and k == KP:
                            pe.wait_ge(pool_lo_done, CH * (NU * b + n) + CH + RING * CH)
                        if ready:
                            ready(k, r)
                        pe.matmul(bank, hi[:, r, k, :], w_hi[:, n % HI, k, :], start=False, stop=False)
                        pe.matmul(bank, hi[:, r, k, :], w_lo[:, n % LO, k, :], start=False, stop=False)
                        last = pe.matmul(bank, lo[:, r, k, :], w_hi[:, n % HI, k, :], start=False, stop=(k == KD - 1))
                last.then_inc(prod_done, 1)

            steps = step_count(pe)
            for r in range(R):
                rows(0, r)
            with pe.Fori(0, steps) as b:
                pe.wait_ge(sel_up_ready, b + 1)
                for j in range(UPS):
                    n, r = divmod(j, R)
                    if n == 0:
                        pe.wait_ge(x_ready, R * b + r + 1)
                    pe.wait_ge(up_free, UPS * b + j + 1)
                    pe.matmul(ps[:, j % 2, :], sel_up[:, :], btab[:, n * UNIT:(n + 1) * UNIT], start=True, stop=False)
                    product(b, n, r, ps[:, j % 2, :], x_hi, x_lo, None)
                    if j:
                        columns(b, j - 1)
                rows(b + 1, 0)
                columns(b, UPS - 1)
                pe.wait_ge(sel_down_ready, b + 1)

                def ready(k, r):
                    if k % 2 == 0:
                        pe.wait_ge(a_ready, UPS * b + (k // 2) * R + r + 3)

                for i in range(DOWNS):
                    h, r = divmod(i, R)
                    pe.wait_ge(y_copied, DOWNS * b + i + 1)
                    bank = ps[:, 4 + i % 2, :]
                    pe.matmul(bank, sel_down[:, :], btab[:, 2 * FF + h * UNIT:2 * FF + (h + 1) * UNIT], start=True, stop=False)
                    product(b, UP + h, r, bank, a_hi, a_lo, ready if h == 0 else None)
                    if h == 0 and r + 1 < R:
                        rows(b + 1, r + 1)


def combine(K):
    nc, io = K.nc, K.io
    ctx = ExitStack()
    with ctx:
        sb, sem = scope(K, ctx)
        yg = sb("yg", [P, 2, TOPK, D])
        XBUF = 4
        x1 = sb("x1_rows", [P, XBUF, D])
        acc, out = sb("acc", [P, 2, D]), sb("out_rows", [P, 2, D])
        squares = sb("squares5", [P, D])
        gate2, gain = sb("gate2", [P, D]), sb("gain5", [P, D])
        stat = sb("stat5", [P, T, 3])
        rows_loaded = sem("rows_loaded5")
        tile_loaded = [sem("tile_loaded5_0"), sem("tile_loaded5_1")]
        stored = [sem("stored5_0"), sem("stored5_1")]
        acc_done, rms_done, out_done, dve_own, act_own = sem("acc_done"), sem("rms_done5"), sem("out_done"), sem("dve_own5"), sem("act_own5")
        y_rows = K.y_d[0:TOPK * SEQ, :].rearrange("(k t p) d -> t p k d", t=T, p=P)
        block = ctx.enter_context(nc.Block())

        @block.sync
        def _(sp):
            for t in range(T):
                if t >= 2:
                    sp.wait_ge(acc_done, t - 1)
                sp.dma_start(yg[:, t % 2, :, :], y_rows[t]).then_inc(tile_loaded[t % 2], 16)
                if t >= XBUF:
                    sp.wait_ge(out_done, t - XBUF + 1)
                sp.dma_start(x1[:, t % XBUF, :], K.x1_d[t * P:(t + 1) * P, :]).then_inc(tile_loaded[t % 2], 16)

        @block.gpsimd
        def _(pool):
            pool.dma_start(gate2[:, :], K.mod_d[0:1, 5 * D:6 * D].to_broadcast([P, D])).then_inc(rows_loaded, 16)
            pool.dma_start(gain[:, :], io["g_post_ffn"].to_broadcast([P, D])).then_inc(rows_loaded, 16)
            pool.wait_ge(rows_loaded, 32)
            for t in range(T):
                pool.wait_ge(out_done, t + 1)
                pool.dma_start(io["out"][0][t * P:(t + 1) * P, :], out[:, t % 2, :]).then_inc(stored[t % 2], 16)
            for s in range(2):
                pool.wait_ge(stored[s], 16 * (T // 2))

        @block.scalar
        def _(act):
            link = linker(act, act_own)
            for t in range(T):
                act.wait_ge(acc_done, t + 1)
                link(act.activation(squares[:, :], acc[:, t % 2, :], ACT.Square, accum_out=stat[:, t, 0:1]))
                act.activation(stat[:, t, 1:2], stat[:, t, 0:1], ACT.Sqrt, bias=K.eps[:, :], scale=1.0 / D).then_inc(rms_done, 1)

        @block.vector
        def _(dve):
            link = linker(dve, dve_own)

            def add(t):
                s = t % 2
                dve.wait_ge(tile_loaded[s], 32 * (t // 2 + 1))
                link(dve.tensor_scalar(acc[:, s, :], yg[:, s, 0, :], K.weights[:, t, 0:1], None, ALU.mult))
                for k in range(1, TOPK):
                    ins = dve.scalar_tensor_tensor(acc[:, s, :], yg[:, s, k, :], K.weights[:, t, k:k + 1], acc[:, s, :], ALU.mult, ALU.add)
                    if k + 1 < TOPK:
                        link(ins)
                ins.then_inc(acc_done, 1)

            def finish(t):
                s = t % 2
                dve.wait_ge(rms_done, t + 1)
                link(dve.reciprocal(stat[:, t, 2:3], stat[:, t, 1:2]))
                if t >= 2:
                    dve.wait_ge(stored[s], 16 * (t // 2))
                link(dve.scalar_tensor_tensor(out[:, s, :], acc[:, s, :], stat[:, t, 2:3], gate2[:, :], ALU.mult, ALU.mult))
                dve.tensor_tensor(out[:, s, :], out[:, s, :], x1[:, t % XBUF, :], ALU.add).then_inc(out_done, 1)

            add(0)
            dve.wait_ge(rows_loaded, 32)
            link(dve.tensor_tensor(gate2[:, :], gate2[:, :], gain[:, :], ALU.mult))
            for t in range(T):
                if t + 1 < T:
                    add(t + 1)
                finish(t)


_INS = ["x", "c", "ctx", "c_ctx", "w_ada", "b_ada", "g_pre_mix", "g_post_mix", "g_pre_ffn", "g_post_ffn",
        "w_in", "g_grp_a", "g_grp_b", "sink_a", "rpb_b", "w_out", "w_router", "b_router",
        "w_mlp1", "b_mlp1", "w_mlp2", "b_mlp2"]


def kernel(**inputs):
    import concourse.bacc as bacc
    from concourse.bass_utils import run_bass_kernel_spmd

    nc = bacc.Bacc("TRN2", target_bir_lowering=False, num_devices=1)
    arrays, io = {}, {}
    given = {name: inputs[name] for name in _INS}
    given.update(constants())
    for name, a in given.items():
        a = np.ascontiguousarray(a)
        arrays["in_" + name] = a
        io[name] = nc.dram_tensor("in_" + name, a.shape, mybir.dt.from_np(a.dtype), kind="ExternalInput").ap()
    io["out"] = nc.dram_tensor("out_0", (1, SEQ, D), F32, kind="ExternalOutput").ap()
    Kernel(nc, io).build()
    r = run_bass_kernel_spmd(nc, [arrays], core_ids=[0])
    return r.results[0]["out_0"]
```
